# Optimizing a Trainium2 kernel written in Bass

```python
import math
import jax, jax.numpy as jnp
from jax import lax
import numpy as np

D_MODEL = 1024
BATCH = 1
SEQ = 2048
DEPTH = 1
DEC_BATCH = 8
DEC_SEQ = 8
PAST_LEN = 2048
PAGE_SIZE = 128

N_META = 16
MIX_W = D_MODEL
GDN_DK = 128
GDN_DV = 128
GDN_HEADS = (MIX_W // 2) // GDN_DV
GDN_CHUNK = 64
CONV_W = 4
SB_HEAD_DIM = 64
SB_HEADS = (MIX_W // 2) // SB_HEAD_DIM
SB_BLOCK = 128
SB_BIAS_HI = -4.0
SB_BIAS_LO = -11.0
GDN_QK = GDN_HEADS * GDN_DK
GDN_VW = GDN_HEADS * GDN_DV
CONV_DIM = 2 * GDN_QK + GDN_VW
SB_W = SB_HEADS * SB_HEAD_DIM
PROJ_SIZES = (CONV_DIM, GDN_VW, GDN_HEADS, GDN_HEADS, SB_W, SB_W, SB_W, SB_W)
IN_DIM = CONV_DIM + GDN_VW + 2 * GDN_HEADS + 4 * SB_W
ALPHA = (2 * DEPTH) ** 0.25
BETA_INIT = (8 * DEPTH) ** -0.25
LN_EPS = 1e-5
RMS_EPS = 1e-6
L2_EPS = 1e-6

kernel_name = "hymba_gdn_stickbreak_step"

def _layernorm(x, g, b):
    xf = x.astype(jnp.float32)
    mu = jnp.mean(xf, -1, keepdims=True)
    var = jnp.mean(jnp.square(xf - mu), -1, keepdims=True)
    return (xf - mu) * lax.rsqrt(var + LN_EPS) * g.astype(jnp.float32) + b.astype(jnp.float32)

def _rmsnorm(x, g):
    return x * lax.rsqrt(jnp.mean(x * x, -1, keepdims=True) + RMS_EPS) * g.astype(jnp.float32)

def _l2norm(x):
    return x * lax.rsqrt(jnp.sum(x * x, -1, keepdims=True) + L2_EPS)

def _project(h, w_in):
    p = jnp.einsum('bld,de->ble', h, w_in).astype(jnp.float32)
    splits = [int(s) for s in np.cumsum(PROJ_SIZES)[:-1]]
    return jnp.split(p, splits, axis=-1)

def _causal_conv(x, buf, w):
    L = x.shape[1]
    xx = jnp.concatenate([buf, x], axis=1)
    wf = w.astype(jnp.float32)
    y = sum(xx[:, i:i + L] * wf[i] for i in range(CONV_W))
    return jax.nn.silu(y), xx[:, -(CONV_W - 1):]

def _gdn_qkv(c):
    B, L, _ = c.shape
    q, k, v = jnp.split(c, [GDN_QK, 2 * GDN_QK], axis=-1)
    q = _l2norm(q.reshape(B, L, GDN_HEADS, GDN_DK)) * (GDN_DK ** -0.5)
    k = _l2norm(k.reshape(B, L, GDN_HEADS, GDN_DK))
    v = v.reshape(B, L, GDN_HEADS, GDN_DV)
    return q, k, v

def _gdn_gates(a, b, a_log, dt_bias):
    g = -jnp.exp(a_log.astype(jnp.float32)) * jax.nn.softplus(a + dt_bias.astype(jnp.float32))
    return g, jax.nn.sigmoid(b)

def _gdn_chunked(q, k, v, g, beta, s0, chunk):
    B, L, H, DK = q.shape
    DV = v.shape[-1]
    n = L // chunk

    def blocks(t):
        return jnp.swapaxes(t.reshape((B, n, chunk) + t.shape[2:]), 2, 3)

    q, k, v, beta = blocks(q), blocks(k), blocks(v), blocks(beta)
    g = jnp.cumsum(blocks(g), axis=-1)
    idx = jnp.arange(chunk)
    causal = idx[:, None] >= idx[None, :]
    strict = idx[:, None] > idx[None, :]
    decay = jnp.exp(jnp.where(causal, g[..., :, None] - g[..., None, :], -jnp.inf))
    kb = k * beta[..., None]
    m = jnp.where(strict, jnp.einsum('bnhid,bnhjd->bnhij', kb, k) * decay, 0.0)
    rhs = jnp.concatenate([v * beta[..., None], kb * jnp.exp(g)[..., None]], axis=-1)
    sol = lax.linalg.triangular_solve(m + jnp.eye(chunk, dtype=m.dtype), rhs,
                                      left_side=True, lower=True, unit_diagonal=True)
    u, w = sol[..., :DV], sol[..., DV:]
    qk = jnp.einsum('bnhid,bnhjd->bnhij', q, k) * decay
    qd = q * jnp.exp(g)[..., None]
    gl = g[..., -1]
    kd = k * jnp.exp(gl[..., None] - g)[..., None]

    def step(s, xs):
        u_c, w_c, qk_c, qd_c, kd_c, gl_c = xs
        v_new = u_c - jnp.einsum('bhck,bhkv->bhcv', w_c, s)
        o = jnp.einsum('bhck,bhkv->bhcv', qd_c, s) + jnp.einsum('bhij,bhjv->bhiv', qk_c, v_new)
        s = s * jnp.exp(gl_c)[..., None, None] + jnp.einsum('bhck,bhcv->bhkv', kd_c, v_new)
        return s, o

    xs = tuple(jnp.moveaxis(t, 1, 0) for t in (u, w, qk, qd, kd, gl))
    s, o = lax.scan(step, s0, xs)
    return o.transpose(1, 0, 3, 2, 4).reshape(B, L, H, DV), s

def _sb_block(q, k, v, q_pos, k_pos, bias):
    z = jnp.einsum('bqhd,bkhd->bhqk', q.astype(jnp.float32), k.astype(jnp.float32)) * (SB_HEAD_DIM ** -0.5)
    z = z + bias.astype(jnp.float32)[None, :, None, None]
    vis = k_pos[None, :] < q_pos[:, None]
    log_keep = jnp.where(vis, jax.nn.log_sigmoid(-z), 0.0)
    after = lax.cumsum(log_keep, axis=3, reverse=True) - log_keep
    a = jnp.where(vis, jnp.exp(jax.nn.log_sigmoid(z) + after), 0.0)
    return jnp.einsum('bhqk,bkhd->bqhd', a, v.astype(jnp.float32))

def _merge(h, o_gdn, z_gdn, o_sb, z_sb, gdn_norm_g, w_out, ln_g, ln_b):
    B, L, _ = h.shape
    og = _rmsnorm(o_gdn, gdn_norm_g).reshape(B, L, GDN_VW) * jax.nn.silu(z_gdn)
    osb = o_sb.reshape(B, L, SB_W) * jax.nn.silu(z_sb)
    mix = jnp.einsum('ble,ed->bld', jnp.concatenate([og, osb], axis=-1), w_out.astype(jnp.float32))
    return _layernorm(ALPHA * h.astype(jnp.float32) + mix, ln_g, ln_b).astype(h.dtype)

def _prompt_layer(h, w_in, conv_w, a_log, dt_bias, gdn_norm_g, sb_bias, w_out, ln_g, ln_b):
    B, L, _ = h.shape
    c, zg, a, b, q, k, v, zs = _project(h, w_in)
    c, conv_buf = _causal_conv(c, jnp.zeros((B, CONV_W - 1, CONV_DIM), jnp.float32), conv_w)
    gq, gk, gv = _gdn_qkv(c)
    g, beta = _gdn_gates(a, b, a_log, dt_bias)
    m = N_META
    s0 = jnp.zeros((B, GDN_HEADS, GDN_DK, GDN_DV), jnp.float32)
    o_meta, s1 = _gdn_chunked(gq[:, :m], gk[:, :m], gv[:, :m], g[:, :m], beta[:, :m], s0, m)
    o_real, s2 = _gdn_chunked(gq[:, m:], gk[:, m:], gv[:, m:], g[:, m:], beta[:, m:], s1, GDN_CHUNK)
    o_gdn = jnp.concatenate([o_meta, o_real], axis=1)
    q = q.reshape(B, L, SB_HEADS, SB_HEAD_DIM)
    k = k.reshape(B, L, SB_HEADS, SB_HEAD_DIM)
    v = v.reshape(B, L, SB_HEADS, SB_HEAD_DIM)
    pos = jnp.arange(L, dtype=jnp.int32)
    o_sb_meta = _sb_block(q[:, :m], k[:, :m], v[:, :m], pos[:m], pos[:m], sb_bias)
    n_blk = (L - m) // SB_BLOCK
    qb = jnp.moveaxis(q[:, m:].reshape(B, n_blk, SB_BLOCK, SB_HEADS, SB_HEAD_DIM), 1, 0)
    pb = pos[m:].reshape(n_blk, SB_BLOCK)
    ob = lax.map(lambda t: _sb_block(t[0], k, v, t[1], pos, sb_bias), (qb, pb))
    o_sb_real = jnp.moveaxis(ob, 0, 1).reshape(B, L - m, SB_HEADS, SB_HEAD_DIM)
    o_sb = jnp.concatenate([o_sb_meta, o_sb_real], axis=1)
    y = _merge(h, o_gdn, zg, o_sb, zs, gdn_norm_g, w_out, ln_g, ln_b)
    return y, k.astype(h.dtype), v.astype(h.dtype), s2, conv_buf.astype(h.dtype)

def _sample_layer(h, cache_k, cache_v, page_table, state_gdn, state_conv,
                  w_in, conv_w, a_log, dt_bias, gdn_norm_g, sb_bias, w_out, ln_g, ln_b):
    B, T, _ = h.shape
    c, zg, a, b, q, k, v, zs = _project(h, w_in)
    c, conv_buf = _causal_conv(c, state_conv.astype(jnp.float32), conv_w)
    gq, gk, gv = _gdn_qkv(c)
    g, beta = _gdn_gates(a, b, a_log, dt_bias)
    o_gdn, s_new = _gdn_chunked(gq, gk, gv, g, beta, state_gdn.astype(jnp.float32), T)
    q = q.reshape(B, T, SB_HEADS, SB_HEAD_DIM)
    k = k.reshape(B, T, SB_HEADS, SB_HEAD_DIM)
    v = v.reshape(B, T, SB_HEADS, SB_HEAD_DIM)
    past = page_table.shape[1] * cache_k.shape[1]
    k_pos = jnp.arange(past + T, dtype=jnp.int32)
    q_pos = k_pos[past:]

    def one_seq(t):
        pt, q1, k1, v1 = t
        kk = jnp.concatenate([cache_k[pt].reshape(past, SB_HEADS, SB_HEAD_DIM).astype(jnp.float32), k1], axis=0)
        vv = jnp.concatenate([cache_v[pt].reshape(past, SB_HEADS, SB_HEAD_DIM).astype(jnp.float32), v1], axis=0)
        return _sb_block(q1[None], kk[None], vv[None], q_pos, k_pos, sb_bias)[0]

    o_sb = lax.map(one_seq, (page_table, q, k, v))
    y = _merge(h, o_gdn, zg, o_sb, zs, gdn_norm_g, w_out, ln_g, ln_b)
    return y, k.astype(h.dtype), v.astype(h.dtype), s_new, conv_buf.astype(h.dtype)

def setup_inputs(seed: int = 0) -> dict:
    key = jax.random.key(seed)
    ks = jax.random.split(key, 20)
    nrm = jax.random.normal
    n_pages = PAST_LEN // PAGE_SIZE
    n_phys = (DEC_BATCH * n_pages * 5) // 4
    x_prompt = nrm(ks[0], (BATCH, SEQ, D_MODEL), jnp.float32)
    x_sample = nrm(ks[1], (DEC_BATCH, DEC_SEQ, D_MODEL), jnp.float32)
    cache_k = nrm(ks[2], (DEPTH, n_phys, PAGE_SIZE, SB_HEADS, SB_HEAD_DIM), jnp.float32)
    cache_v = nrm(ks[3], (DEPTH, n_phys, PAGE_SIZE, SB_HEADS, SB_HEAD_DIM), jnp.float32)
    page_table = jax.random.permutation(ks[4], n_phys)[:DEC_BATCH * n_pages].reshape(DEC_BATCH, n_pages).astype(jnp.int32)
    state_gdn = 0.1 * nrm(ks[5], (DEPTH, DEC_BATCH, GDN_HEADS, GDN_DK, GDN_DV), jnp.float32)
    state_conv = nrm(ks[6], (DEPTH, DEC_BATCH, CONV_W - 1, CONV_DIM), jnp.float32)
    meta_tokens = nrm(ks[7], (N_META, D_MODEL), jnp.float32)
    ln_in_g = 1.0 + 0.02 * nrm(ks[8], (D_MODEL,), jnp.float32)
    ln_in_b = 0.02 * nrm(ks[9], (D_MODEL,), jnp.float32)
    w_in = nrm(ks[10], (DEPTH, D_MODEL, IN_DIM), jnp.float32) * (D_MODEL ** -0.5)
    conv_w = nrm(ks[11], (DEPTH, CONV_W, CONV_DIM), jnp.float32) * (CONV_W ** -0.5)
    a_log = jnp.log(jax.random.uniform(ks[12], (DEPTH, GDN_HEADS), jnp.float32, 1.0, 16.0))
    dt = jnp.exp(jax.random.uniform(ks[13], (DEPTH, GDN_HEADS), jnp.float32, math.log(1e-3), math.log(1e-1)))
    dt_bias = dt + jnp.log(-jnp.expm1(-dt))
    gdn_norm_g = 1.0 + 0.02 * nrm(ks[14], (DEPTH, GDN_DV), jnp.float32)
    sb_bias = jnp.broadcast_to(jnp.linspace(SB_BIAS_HI, SB_BIAS_LO, SB_HEADS, dtype=jnp.float32), (DEPTH, SB_HEADS)) \
        + 0.1 * nrm(ks[18], (DEPTH, SB_HEADS), jnp.float32)
    w_out = nrm(ks[15], (DEPTH, MIX_W, D_MODEL), jnp.float32) * (MIX_W ** -0.5) * BETA_INIT
    ln_out_g = 1.0 + 0.02 * nrm(ks[16], (DEPTH, D_MODEL), jnp.float32)
    ln_out_b = 0.02 * nrm(ks[17], (DEPTH, D_MODEL), jnp.float32)
    return {"x_prompt": x_prompt, "x_sample": x_sample, "cache_k": cache_k, "cache_v": cache_v,
            "page_table": page_table, "state_gdn": state_gdn, "state_conv": state_conv,
            "meta_tokens": meta_tokens, "ln_in_g": ln_in_g, "ln_in_b": ln_in_b, "w_in": w_in,
            "conv_w": conv_w, "a_log": a_log, "dt_bias": dt_bias, "gdn_norm_g": gdn_norm_g,
            "sb_bias": sb_bias, "w_out": w_out, "ln_out_g": ln_out_g, "ln_out_b": ln_out_b}

def reference(x_prompt, x_sample, cache_k, cache_v, page_table, state_gdn, state_conv,
              meta_tokens, ln_in_g, ln_in_b, w_in, conv_w, a_log, dt_bias, gdn_norm_g,
              sb_bias, w_out, ln_out_g, ln_out_b):
    B = x_prompt.shape[0]
    meta = jnp.broadcast_to(meta_tokens[None].astype(x_prompt.dtype), (B, N_META, D_MODEL))
    hp = _layernorm(jnp.concatenate([meta, x_prompt], axis=1), ln_in_g, ln_in_b).astype(x_prompt.dtype)
    hs = _layernorm(x_sample, ln_in_g, ln_in_b).astype(x_sample.dtype)
    kp, vp, ksm, vsm, sp, ss, cp, cs = [], [], [], [], [], [], [], []
    for l in range(DEPTH):
        hp, k1, v1, s1, c1 = _prompt_layer(hp, w_in[l], conv_w[l], a_log[l], dt_bias[l], gdn_norm_g[l],
                                           sb_bias[l], w_out[l], ln_out_g[l], ln_out_b[l])
        hs, k2, v2, s2, c2 = _sample_layer(hs, cache_k[l], cache_v[l], page_table, state_gdn[l], state_conv[l],
                                           w_in[l], conv_w[l], a_log[l], dt_bias[l], gdn_norm_g[l],
                                           sb_bias[l], w_out[l], ln_out_g[l], ln_out_b[l])
        kp.append(k1); vp.append(v1); sp.append(s1); cp.append(c1)
        ksm.append(k2); vsm.append(v2); ss.append(s2); cs.append(c2)
    y_prompt = hp[:, N_META:]
    y_sample = hs
    return (y_prompt, y_sample, jnp.stack(kp), jnp.stack(vp), jnp.stack(ksm), jnp.stack(vsm),
            jnp.stack(sp), jnp.stack(ss), jnp.stack(cp), jnp.stack(cs))


_drawn_inputs = setup_inputs


def setup_inputs(seed=0):
    import zlib

    import numpy as np

    out = dict(_drawn_inputs(seed))
    spreads = {}
    factors = {'cache_k': 4.8,
     'cache_v': 3.698,
     'gdn_norm_g': 8.0,
     'sb_bias': 3.453,
     'ln_out_g': 2.86,
     'ln_out_b': 2.874}
    for name, (base, spread) in spreads.items():
        noise = np.random.default_rng([zlib.crc32(name.encode()), seed]).standard_normal(out[name].shape)
        drawn = base * np.exp(spread * noise) if base else spread * noise
        out[name] = __import__('jax').numpy.asarray(drawn.astype(out[name].dtype))
    for name, factor in factors.items():
        out[name] = (out[name] * factor).astype(out[name].dtype)
    return out
```

```python
from contextlib import ExitStack

import numpy as np

import concourse.bass as bass
from concourse import mybir

F32 = mybir.dt.float32
I32 = mybir.dt.int32
ALU = mybir.AluOpType
ACT = mybir.ActivationFunctionType
ds = bass.ds

P = 128
D = 1024
KC = D // P
SEQ, N_META = 2048, 16
SEQS, STEPS = 8, 8
NS = SEQS * STEPS
NT = 1 + SEQ // P
TOK = NT * P
M0 = P - N_META
GH, DK = 4, 128
SH, SD = 8, 64
PAIRS = SH // 2
HALF = 512
CONV = 4
CB = 12
PAGE, PAGES = 128, 16
COL_ZG, COL_AB, COL_Q, COL_K, COL_V, COL_ZS = 1536, 2048, 2056, 2568, 3080, 3592
IN_DIM = 4104
ALPHA = 2.0 ** 0.25
LN_EPS, RMS_EPS, L2_EPS = 1e-5, 1e-6, 1e-6
CHUNKS = [(0, 512), (512, 512), (1024, 512), (1536, 512), (2048, 128)]
START = 1
LEVELS = 7

C_ID, C_UT, C_ONE, C_LM, C_U8, C_MB = 0, P, 2 * P, 3 * P, (3 + LEVELS) * P, (3 + LEVELS) * P + NS
C_MH = C_MB + 112
C_NM = C_MH + 1
C_W = C_NM + P


def shape_constants():
    i, j = np.arange(P)[:, None], np.arange(P)[None, :]
    parts = [i == j, i <= j, np.ones((P, P))]
    for l in range(LEVELS):
        s = 1 << l
        parts.append((i // (2 * s) == j // (2 * s)) & (i // s % 2 == 1) & (j // s % 2 == 0))
    parts.append(((i // STEPS == j // STEPS) & (i <= j))[:, :NS])
    c = np.arange(112)[None, :] - 48
    parts.append((c // STEPS == i // NS) & (c >= 0) & (c % STEPS < i % STEPS))
    parts.append(np.full((P, 1), -0.5))
    parts.append(np.where(j >= i, -1e30, 0.0))
    return np.concatenate([np.asarray(p, np.float32) for p in parts], axis=1)


class Program:

    def __init__(self, nc, io, stack, debug):
        self.nc, self.io, self.stack = nc, io, stack
        self.n_phys = io["cache_k"].shape[1]
        kind = "ExternalOutput" if debug else "Internal"

        def scratch(name, shape):
            return nc.dram_tensor(name, shape, F32, kind=kind).ap()

        self.h_rows = scratch("h_rows", (NT, P, D))
        self.gates = scratch("gates", (NT, P, D))
        self.chan = scratch("chan", (20, P, TOK))
        self.o_rows = scratch("o_rows", (NT, P, D))
        self.ps = stack.enter_context(nc.psum_tensor("ps", [P, 8, 512], F32))
        self.con = self.sb("con", [P, C_W])
        self.ab = self.sb("ab", [P, NT, 8])
        self.lnT = self.sb("lnT", [P, 16])
        self.rows28 = self.sb("rows28", [28, CB, P])
        self.sc = self.sb("sc", [P, CB, 28])
        self.tails = self.sb("tails", [P, CB, 27])
        self.small = self.sb("small", [P, 64])
        self.g = self.sb("g", [P, NT, GH])
        self.g_s = self.sb("g_s", [P, GH])
        self.beta = self.sb("beta", [P, NT, GH])
        self.ident = self.con[:, C_ID:C_ID + P]
        self.utri = self.con[:, C_UT:C_UT + P]
        self.ones = self.con[:, C_ONE:C_ONE + P]

    def sb(self, name, shape, dt=F32, stack=None):
        return (stack or self.stack).enter_context(self.nc.sbuf_tensor(name, shape, dt))

    def sem(self, name):
        self.stage_sems.append(self.nc.alloc_semaphore(name=name))
        return self.stage_sems[-1]

    def block(self, stack):
        for s in self.stage_sems:
            self.nc.gpsimd.sem_inc(s, START)
        self.nc.all_engine_barrier()
        return stack.enter_context(self.nc.Block())

    def run(self, stage, *args):
        self.stage_sems = []
        stage(self, *args)
        self.nc.clear_and_free_semaphores(self.stage_sems)


def row(ap, n=P):
    return ap.partition_broadcast(n)


def setup(p):
    nc, io = p.nc, p.io
    loaded, turned, copied = p.sem("su_loaded"), p.sem("su_turned"), p.sem("su_copied")
    with ExitStack() as st:
        ln16 = p.sb("ln16", [16, P], stack=st)
        block = p.block(st)

        @block.sync
        def _(sp):
            sp.dma_start(p.con[:, :], io["consts"]).then_inc(loaded, 16)
            sp.dma_start(p.rows28[0:24, :, :], io["state_conv"][0].rearrange("b i (c p) -> (b i) c p", p=P)).then_inc(loaded, 16)
            sp.dma_start(p.rows28[24:28, :, :], io["conv_w"][0].rearrange("i (c p) -> i c p", p=P)).then_inc(loaded, 16)
            sp.dma_start(ln16[0:8, :], io["ln_in_g"].rearrange("(c p) -> c p", p=P)).then_inc(loaded, 16)
            sp.dma_start(ln16[8:16, :], io["ln_in_b"].rearrange("(c p) -> c p", p=P)).then_inc(loaded, 16)
            sp.dma_start(p.small[:, 0:4], row(io["a_log"][0])).then_inc(loaded, 16)
            sp.dma_start(p.small[:, 4:8], row(io["dt_bias"][0])).then_inc(loaded, 16)
            sp.dma_start(p.small[:, 8:16], row(io["sb_bias"][0])).then_inc(loaded, 16)

        @block.tensor
        def _(pe):
            pe.wait_ge(loaded, START + 16 * 8)
            for c in range(CB):
                pe.transpose(p.ps[:, 0, 28 * c:28 * c + 28], p.rows28[:, c, :], p.con[0:28, 0:28])
            pe.transpose(p.ps[:, 1, 0:16], ln16[:, :], p.con[0:16, 0:16]).then_inc(turned, 1)

        @block.vector
        def _(dve):
            dve.wait_ge(turned, START + 1)
            dve.tensor_copy(p.sc[:, :, :].rearrange("p c i -> p (c i)"), p.ps[:, 0, 0:28 * CB]).then_inc(copied, 1)
            dve.tensor_copy(p.lnT[:, :], p.ps[:, 1, 0:16]).then_inc(copied, 1)
            dve.tensor_scalar(p.small[:, 16:24], p.small[:, 8:16], -1.0, None, ALU.mult).then_inc(copied, 1)
            dve.wait_ge(copied, START + 3)


def token_major(p, hT):
    nc, io, ps = p.nc, p.io, p.ps
    x_loaded = [p.sem("x_even_loaded"), p.sem("x_odd_loaded")]
    w_loaded, g_loaded = p.sem("w_loaded"), p.sem("g_loaded")
    padded = p.sem("padded")
    stats, centred, rooted, normed = p.sem("stats"), p.sem("centred"), p.sem("rooted"), p.sem("normed")
    turned, evacuated = p.sem("x_turned"), p.sem("xT_evacuated")
    v_acc, zg_acc, zs_acc, ab_acc = p.sem("v_acc"), p.sem("zg_acc"), p.sem("zs_acc"), p.sem("ab_acc")
    v_out, zg_out, zs_out, ab_out = p.sem("v_out"), p.sem("zg_out"), p.sem("zs_out"), p.sem("ab_out")
    scaled, shifted, kept = p.sem("h_scaled"), p.sem("h_shifted"), p.sem("hT_kept")
    h_stored = p.sem("h_stored")
    v_stored = [p.sem("v_even_stored"), p.sem("v_odd_stored")]
    g_stored = [p.sem("g_even_stored"), p.sem("g_odd_stored")]
    w = io["w_in"][0].rearrange("(c p) n -> p c n", p=P)
    v_p = io["v_prompt"][0, 0].rearrange("l h d -> l (h d)")
    v_s = io["v_sample"][0].rearrange("b t h d -> (b t) (h d)")
    with ExitStack() as st:
        wt = p.sb("wt", [P, KC, 1536], stack=st)
        wab = p.sb("wab", [P, KC, 8], stack=st)
        xin = p.sb("xin", [P, 2, D], stack=st)
        xh = p.sb("xh", [P, 2, D], stack=st)
        hg = p.sb("hg", [P, D], stack=st)
        gain = p.sb("gain", [P, 2, D], stack=st)
        cur = [p.sb(f"hT_now{i}", [P, KC, P], stack=st) for i in range(2)]
        vb = p.sb("vb", [P, 2, 512], stack=st)
        gb = p.sb("gb", [P, 2, D], stack=st)
        st6 = p.sb("st6", [P, 2, 6], stack=st)
        mv = p.sb("mv", [P, 4], stack=st)
        block = p.block(st)

        @block.sync
        def _(sp):
            def load(t, b):
                sp.wait_ge(normed, START + t - 1)
                sp.dma_start(xin[:, b, :], io["x_prompt"][0, ds((t - 1) * P, P), :]).then_inc(x_loaded[b], 16)

            def store(t, b):
                sp.wait_ge(shifted, START + t + 1)
                sp.dma_start(p.h_rows[ds(t, 1)].rearrange("a p d -> (a p) d"), hg[:, :]).then_inc(h_stored, 16)
                sp.wait_ge(v_out, START + t + 1)
                sp.dma_start(v_p[ds(t * P - M0, P), :], vb[:, b, :]).then_inc(v_stored[b], 16)
                sp.wait_ge(zs_out, START + t + 1)
                sp.dma_start(p.gates[ds(t, 1)].rearrange("a p d -> (a p) d"), gb[:, b, :]).then_inc(g_stored[b], 16)

            sp.dma_start(xin[0:NS, 0, :], io["x_sample"].rearrange("b t d -> (b t) d")).then_inc(x_loaded[0], 16)
            sp.dma_start(xin[M0:P, 0, :], io["meta_tokens"]).then_inc(x_loaded[0], 16)
            sp.dma_start(gain[:, 0, :], row(io["ln_in_g"])).then_inc(g_loaded, 16)
            sp.dma_start(gain[:, 1, :], row(io["ln_in_b"])).then_inc(g_loaded, 16)
            sp.dma_start(wt[:, :, 0:512], w[:, :, COL_V:COL_V + 512]).then_inc(w_loaded, 16)
            sp.dma_start(wt[:, :, 512:1024], w[:, :, COL_ZG:COL_ZG + 512]).then_inc(w_loaded, 16)
            sp.dma_start(wt[:, :, 1024:1536], w[:, :, COL_ZS:COL_ZS + 512]).then_inc(w_loaded, 16)
            sp.dma_start(wab[:, :, :], w[:, :, COL_AB:COL_AB + 8]).then_inc(w_loaded, 16)
            sp.dma_start(xin[:, 1, :], io["x_prompt"][0, 0:P, :]).then_inc(x_loaded[1], 16)
            sp.wait_ge(shifted, START + 1)
            sp.dma_start(p.h_rows[0], hg[:, :]).then_inc(h_stored, 16)
            sp.wait_ge(v_out, START + 1)
            sp.dma_start(v_s, vb[0:NS, 0, :]).then_inc(v_stored[0], 16)
            sp.dma_start(v_p[0:N_META, :], vb[M0:P, 0, :]).then_inc(v_stored[0], 16)
            sp.wait_ge(zs_out, START + 1)
            sp.dma_start(p.gates[0], gb[:, 0, :]).then_inc(g_stored[0], 16)
            with sp.Fori(0, (NT - 1) // 2 - 1) as i:
                load(2 * i + 2, 0)
                store(2 * i + 1, 1)
                load(2 * i + 3, 1)
                store(2 * i + 2, 0)
            load(NT - 1, 0)
            store(NT - 2, 1)
            store(NT - 1, 0)
            sp.wait_ge(h_stored, START + 16 * NT)
            sp.wait_ge(v_stored[0], START + 16 * (NT // 2 + 2))
            sp.wait_ge(v_stored[1], START + 16 * (NT // 2))
            sp.wait_ge(g_stored[0], START + 16 * (NT // 2 + 1))
            sp.wait_ge(g_stored[1], START + 16 * (NT // 2))

        @block.gpsimd
        def _(pool):
            pool.memset(xin[NS:M0, 0, :], 0.0).then_inc(padded, 1)
            pool.wait_ge(padded, START + 1)
            pool.memset(cur[0][:, :, NS:M0], 0.0).then_inc(padded, 1)

            def rows(t, b):
                pool.wait_ge(centred, START + t + 1)
                pool.tensor_tensor(mv[:, 3:4], mv[:, 2:3], p.con[:, C_MH:C_MH + 1], ALU.pow).then_inc(rooted, 1)
                pool.wait_ge(normed, START + t + 1)
                pool.wait_ge(h_stored, START + 16 * t)
                pool.tensor_tensor(hg[:, :], xh[:, b, :], gain[:, 0, :], ALU.mult).then_inc(scaled, 1)
                pool.wait_ge(scaled, START + t + 1)
                pool.tensor_tensor(hg[:, :], hg[:, :], gain[:, 1, :], ALU.add).then_inc(shifted, 1)
                pool.wait_ge(evacuated, START + t + 1)
                pool.tensor_copy(hT[:, :, ds(t * P, P)], cur[b][:, :, :]).then_inc(kept, 1)

            pool.wait_ge(g_loaded, START + 32)
            rows(0, 0)
            with pool.Fori(0, (NT - 1) // 2) as i:
                rows(2 * i + 1, 1)
                rows(2 * i + 2, 0)

        @block.vector
        def _(dve):
            def norm(t, b, loaded):
                dve.wait_ge(x_loaded[b], START + loaded)
                if not (isinstance(t, int) and t == 0):
                    dve.wait_ge(normed, START + t)
                dve.bn_stats(st6[:, 0, :], xin[:, b, 0:512]).then_inc(stats, 1)
                dve.bn_stats(st6[:, 1, :], xin[:, b, 512:1024]).then_inc(stats, 1)
                dve.wait_ge(stats, START + 3 * t + 2)
                dve.tensor_copy(mv[:, 2:3], st6[:, 1, 0:1])
                dve.bn_aggr(mv[:, 0:2], st6[:, :, :].rearrange("p a b -> p (a b)")).then_inc(stats, 1)
                dve.wait_ge(stats, START + 3 * t + 3)
                dve.tensor_scalar(mv[:, 2:3], mv[:, 1:2], LN_EPS, None, ALU.add).then_inc(centred, 1)
                dve.wait_ge(rooted, START + t + 1)
                if not (isinstance(t, int) and t == 0):
                    dve.wait_ge(shifted, START + t - 1)
                    dve.wait_ge(turned, START + t - 1)
                dve.tensor_scalar(xh[:, b, :], xin[:, b, :], mv[:, 0:1], mv[:, 3:4], ALU.subtract, ALU.mult).then_inc(normed, 1)

            def logits(t):
                dve.wait_ge(ab_acc, START + t + 1)
                dve.tensor_copy(p.ab[:, ds(t, 1), :].rearrange("p a b -> p (a b)"), ps[:, 5, 0:8]).then_inc(ab_out, 1)

            dve.wait_ge(padded, START + 1)
            norm(0, 0, 32)
            with dve.Fori(0, (NT - 1) // 2) as i:
                norm(2 * i + 1, 1, 16 * i + 16)
                logits(2 * i)
                norm(2 * i + 2, 0, 16 * i + 48)
                logits(2 * i + 1)
            logits(NT - 1)
            dve.wait_ge(ab_out, START + NT)

        @block.tensor
        def _(pe):
            def turn(t, b):
                pe.wait_ge(normed, START + t + 1)
                pe.wait_ge(evacuated, START + t)
                for c in range(KC):
                    m = pe.transpose(ps[:, c // 4, (c % 4) * P:(c % 4 + 1) * P], xh[:, b, c * P:(c + 1) * P], p.ident)
                m.then_inc(turned, 1)

            def products(t, b):
                pe.wait_ge(evacuated, START + t + 1)
                for g, (done, acc) in enumerate(((v_out, v_acc), (zg_out, zg_acc), (zs_out, zs_acc))):
                    pe.wait_ge(done, START + t)
                    for c in range(KC):
                        m = pe.matmul(ps[:, 2 + g, :], cur[b][:, c, :], wt[:, c, 512 * g:512 * g + 512],
                                      start=(c == 0), stop=(c == KC - 1))
                    m.then_inc(acc, 1)
                pe.wait_ge(ab_out, START + t)
                for c in range(KC):
                    m = pe.matmul(ps[:, 5, 0:8], cur[b][:, c, :], wab[:, c, :], start=(c == 0), stop=(c == KC - 1))
                m.then_inc(ab_acc, 1)

            turn(0, 0)
            pe.wait_ge(w_loaded, START + 64)
            with pe.Fori(0, (NT - 1) // 2) as i:
                turn(2 * i + 1, 1)
                products(2 * i, 0)
                turn(2 * i + 2, 0)
                products(2 * i + 1, 1)
            products(NT - 1, 0)

        @block.scalar
        def _(act):
            def evacuate(t, b):
                act.wait_ge(turned, START + t + 1)
                first = isinstance(t, int) and t == 0
                if first:
                    act.wait_ge(padded, START + 2)
                else:
                    if not (isinstance(t, int) and t < 2):
                        act.wait_ge(ab_acc, START + t - 1)
                        act.wait_ge(kept, START + t - 1)
                for c in range(KC):
                    for lo, hi in ((0, NS), (M0, P)) if first else ((0, P),):
                        a = act.activation(cur[b][:, c, lo:hi], ps[:, c // 4, (c % 4) * P + lo:(c % 4) * P + hi],
                                           ACT.Identity, scale=p.lnT[:, c:c + 1], bias=p.lnT[:, 8 + c:9 + c])
                a.then_inc(evacuated, 1)

            def outputs(t, b, v_before, g_before):
                act.wait_ge(v_acc, START + t + 1)
                if not (isinstance(t, int) and t < 2):
                    act.wait_ge(v_stored[b], START + v_before)
                    act.wait_ge(g_stored[b], START + g_before)
                act.activation(vb[:, b, :], ps[:, 2, :], ACT.Copy).then_inc(v_out, 1)
                act.wait_ge(zg_acc, START + t + 1)
                act.activation(gb[:, b, 0:512], ps[:, 3, :], ACT.Silu).then_inc(zg_out, 1)
                act.wait_ge(zs_acc, START + t + 1)
                act.activation(gb[:, b, 512:1024], ps[:, 4, :], ACT.Silu).then_inc(zs_out, 1)

            evacuate(0, 0)
            evacuate(1, 1)
            outputs(0, 0, 0, 0)
            with act.Fori(0, (NT - 1) // 2 - 1) as i:
                evacuate(2 * i + 2, 0)
                outputs(2 * i + 1, 1, 16 * i, 16 * i)
                evacuate(2 * i + 3, 1)
                outputs(2 * i + 2, 0, 16 * i + 32, 16 * i + 16)
            n = (NT - 1) // 2 - 1
            evacuate(NT - 1, 0)
            outputs(NT - 2, 1, 16 * n, 16 * n)
            outputs(NT - 1, 0, 16 * n + 32, 16 * n + 16)


def channel_major(p, hT):
    nc, io, ps = p.nc, p.io, p.ps
    w = io["w_in"][0].rearrange("(c p) n -> p c n", p=P)
    w_in, acc, evac = [p.sem(f"cw{k}_loaded") for k in range(3)], p.sem("c_acc"), p.sem("c_evacuated")
    smp, conv, silu = p.sem("smp_ready"), p.sem("conv_step"), p.sem("c_silu")
    tailed, squared, summed = p.sem("tailed"), p.sem("squared"), p.sem("summed")
    rooted, inverted, scaled, stored = p.sem("c_rooted"), p.sem("inverted"), p.sem("c_scaled"), p.sem("c_stored")
    zeroed, epsd = p.sem("c_zeroed"), p.sem("epsd")
    v_stored = p.sem("cv_stored")
    with ExitStack() as st:
        wc = [p.sb(f"wc{k}", [P, KC, P], stack=st) for k in range(3)]
        pre = [p.sb(f"pre{k}", [P, TOK], stack=st) for k in range(3)]
        y = [p.sb(f"y{k}", [P, TOK], stack=st) for k in range(3)]
        sq = p.sb("sq", [P, TOK], stack=st)
        nrm = p.sb("nrm", [P, TOK], stack=st)
        xs = p.sb("xs", [P, SEQS, 11], stack=st)
        eps = p.sb("eps", [P, 2], stack=st)
        block = p.block(st)
        COLS = (0, 512, 1024)
        STEPS_N = 4 + 4

        @block.sync
        def _(sp):
            def load(h, k):
                sp.dma_start(wc[k][:, :, :], w[:, :, ds(h * P + COLS[k], P)]).then_inc(w_in[k], 16)

            def store(h, k):
                done = stored
                if k < 2:
                    sp.wait_ge(scaled, START + 2 * h + k + 1)
                else:
                    sp.wait_ge(silu, START + 3 * h + 3)
                    done = v_stored
                sp.dma_start(p.chan[ds(h + 4 * k, 1)].rearrange("a p n -> (a p) n"), y[k][:, :]).then_inc(done, 16)

            for k in range(3):
                load(0, k)
            with sp.Fori(0, GH - 1) as h:
                for k in range(3):
                    sp.wait_ge(acc, START + 15 * h + 5 * (k + 1))
                    load(h + 1, k)
                for k in range(3):
                    store(h, k)
            for k in range(3):
                store(GH - 1, k)
            sp.wait_ge(stored, START + 16 * 8)
            sp.wait_ge(v_stored, START + 16 * 4)

        @block.tensor
        def _(pe):
            def products(h, k):
                pe.wait_ge(w_in[k], START + 16 * h + 16)
                for ci, (c0, n) in enumerate(CHUNKS):
                    if k:
                        pe.wait_ge(evac, START + 15 * h + 5 * (k - 1) + ci + 1)
                    else:
                        pe.wait_ge(evac, START + 15 * h)
                    for c in range(KC):
                        m = pe.matmul(ps[:, ci, 0:n], wc[k][:, c, :], hT[:, c, c0:c0 + n], start=(c == 0), stop=(c == KC - 1))
                    m.then_inc(acc, 1)

            def sums(h, k):
                pe.wait_ge(squared, START + 2 * h + k + 1)
                for ci, (c0, n) in enumerate(CHUNKS):
                    pe.wait_ge(rooted, START + 10 * h + 5 * k + max(ci - 2, 0))
                    pe.matmul(ps[:, 5 + ci % 3, 0:n], p.ones, sq[:, c0:c0 + n], start=True, stop=True).then_inc(summed, 1)

            with pe.Fori(0, GH) as h:
                for k in range(3):
                    products(h, k)
                sums(h, 0)
                sums(h, 1)

        @block.scalar
        def _(act):
            def evacuate(h, k):
                for ci, (c0, n) in enumerate(CHUNKS):
                    act.wait_ge(acc, START + 15 * h + 5 * k + ci + 1)
                    if ci == 0:
                        act.wait_ge(tailed, START + 3 * h + k)
                    act.activation(pre[k][:, c0:c0 + n], ps[:, ci, 0:n], ACT.Copy).then_inc(evac, 1)

            def swish(h, k):
                act.wait_ge(conv, START + 8 * (3 * h + k + 1))
                act.activation(y[k][:, 0:NS], y[k][:, 0:NS], ACT.Silu)
                act.activation(y[k][:, M0:TOK], y[k][:, M0:TOK], ACT.Silu).then_inc(silu, 1)

            def root(h, k):
                for ci, (c0, n) in enumerate(CHUNKS):
                    act.wait_ge(summed, START + 10 * h + 5 * k + ci + 1)
                    if ci == 0:
                        act.wait_ge(scaled, START + 2 * h + k)
                    act.activation(nrm[:, c0:c0 + n], ps[:, 5 + ci % 3, 0:n], ACT.Sqrt,
                                   scale=float(DK) if k == 0 else 1.0, bias=eps[:, k:k + 1]).then_inc(rooted, 1)

            act.wait_ge(epsd, START + 2)
            with act.Fori(0, GH) as h:
                evacuate(h, 0)
                evacuate(h, 1)
                swish(h, 0)
                swish(h, 1)
                evacuate(h, 2)
                root(h, 0)
                root(h, 1)
                swish(h, 2)

        @block.vector
        def _(dve):
            for k in range(3):
                dve.memset(y[k][:, NS:M0], 0.0).then_inc(zeroed, 1)
            dve.memset(eps[:, 0:1], L2_EPS * DK).then_inc(epsd, 1)
            dve.memset(eps[:, 1:2], L2_EPS).then_inc(epsd, 1)
            dve.wait_ge(zeroed, START + 3)

            def convolve(h, k):
                n = 3 * h + k
                wt = [p.sc[:, ds(h + 4 * k, 1), 24 + i:25 + i].rearrange("p a b -> p (a b)") for i in range(CONV)]
                dve.wait_ge(evac, START + 5 * (n + 1))
                if k < 2:
                    dve.wait_ge(stored, START + 32 * h)
                else:
                    dve.wait_ge(v_stored, START + 16 * h)
                dve.wait_ge(tailed, START + n)
                dve.tensor_copy(xs[:, :, 0:3], p.sc[:, ds(h + 4 * k, 1), 0:24].rearrange("p a (b i) -> p (a b) i", i=3)).then_inc(smp, 1)
                dve.tensor_copy(xs[:, :, 3:11], pre[k][:, 0:NS].rearrange("p (b t) -> p b t", t=STEPS)).then_inc(smp, 1)
                dve.wait_ge(smp, START + 2 * (n + 1))
                ys = y[k][:, 0:NS].rearrange("p (b t) -> p b t", t=STEPS)
                for i in range(CONV):
                    src, srcs = pre[k][:, M0 - 3 + i:TOK - 3 + i], xs[:, :, i:i + STEPS]
                    if i == 0:
                        dve.tensor_scalar(y[k][:, M0:TOK], src, wt[i], None, ALU.mult).then_inc(conv, 1)
                        dve.tensor_scalar(ys, srcs, wt[i], None, ALU.mult).then_inc(conv, 1)
                    else:
                        dve.wait_ge(conv, START + 8 * n + 2 * i)
                        dve.scalar_tensor_tensor(out=y[k][:, M0:TOK], in0=src, scalar=wt[i], in1=y[k][:, M0:TOK], op0=ALU.mult, op1=ALU.add).then_inc(conv, 1)
                        dve.scalar_tensor_tensor(out=ys, in0=srcs, scalar=wt[i], in1=ys, op0=ALU.mult, op1=ALU.add).then_inc(conv, 1)
                dve.tensor_copy(p.tails[:, ds(h + 4 * k, 1), 0:24].rearrange("p a (b i) -> p (a b) i", i=3), xs[:, :, STEPS:STEPS + 3])
                dve.tensor_copy(p.tails[:, ds(h + 4 * k, 1), 24:27].rearrange("p a b -> p (a b)"), pre[k][:, TOK - 3:TOK]).then_inc(tailed, 1)

            def scale(h, k):
                dve.wait_ge(rooted, START + 10 * h + 5 * (k + 1))
                dve.reciprocal(nrm[:, :], nrm[:, :]).then_inc(inverted, 1)
                dve.wait_ge(inverted, START + 2 * h + k + 1)
                dve.tensor_tensor(y[k][:, :], y[k][:, :], nrm[:, :], ALU.mult).then_inc(scaled, 1)

            with dve.Fori(0, GH) as h:
                convolve(h, 0)
                convolve(h, 1)
                convolve(h, 2)
                scale(h, 0)
                scale(h, 1)

        @block.gpsimd
        def _(pool):
            pool.wait_ge(zeroed, START + 3)

            def square(h, k):
                pool.wait_ge(silu, START + 3 * h + k + 1)
                if k:
                    pool.wait_ge(summed, START + 10 * h + 5)
                else:
                    pool.wait_ge(summed, START + 10 * h)
                pool.tensor_tensor(sq[:, :], y[k][:, :], y[k][:, :], ALU.mult).then_inc(squared, 1)

            with pool.Fori(0, GH) as h:
                square(h, 0)
                square(h, 1)


def attention_heads(p, hT):
    nc, io, ps = p.nc, p.io, p.ps
    w = io["w_in"][0].rearrange("(c p) n -> p c n", p=P)
    w_in, acc, evac, stored = [p.sem(f"aw{k}_loaded") for k in range(2)], p.sem("a_acc"), p.sem("a_evac"), p.sem("a_stored")
    turned, out, k_stored = p.sem("k_turned"), p.sem("k_out"), p.sem("k_stored")
    k_p = io["k_prompt"][0, 0].rearrange("l h d -> l (h d)")
    k_s = io["k_sample"][0].rearrange("b t h d -> (b t) (h d)")
    groups = [(g, min(4, NT - 4 * g)) for g in range(5)]
    with ExitStack() as st:
        wc = [p.sb(f"wa{k}", [P, KC, P], stack=st) for k in range(2)]
        y = [p.sb(f"ya{k}", [P, TOK], stack=st) for k in range(2)]
        kr = p.sb("kr", [P, NT, P], stack=st)
        block = p.block(st)

        @block.sync
        def _(sp):
            def load(h, k):
                sp.dma_start(wc[k][:, :, :], w[:, :, ds(h * P + (COL_Q, COL_K)[k], P)]).then_inc(w_in[k], 16)

            def store(h):
                sp.wait_ge(evac, START + 10 * h + 10)
                sp.dma_start(p.chan[ds(h + 12, 1)].rearrange("a p n -> (a p) n"), y[0][:, :]).then_inc(stored, 16)
                sp.dma_start(p.chan[ds(h + 16, 1)].rearrange("a p n -> (a p) n"), y[1][:, :]).then_inc(stored, 16)
                sp.wait_ge(out, START + 5 * h + 5)
                cols = ds(h * P, P)
                sp.dma_start(k_p[N_META:, cols].rearrange("(t p) n -> p t n", p=P), kr[:, 1:, :]).then_inc(k_stored, 16)
                sp.dma_start(k_p[0:N_META, cols], kr[M0:P, 0, :]).then_inc(k_stored, 16)
                sp.dma_start(k_s[:, cols], kr[0:NS, 0, :]).then_inc(k_stored, 16)

            for k in range(2):
                load(0, k)
            with sp.Fori(0, PAIRS - 1) as h:
                for k in range(2):
                    sp.wait_ge(acc, START + 10 * h + 5 * (k + 1))
                    load(h + 1, k)
                store(h)
            store(PAIRS - 1)
            sp.wait_ge(stored, START + 16 * 8)
            sp.wait_ge(k_stored, START + 48 * 4)

        @block.tensor
        def _(pe):
            with pe.Fori(0, PAIRS) as h:
                for k in range(2):
                    pe.wait_ge(w_in[k], START + 16 * h + 16)
                    for ci, (c0, n) in enumerate(CHUNKS):
                        pe.wait_ge(evac, START + (10 * h + (ci + 1 if k else 0)))
                        for c in range(KC):
                            m = pe.matmul(ps[:, ci, 0:n], wc[k][:, c, :], hT[:, c, c0:c0 + n], start=(c == 0), stop=(c == KC - 1))
                        m.then_inc(acc, 1)
                pe.wait_ge(evac, START + 10 * h + 10)
                for g, n in groups:
                    pe.wait_ge(out, START + 5 * h + max(g - 2, 0))
                    for j in range(n):
                        m = pe.transpose(ps[:, 5 + g % 3, j * P:(j + 1) * P], y[1][:, (4 * g + j) * P:(4 * g + j + 1) * P], p.ident)
                    m.then_inc(turned, 1)

        @block.scalar
        def _(act):
            with act.Fori(0, PAIRS) as h:
                for k in range(2):
                    for ci, (c0, n) in enumerate(CHUNKS):
                        act.wait_ge(acc, START + 10 * h + 5 * k + ci + 1)
                        if ci == 0:
                            act.wait_ge(stored, START + 32 * h)
                            act.wait_ge(turned, START + 5 * h)
                        act.activation(y[k][:, c0:c0 + n], ps[:, ci, 0:n], ACT.Copy).then_inc(evac, 1)

        @block.vector
        def _(dve):
            with dve.Fori(0, PAIRS) as h:
                for g, n in groups:
                    dve.wait_ge(turned, START + 5 * h + g + 1)
                    if g == 0:
                        dve.wait_ge(k_stored, START + 48 * h)
                    dve.tensor_copy(kr[:, 4 * g:4 * g + n, :].rearrange("p a b -> p (a b)"), ps[:, 5 + g % 3, 0:n * P]).then_inc(out, 1)


def delta_gates(p):
    nc = p.nc
    d, a = p.sem("dg_vector"), p.sem("dg_scalar")
    shape = [P, NT, GH]
    with ExitStack() as st:
        x, ax, e, sp, eb = [p.sb(n, shape, stack=st) for n in ("g_x", "g_ax", "g_e", "g_sp", "g_eb")]
        ea = p.sb("g_ea", [P, GH], stack=st)
        one = p.sb("g_one", [P, 1], stack=st)
        before = p.sb("g_before", [P, 1], stack=st)
        block = p.block(st)

        @block.vector
        def _(dve):
            dve.memset(one[:, :], 1.0).then_inc(d, 1)
            dve.tensor_tensor(x[:, :, :], p.ab[:, :, 0:4], p.small[:, 4:8].unsqueeze(1).broadcast_to(shape), ALU.add).then_inc(d, 1)
            dve.tensor_scalar(before[:, :], p.utri[:, M0 - 1:M0], -1.0, 1.0, ALU.mult, ALU.add).then_inc(d, 1)
            dve.wait_ge(d, START + 3)
            dve.tensor_scalar(ax[:, :, :], x[:, :, :], -1.0, None, ALU.mult).then_inc(d, 1)
            dve.wait_ge(d, START + 4)
            dve.tensor_tensor(ax[:, :, :], ax[:, :, :], x[:, :, :], ALU.max).then_inc(d, 1)
            dve.wait_ge(a, START + 4)
            dve.scalar_tensor_tensor(out=sp[:, :, :], in0=x[:, :, :], scalar=0.0, in1=sp[:, :, :], op0=ALU.max, op1=ALU.add).then_inc(d, 1)
            dve.tensor_scalar(eb[:, :, :], eb[:, :, :], 1.0, None, ALU.add).then_inc(d, 1)
            dve.wait_ge(d, START + 7)
            dve.scalar_tensor_tensor(out=p.g[:, :, :], in0=sp[:, :, :], scalar=-1.0, in1=ea[:, :].unsqueeze(1).broadcast_to(shape), op0=ALU.mult, op1=ALU.mult).then_inc(d, 1)
            dve.reciprocal(p.beta[:, :, :], eb[:, :, :]).then_inc(d, 1)
            dve.wait_ge(d, START + 9)
            dve.tensor_copy(p.g_s[:, :], p.g[:, 0, :]).then_inc(d, 1)
            dve.wait_ge(d, START + 10)
            dve.tensor_scalar(p.g[:, 0, :], p.g[:, 0, :], before[:, 0:1], None, ALU.mult).then_inc(d, 1)
            dve.wait_ge(d, START + 11)

        @block.scalar
        def _(act):
            act.wait_ge(d, START + 5)
            act.activation(e[:, :, :], ax[:, :, :], ACT.Exp, scale=-1.0).then_inc(a, 1)
            act.activation(ea[:, :], p.small[:, 0:4], ACT.Exp).then_inc(a, 1)
            act.activation(eb[:, :, :], p.ab[:, :, 4:8], ACT.Exp, scale=-1.0).then_inc(a, 1)
            act.wait_ge(a, START + 3)
            act.activation(sp[:, :, :], e[:, :, :], ACT.Ln, bias=one[:, 0:1]).then_inc(a, 1)


def delta_net(p):
    nc, ps = p.nc, p.ps
    loaded = [p.sem("d_even_loaded"), p.sem("d_odd_loaded")]
    names = ("g_spread", "g_now", "G_acc", "kk_acc", "qk_acc", "G_col", "G_diff", "G_clamped", "decays", "edges",
             "E2_masked", "A_ready", "qk_ready", "kv_turned", "kd_ready", "v_ready", "levels_masked", "scaled_by_G",
             "m0_turned", "T_begun", "Ub_ready", "ks_acc", "rhs_ready", "vn_acc", "vn_ready", "o_acc", "o_ready",
             "ds_acc", "state", "o_stored", "zeroed_d", "s_stored")
    s = {n: p.sem("d_" + n) for n in names}
    q_acc, q_out, ut_acc, ut_done = p.sem("Q_acc"), p.sem("Q_out"), p.sem("UT_acc"), p.sem("UT_done")
    LV = 2 * (LEVELS - 1)
    G_BANK, K_BANK, Q_BANK, KS_BANK, VN_BANK, O_BANK = range(6)

    def heads(bank, h=None, n=P):
        v = ps[:, bank, :].rearrange("p (h n) -> p h n", h=GH)
        return v if h is None else v[:, h, :]

    with ExitStack() as st:
        def sb(name, shape=(P, GH, P)):
            return p.sb(name, list(shape), stack=st)

        ld = [sb(f"d_ld{b}", (P, 12, P)) for b in range(2)]
        kE, qE, QK, kd, vt, Ub = ([sb(f"d_{n}{b}") for b in range(2)] for n in ("kE", "qE", "QK", "kd", "vt", "Ub"))
        last = [sb(f"d_last{b}", (P, GH)) for b in range(2)]
        gB, dif, E1, E2, EG, A = (sb("d_" + n) for n in ("gB", "dif", "E1", "E2", "EG", "A"))
        ML = sb("d_ML", (P, LEVELS, GH, P))
        UT = [sb(f"d_UT{g}", (P, 2, 2, P)) for g in range(2)]
        Qs = [sb(f"d_Qs{g}", (P, 2, P)) for g in range(2)]
        gc, Gc, beta = sb("d_gc", (P, GH)), sb("d_Gc", (P, GH)), sb("d_beta", (P, GH))
        rhs, Vn, ob, S = sb("d_rhs"), sb("d_Vn"), sb("d_ob"), sb("d_S")
        bc = [P, GH, P]
        chan = p.chan[0:12].rearrange("c p n -> p c n")
        block = p.block(st)

        def once_per_turn(eng, t, what, value):
            if not isinstance(t, int) or value > 0:
                eng.wait_ge(s[what], START + value)

        @block.sync
        def _(sp):
            sp.wait_ge(s["zeroed_d"], START + 2)
            sp.dma_start(ld[0][:, :, M0:P], chan[:, :, M0:P]).then_inc(loaded[0], 16)
            sp.dma_start(ld[1][:, :, :], chan[:, :, P:2 * P]).then_inc(loaded[1], 16)

            def load(t, b):
                sp.wait_ge(s["kv_turned"], START + t - 1)
                sp.wait_ge(s["scaled_by_G"], START + t - 1)
                sp.dma_start(ld[b][:, :, :], chan[:, :, ds(t * P, P)]).then_inc(loaded[b], 16)

            def store(t):
                sp.wait_ge(s["o_ready"], START + t + 1)
                sp.dma_start(p.o_rows[ds(t, 1)].rearrange("a p n -> (a p) n")[:, 0:HALF],
                             ob[:, :, :].rearrange("p h n -> p (h n)")).then_inc(s["o_stored"], 16)

            with sp.Fori(0, (NT - 1) // 2 - 1) as i:
                load(2 * i + 2, 0)
                store(2 * i)
                load(2 * i + 3, 1)
                store(2 * i + 1)
            load(NT - 1, 0)
            for t in (NT - 3, NT - 2, NT - 1):
                store(t)
            sp.wait_ge(s["state"], START + NT + 1)
            sp.dma_start(p.io["gdn_prompt"][0, 0].rearrange("h k v -> k h v"), S[:, :, :]).then_inc(s["s_stored"], 16)
            sp.wait_ge(s["o_stored"], START + 16 * NT)
            sp.wait_ge(s["s_stored"], START + 16)

        @block.tensor
        def _(pe):
            def begin(t, b, ld_count):
                pe.wait_ge(s["g_spread"], START + t + 1)
                pe.wait_ge(s["decays"], START + t)
                pe.wait_ge(s["kd_ready"], START + t)
                pe.wait_ge(s["v_ready"], START + t)
                for h in range(GH):
                    pe.matmul(heads(G_BANK, h), gB[:, h, :], p.utri, start=True, stop=True)
                pe.matmul(ps[:, Q_BANK, 0:GH], p.utri, gc[:, :], start=True, stop=True).then_inc(s["G_acc"], 1)
                pe.wait_ge(loaded[b], START + ld_count)
                for h in range(GH):
                    m = pe.matmul(heads(K_BANK, h), ld[b][:, GH + h, :], ld[b][:, GH + h, :], start=True, stop=True)
                m.then_inc(s["kk_acc"], 1)
                pe.wait_ge(s["G_col"], START + t + 1)
                for h in range(GH):
                    m = pe.matmul(heads(Q_BANK, h), ld[b][:, GH + h, :], ld[b][:, h, :], start=True, stop=True)
                m.then_inc(s["qk_acc"], 1)

            def turn(t, b):
                pe.wait_ge(s["A_ready"], START + t + 1)
                pe.wait_ge(s["qk_ready"], START + t + 1)
                for h in range(GH):
                    pe.transpose(heads(K_BANK, h), ld[b][:, GH + h, :], p.ident)
                    m = pe.transpose(heads(Q_BANK, h), ld[b][:, 2 * GH + h, :], p.ident)
                m.then_inc(s["kv_turned"], 1)

            def turn_m0(t):
                pe.wait_ge(s["levels_masked"], START + LEVELS * t + 1)
                for h in range(GH):
                    m = pe.transpose(ps[:, 6 + h // 2, (h % 2) * P:(h % 2 + 1) * P], ML[:, 0, h, :], p.ident)
                m.then_inc(s["m0_turned"], 1)

            def level_q(t, l):
                if l == 1:
                    pe.wait_ge(s["T_begun"], START + t + 1)
                pe.wait_ge(s["levels_masked"], START + LEVELS * t + l + 1)
                for g in range(2):
                    if l > 1:
                        pe.wait_ge(ut_done, START + LV * t + 2 * (l - 2) + g + 1)
                    for h in range(2):
                        m = pe.matmul(ps[:, 6 + g, h * P:(h + 1) * P], ML[:, l, 2 * g + h, :], UT[g][:, 1, h, :], start=True, stop=True)
                    m.then_inc(q_acc, 1)

            def level_ut(t, l):
                for g in range(2):
                    pe.wait_ge(q_out, START + LV * t + 2 * (l - 1) + g + 1)
                    for h in range(2):
                        m = pe.matmul(ps[:, 6 + g, (2 + h) * P:(3 + h) * P], UT[g][:, 0, h, :], Qs[g][:, h, :], start=True, stop=True)
                    if l < LEVELS - 1:
                        for h in range(2):
                            m = pe.matmul(ps[:, 6 + g, h * P:(h + 1) * P], Qs[g][:, h, :], UT[g][:, 0, h, :], start=True, stop=True)
                    m.then_inc(ut_acc, 1)

            def state_ks(t, b):
                pe.wait_ge(s["state"], START + t + 1)
                pe.wait_ge(s["scaled_by_G"], START + t + 1)
                for h in range(GH):
                    m = pe.matmul(heads(KS_BANK, h), kE[b][:, h, :], S[:, h, :], start=True, stop=True)
                m.then_inc(s["ks_acc"], 1)

            def state_vn(t, b):
                pe.wait_ge(s["rhs_ready"], START + t + 1)
                pe.wait_ge(s["Ub_ready"], START + t + 1)
                for h in range(GH):
                    m = pe.matmul(heads(VN_BANK, h), Ub[b][:, h, :], rhs[:, h, :], start=True, stop=True)
                m.then_inc(s["vn_acc"], 1)

            def state_update(t, b):
                pe.wait_ge(s["vn_ready"], START + t + 1)
                for h in range(GH):
                    m = pe.matmul(heads(KS_BANK, h), kd[b][:, h, :], Vn[:, h, :], start=True, stop=True)
                m.then_inc(s["ds_acc"], 1)

            def outputs(t, b):
                pe.wait_ge(s["o_ready"], START + t)
                for h in range(GH):
                    pe.matmul(heads(O_BANK, h), qE[b][:, h, :], S[:, h, :], start=True, stop=False)
                    m = pe.matmul(heads(O_BANK, h), QK[b][:, h, :], Vn[:, h, :], start=False, stop=True)
                m.then_inc(s["o_acc"], 1)

            def prepare(t, b, ld_count, state=None):
                begin(t, b, ld_count)
                if state:
                    state_ks(*state)
                turn(t, b)
                turn_m0(t)
                if state:
                    state_vn(*state)
                level_q(t, 1)
                if state:
                    state_update_and_outputs(*state)
                level_ut(t, 1)
                for l in range(2, LEVELS):
                    level_q(t, l)
                    level_ut(t, l)

            def state_update_and_outputs(t, b):
                pe.wait_ge(s["vn_ready"], START + t + 1)
                outputs(t, b)
                state_update(t, b)

            prepare(0, 0, 16)
            with pe.Fori(0, (NT - 1) // 2) as i:
                prepare(2 * i + 1, 1, 16 * i + 16, (2 * i, 0))
                prepare(2 * i + 2, 0, 16 * i + 32, (2 * i + 1, 1))
            state_ks(NT - 1, 0)
            state_vn(NT - 1, 0)
            state_update_and_outputs(NT - 1, 0)

        @block.vector
        def _(dve):
            def spread(t):
                once_per_turn(dve, t, "Ub_ready", t)
                once_per_turn(dve, t, "G_acc", t)
                dve.tensor_copy(gc[:, :], p.g[:, ds(t, 1), :].rearrange("p a h -> p (a h)")).then_inc(s["g_now"], 1)
                dve.tensor_copy(beta[:, :], p.beta[:, ds(t, 1), :].rearrange("p a h -> p (a h)")).then_inc(s["g_now"], 1)
                dve.wait_ge(s["g_now"], START + 2 * t + 2)
                dve.tensor_copy(gB[:, :, :], gc[:, :].unsqueeze(2).broadcast_to(bc)).then_inc(s["g_spread"], 1)

            def decays(t):
                dve.wait_ge(s["G_acc"], START + t + 1)
                dve.tensor_copy(Gc[:, :], ps[:, Q_BANK, 0:GH]).then_inc(s["G_col"], 1)
                dve.wait_ge(s["G_col"], START + t + 1)
                dve.tensor_tensor(dif[:, :, :], heads(G_BANK), Gc[:, :].unsqueeze(2).broadcast_to(bc), ALU.subtract).then_inc(s["G_diff"], 1)
                dve.wait_ge(s["G_diff"], START + t + 1)
                dve.tensor_scalar(E1[:, :, :], dif[:, :, :], 0.0, None, ALU.max).then_inc(s["G_clamped"], 1)
                once_per_turn(dve, t, "E2_masked", t)
                dve.tensor_scalar(E2[:, :, :], dif[:, :, :], 0.0, None, ALU.min).then_inc(s["G_clamped"], 1)

            def products(t, b):
                dve.wait_ge(s["decays"], START + t + 1)
                dve.wait_ge(s["kk_acc"], START + t + 1)
                for h in range(GH):
                    m = dve.scalar_tensor_tensor(out=A[:, h, :], in0=heads(K_BANK, h), scalar=beta[:, h:h + 1], in1=E1[:, h, :], op0=ALU.mult, op1=ALU.mult)
                m.then_inc(s["A_ready"], 1)
                dve.wait_ge(s["E2_masked"], START + t + 1)
                dve.wait_ge(s["qk_acc"], START + t + 1)
                dve.tensor_tensor(QK[b][:, :, :], heads(Q_BANK), E2[:, :, :], ALU.mult).then_inc(s["qk_ready"], 1)
                dve.wait_ge(s["kv_turned"], START + t + 1)
                dve.tensor_tensor(kd[b][:, :, :], heads(K_BANK), E2[:, :, P - 1:P].broadcast_to(bc), ALU.mult).then_inc(s["kd_ready"], 1)
                for g in range(2):
                    if g == 0:
                        dve.wait_ge(s["levels_masked"], START + LEVELS * t + 1)
                    dve.tensor_tensor(UT[g][:, 0, :, :], p.ident.unsqueeze(1).broadcast_to([P, 2, P]), ML[:, 0, 2 * g:2 * g + 2, :], ALU.subtract)
                dve.wait_ge(s["m0_turned"], START + t + 1)
                for g in range(2):
                    m = dve.tensor_tensor(UT[g][:, 1, :, :], p.ident.unsqueeze(1).broadcast_to([P, 2, P]),
                                          ps[:, 6 + g, 0:2 * P].rearrange("p (h n) -> p h n", h=2), ALU.subtract)
                m.then_inc(s["T_begun"], 1)

            def level(t, l):
                for g in range(2):
                    dve.wait_ge(ut_acc, START + LV * t + 2 * (l - 1) + g + 1)
                    if l < LEVELS - 1:
                        v = UT[g][:, :, :, :].rearrange("p u h n -> p (u h n)")
                        dve.tensor_tensor(v, v, ps[:, 6 + g, :], ALU.subtract).then_inc(ut_done, 1)
                    else:
                        v = UT[g][:, 1, :, :].rearrange("p h n -> p (h n)")
                        dve.tensor_tensor(v, v, ps[:, 6 + g, 2 * P:4 * P], ALU.subtract).then_inc(ut_done, 1)

            def finish(t, b):
                dve.wait_ge(ut_done, START + LV * t + LV)
                for g in range(2):
                    m = dve.tensor_tensor(Ub[b][:, 2 * g:2 * g + 2, :], UT[g][:, 1, :, :],
                                          beta[:, 2 * g:2 * g + 2].unsqueeze(2).broadcast_to([P, 2, P]), ALU.mult)
                m.then_inc(s["Ub_ready"], 1)

            def state_rhs(t, b):
                dve.wait_ge(s["ks_acc"], START + t + 1)
                dve.wait_ge(s["v_ready"], START + t + 1)
                dve.tensor_tensor(rhs[:, :, :], vt[b][:, :, :], heads(KS_BANK), ALU.subtract).then_inc(s["rhs_ready"], 1)

            def state_update(t, b):
                dve.wait_ge(s["ds_acc"], START + t + 1)
                dve.wait_ge(s["o_acc"], START + t + 1)
                for h in range(GH):
                    m = dve.scalar_tensor_tensor(out=S[:, h, :], in0=S[:, h, :], scalar=last[b][:, h:h + 1], in1=heads(KS_BANK, h), op0=ALU.mult, op1=ALU.add)
                m.then_inc(s["state"], 1)

            def prepare(t, b, state=None):
                spread(t)
                decays(t)
                if state:
                    state_rhs(*state)
                products(t, b)
                if state:
                    state_update(*state)
                for l in range(1, LEVELS):
                    level(t, l)
                finish(t, b)

            dve.memset(S[:, :, :], 0.0).then_inc(s["state"], 1)
            prepare(0, 0)
            with dve.Fori(0, (NT - 1) // 2) as i:
                prepare(2 * i + 1, 1, (2 * i, 0))
                prepare(2 * i + 2, 0, (2 * i + 1, 1))
            state_rhs(NT - 1, 0)
            state_update(NT - 1, 0)

        @block.scalar
        def _(act):
            def decays(t, b):
                act.wait_ge(s["G_clamped"], START + 2 * t + 2)
                act.activation(E1[:, :, :], E1[:, :, :], ACT.Exp, scale=-1.0)
                act.activation(E2[:, :, :], E2[:, :, :], ACT.Exp)
                once_per_turn(act, t, "scaled_by_G", t)
                act.activation(EG[:, :, :], heads(G_BANK), ACT.Exp).then_inc(s["decays"], 1)
                if not isinstance(t, int) or t >= 2:
                    act.wait_ge(s["state"], START + t)
                act.activation(last[b][:, :], heads(G_BANK)[:, :, P - 1], ACT.Exp).then_inc(s["edges"], 1)

            def values(t, b):
                act.wait_ge(s["kv_turned"], START + t + 1)
                act.activation(vt[b][:, :, :], heads(Q_BANK), ACT.Copy).then_inc(s["v_ready"], 1)

            def level(t, l):
                for g in range(2):
                    act.wait_ge(q_acc, START + LV * t + 2 * (l - 1) + g + 1)
                    act.activation(Qs[g][:, :, :], ps[:, 6 + g, 0:2 * P].rearrange("p (h n) -> p h n", h=2), ACT.Copy).then_inc(q_out, 1)

            def state_vn(t):
                act.wait_ge(s["vn_acc"], START + t + 1)
                act.activation(Vn[:, :, :], heads(VN_BANK), ACT.Copy).then_inc(s["vn_ready"], 1)

            def outputs(t):
                act.wait_ge(s["o_acc"], START + t + 1)
                act.wait_ge(s["o_stored"], START + 16 * t)
                act.activation(ob[:, :, :], heads(O_BANK), ACT.Copy).then_inc(s["o_ready"], 1)

            def prepare(t, b, state=None):
                decays(t, b)
                values(t, b)
                if state is not None:
                    state_vn(state)
                level(t, 1)
                if state is not None:
                    outputs(state)
                for l in range(2, LEVELS):
                    level(t, l)

            prepare(0, 0)
            with act.Fori(0, (NT - 1) // 2) as i:
                prepare(2 * i + 1, 1, 2 * i)
                prepare(2 * i + 2, 0, 2 * i + 1)
            state_vn(NT - 1)
            outputs(NT - 1)

        @block.gpsimd
        def _(pool):
            def prepare(t, b, ld_count):
                pool.wait_ge(s["decays"], START + t + 1)
                pool.tensor_tensor(E2[:, :, :], E2[:, :, :], p.utri.unsqueeze(1).broadcast_to(bc), ALU.mult).then_inc(s["E2_masked"], 1)
                pool.wait_ge(s["A_ready"], START + t + 1)
                for l in range(LEVELS):
                    mask = p.con[:, C_LM + l * P:C_LM + (l + 1) * P].unsqueeze(1).broadcast_to(bc)
                    pool.tensor_tensor(ML[:, l, :, :], A[:, :, :], mask, ALU.mult).then_inc(s["levels_masked"], 1)
                    if l == 2:
                        if not isinstance(t, int) or t >= 2:
                            pool.wait_ge(s["o_acc"], START + t - 1)
                        pool.wait_ge(loaded[b], START + ld_count)
                        pool.tensor_tensor(kE[b][:, :, :], ld[b][:, GH:2 * GH, :], EG[:, :, :], ALU.mult)
                        pool.tensor_tensor(qE[b][:, :, :], ld[b][:, 0:GH, :], EG[:, :, :], ALU.mult).then_inc(s["scaled_by_G"], 1)

            pool.memset(ld[0][:, :, 0:M0], 0.0).then_inc(s["zeroed_d"], 1)
            pool.wait_ge(s["zeroed_d"], START + 1)
            pool.memset(ob[:, :, :], 0.0).then_inc(s["zeroed_d"], 1)
            prepare(0, 0, 16)
            with pool.Fori(0, (NT - 1) // 2) as i:
                prepare(2 * i + 1, 1, 16 * i + 16)
                prepare(2 * i + 2, 0, 16 * i + 32)


def conv_states(p):
    nc, ps = p.nc, p.ps
    turned, out, stored = p.sem("cs_turned"), p.sem("cs_out"), p.sem("cs_stored")
    with ExitStack() as st:
        rows = p.sb("cs_rows", [27, CB * P], stack=st)
        block = p.block(st)

        @block.tensor
        def _(pe):
            for c in range(CB):
                m = pe.transpose(ps[0:27, c // 4, (c % 4) * P:(c % 4 + 1) * P], p.tails[:, c, :], p.ident)
            m.then_inc(turned, 1)

        @block.vector
        def _(dve):
            dve.wait_ge(turned, START + 1)
            for c in range(3):
                dve.tensor_copy(rows[:, 512 * c:512 * c + 512], ps[0:27, c, :]).then_inc(out, 1)

        @block.sync
        def _(sp):
            sp.wait_ge(out, START + 3)
            sp.dma_start(p.io["conv_sample"][0].rearrange("b i n -> (b i) n"), rows[0:24, :]).then_inc(stored, 16)
            sp.dma_start(p.io["conv_prompt"][0, 0], rows[24:27, :]).then_inc(stored, 16)
            sp.wait_ge(stored, START + 32)


def sample_delta(p):
    nc, ps = p.nc, p.ps
    names = ("loaded", "spread", "G_acc", "G_col", "dif", "clamped", "decays", "kk_acc", "A_ready", "masked", "E2_masked",
             "QK_ready", "k_turned", "kd_ready", "m0_turned", "T_begun", "Q_acc", "Q_out", "UT_acc", "UT_done", "Ub_ready",
             "scaled", "ks_acc", "rhsT_ready", "rhs_turned", "rhs_ready", "vn_acc", "vn_ready", "oT_acc", "oT_ready",
             "o_turned", "o_ready", "ds_acc", "s_ready", "stored")
    s = {n: p.sem("e_" + n) for n in names}
    u8 = p.con[0:NS, C_U8:C_U8 + NS]
    ident = p.con[0:NS, C_ID:C_ID + NS]
    bc = [NS, GH, NS]
    with ExitStack() as st:
        def sb(name, *shape):
            return p.sb("e_" + name, list(shape), stack=st)

        ld, S = sb("ld", P, 12, NS), sb("S", P, SEQS, GH, P)
        gB, Gc = sb("gB", NS, GH, P), sb("Gc", NS, GH)
        dif, E1, E2, A = (sb(n, NS, GH, NS) for n in ("dif", "E1", "E2", "A"))
        EG, kE, qE = (sb(n, P, GH, NS) for n in ("EG", "kE", "qE"))
        ML, T, U, Qs, QK, Ub = sb("ML", NS, 3, GH, NS), *(sb(n, NS, GH, NS) for n in ("T", "U", "Qs", "QK", "Ub"))
        kd = sb("kd", NS, SEQS, GH, P)
        rhsT, oT = sb("rhsT", P, GH, NS), sb("oT", P, GH, NS)
        rhs, Vn, ob = (sb(n, NS, GH, P) for n in ("rhs", "Vn", "ob"))
        block = p.block(st)

        def b64(bank, half=0):
            return ps[0:NS, bank, 256 * half:256 * half + 256].rearrange("p (h n) -> p h n", h=GH)

        def b128(bank, n=NS):
            return ps[0:n, bank, :].rearrange("p (h n) -> p h n", h=GH)

        def c64(bank):
            return ps[:, bank, 0:256].rearrange("p (h n) -> p h n", h=GH)

        @block.sync
        def _(sp):
            sp.dma_start(ld[:, :, :], p.chan[0:12].rearrange("c p n -> p c n")[:, :, 0:NS]).then_inc(s["loaded"], 16)
            sp.dma_start(S[:, :, :, :].rearrange("p b h n -> p (b h) n"), p.io["state_gdn"][0].rearrange("b h k v -> k (b h) v")).then_inc(s["loaded"], 16)
            sp.wait_ge(s["o_ready"], START + 1)
            sp.dma_start(p.o_rows[0][0:NS, 0:HALF], ob[:, :, :].rearrange("p h n -> p (h n)")).then_inc(s["stored"], 16)
            sp.wait_ge(s["s_ready"], START + SEQS)
            sp.dma_start(p.io["gdn_sample"][0].rearrange("b h k v -> k (b h) v"), S[:, :, :, :].rearrange("p b h n -> p (b h) n")).then_inc(s["stored"], 16)
            sp.wait_ge(s["stored"], START + 32)

        @block.tensor
        def _(pe):
            pe.wait_ge(s["spread"], START + 1)
            for h in range(GH):
                pe.matmul(c64(0)[:, h, :], gB[:, h, :], u8, start=True, stop=True)
            pe.matmul(ps[0:NS, 1, 0:GH], u8, p.g_s[0:NS, :], start=True, stop=True).then_inc(s["G_acc"], 1)
            pe.wait_ge(s["loaded"], START + 32)
            for h in range(GH):
                pe.matmul(b64(2)[:, h, :], ld[:, GH + h, :], ld[:, GH + h, :], start=True, stop=True)
                m = pe.matmul(b64(3)[:, h, :], ld[:, GH + h, :], ld[:, h, :], start=True, stop=True)
            m.then_inc(s["kk_acc"], 1)
            for h in range(GH):
                m = pe.transpose(b128(4)[:, h, :], ld[:, GH + h, :], p.ident)
            m.then_inc(s["k_turned"], 1)
            pe.wait_ge(s["masked"], START + 3)
            for h in range(GH):
                m = pe.transpose(b64(5)[:, h, :], ML[:, 0, h, :], ident)
            m.then_inc(s["m0_turned"], 1)
            pe.wait_ge(s["scaled"], START + 2)
            for b in range(SEQS):
                for h in range(GH):
                    m = pe.matmul(c64(6)[:, h, STEPS * b:STEPS * b + STEPS], S[:, b, h, :], kE[:, h, STEPS * b:STEPS * b + STEPS], start=True, stop=True)
            m.then_inc(s["ks_acc"], 1)
            pe.wait_ge(s["T_begun"], START + 1)
            for l in (1, 2):
                if l == 2:
                    pe.wait_ge(s["UT_done"], START + 1)
                for h in range(GH):
                    m = pe.matmul(b64(5)[:, h, :], ML[:, l, h, :], U[:, h, :], start=True, stop=True)
                m.then_inc(s["Q_acc"], 1)
                pe.wait_ge(s["Q_out"], START + l)
                for h in range(GH):
                    m = pe.matmul(b64(2)[:, h, :], T[:, h, :], Qs[:, h, :], start=True, stop=True)
                    if l == 1:
                        m = pe.matmul(b64(3)[:, h, :], Qs[:, h, :], T[:, h, :], start=True, stop=True)
                m.then_inc(s["UT_acc"], 1)
            pe.wait_ge(s["rhsT_ready"], START + 1)
            for h in range(GH):
                m = pe.transpose(b128(7)[:, h, :], rhsT[:, h, :], p.ident)
            m.then_inc(s["rhs_turned"], 1)
            pe.wait_ge(s["rhs_ready"], START + 1)
            pe.wait_ge(s["Ub_ready"], START + 1)
            for h in range(GH):
                m = pe.matmul(b128(1)[:, h, :], Ub[:, h, :], rhs[:, h, :], start=True, stop=True)
            m.then_inc(s["vn_acc"], 1)
            pe.wait_ge(s["vn_ready"], START + 1)
            for h in range(GH):
                pe.matmul(c64(0)[:, h, :], Vn[:, h, :], QK[:, h, :], start=True, stop=False)
                for b in range(SEQS):
                    m = pe.matmul(c64(0)[:, h, STEPS * b:STEPS * b + STEPS], S[:, b, h, :], qE[:, h, STEPS * b:STEPS * b + STEPS],
                                  start=False, stop=(b == SEQS - 1))
            m.then_inc(s["oT_acc"], 1)
            pe.wait_ge(s["kd_ready"], START + SEQS)
            for b in range(SEQS):
                if b >= 2:
                    pe.wait_ge(s["s_ready"], START + b - 1)
                for h in range(GH):
                    m = pe.matmul(b128(2 + b % 2, P)[:, h, :], kd[:, b, h, :], Vn[:, h, :], start=True, stop=True)
                m.then_inc(s["ds_acc"], 1)
            pe.wait_ge(s["oT_ready"], START + 1)
            for h in range(GH):
                m = pe.transpose(b128(5)[:, h, :], oT[:, h, :], p.ident)
            m.then_inc(s["o_turned"], 1)

        @block.vector
        def _(dve):
            beta = p.beta[0:NS, 0, :]
            dve.tensor_copy(gB[:, :, :], p.g_s[0:NS, :].unsqueeze(2).broadcast_to([NS, GH, P])).then_inc(s["spread"], 1)
            dve.wait_ge(s["G_acc"], START + 1)
            dve.tensor_copy(Gc[:, :], ps[0:NS, 1, 0:GH]).then_inc(s["G_col"], 1)
            dve.wait_ge(s["G_col"], START + 1)
            dve.tensor_tensor(dif[:, :, :], c64(0)[0:NS], Gc[:, :].unsqueeze(2).broadcast_to(bc), ALU.subtract).then_inc(s["dif"], 1)
            dve.wait_ge(s["dif"], START + 1)
            dve.tensor_scalar(E1[:, :, :], dif[:, :, :], 0.0, None, ALU.max).then_inc(s["clamped"], 1)
            dve.tensor_scalar(E2[:, :, :], dif[:, :, :], 0.0, None, ALU.min).then_inc(s["clamped"], 1)
            dve.wait_ge(s["decays"], START + 3)
            dve.wait_ge(s["kk_acc"], START + 1)
            for h in range(GH):
                m = dve.scalar_tensor_tensor(out=A[:, h, :], in0=b64(2)[:, h, :], scalar=beta[:, h:h + 1], in1=E1[:, h, :], op0=ALU.mult, op1=ALU.mult)
            m.then_inc(s["A_ready"], 1)
            dve.wait_ge(s["E2_masked"], START + 1)
            dve.tensor_tensor(QK[:, :, :], b64(3), E2[:, :, :], ALU.mult).then_inc(s["QK_ready"], 1)
            dve.wait_ge(s["k_turned"], START + 1)
            for b in range(SEQS):
                c = STEPS * b + STEPS - 1
                dve.tensor_tensor(kd[:, b, :, :], b128(4), E2[:, :, c:c + 1].broadcast_to([NS, GH, P]), ALU.mult).then_inc(s["kd_ready"], 1)
            dve.wait_ge(s["m0_turned"], START + 1)
            eye = ident.unsqueeze(1).broadcast_to(bc)
            dve.tensor_tensor(T[:, :, :], eye, ML[:, 0, :, :], ALU.subtract)
            dve.tensor_tensor(U[:, :, :], eye, b64(5), ALU.subtract).then_inc(s["T_begun"], 1)
            dve.wait_ge(s["ks_acc"], START + 1)
            dve.tensor_tensor(rhsT[:, :, :], ld[:, 2 * GH:3 * GH, :], c64(6), ALU.subtract).then_inc(s["rhsT_ready"], 1)
            dve.wait_ge(s["UT_acc"], START + 1)
            dve.tensor_tensor(T[:, :, :], T[:, :, :], b64(3), ALU.subtract)
            dve.tensor_tensor(U[:, :, :], U[:, :, :], b64(2), ALU.subtract).then_inc(s["UT_done"], 1)
            dve.wait_ge(s["UT_acc"], START + 2)
            dve.wait_ge(s["UT_done"], START + 1)
            dve.tensor_tensor(U[:, :, :], U[:, :, :], b64(2), ALU.subtract).then_inc(s["UT_done"], 1)
            dve.wait_ge(s["UT_done"], START + 2)
            dve.tensor_tensor(Ub[:, :, :], U[:, :, :], beta.unsqueeze(2).broadcast_to(bc), ALU.mult).then_inc(s["Ub_ready"], 1)
            dve.wait_ge(s["oT_acc"], START + 1)
            for b in range(SEQS):
                c = STEPS * b + STEPS - 1
                dve.wait_ge(s["ds_acc"], START + b + 1)
                for h in range(GH):
                    m = dve.scalar_tensor_tensor(out=S[:, b, h, :], in0=S[:, b, h, :], scalar=EG[:, h, c:c + 1], in1=b128(2 + b % 2, P)[:, h, :], op0=ALU.mult, op1=ALU.add)
                m.then_inc(s["s_ready"], 1)

        @block.scalar
        def _(act):
            act.wait_ge(s["clamped"], START + 2)
            act.activation(E1[:, :, :], E1[:, :, :], ACT.Exp, scale=-1.0).then_inc(s["decays"], 1)
            act.activation(E2[:, :, :], E2[:, :, :], ACT.Exp).then_inc(s["decays"], 1)
            act.activation(EG[:, :, :], c64(0), ACT.Exp).then_inc(s["decays"], 1)
            for l in (1, 2):
                act.wait_ge(s["Q_acc"], START + l)
                act.activation(Qs[:, :, :], b64(5), ACT.Copy).then_inc(s["Q_out"], 1)
            act.wait_ge(s["rhs_turned"], START + 1)
            act.activation(rhs[:, :, :], b128(7), ACT.Copy).then_inc(s["rhs_ready"], 1)
            act.wait_ge(s["vn_acc"], START + 1)
            act.activation(Vn[:, :, :], b128(1), ACT.Copy).then_inc(s["vn_ready"], 1)
            act.wait_ge(s["oT_acc"], START + 1)
            act.activation(oT[:, :, :], c64(0), ACT.Copy).then_inc(s["oT_ready"], 1)
            act.wait_ge(s["o_turned"], START + 1)
            act.activation(ob[:, :, :], b128(5), ACT.Copy).then_inc(s["o_ready"], 1)

        @block.gpsimd
        def _(pool):
            pool.wait_ge(s["decays"], START + 3)
            pool.tensor_tensor(E2[:, :, :], E2[:, :, :], u8.unsqueeze(1).broadcast_to(bc), ALU.mult).then_inc(s["E2_masked"], 1)
            pool.wait_ge(s["loaded"], START + 32)
            pool.tensor_tensor(kE[:, :, :], ld[:, GH:2 * GH, :], EG[:, :, :], ALU.mult).then_inc(s["scaled"], 1)
            pool.tensor_tensor(qE[:, :, :], ld[:, 0:GH, :], EG[:, :, :], ALU.mult).then_inc(s["scaled"], 1)
            pool.wait_ge(s["A_ready"], START + 1)
            for l in range(3):
                mask = p.con[0:NS, C_LM + l * P:C_LM + l * P + NS].unsqueeze(1).broadcast_to(bc)
                pool.tensor_tensor(ML[:, l, :, :], A[:, :, :], mask, ALU.mult).then_inc(s["masked"], 1)


ROWS = SEQ // P
LAG = 3
RING = 4


def row_pieces(t):
    w = N_META + P * t
    n = -(-w // 1024)
    cut = [min(w, P * -(-(w * i // n) // P)) for i in range(n)] + [w]
    return [(a, b) for a, b in zip(cut, cut[1:])]


def prompt_attention(p):
    nc, ps = p.nc, p.ps
    W = TOK
    pieces = [row_pieces(r + 1) for r in range(ROWS)]
    first_piece = np.cumsum([0] + [len(x) for x in pieces]).tolist()
    groups = [-(-(r + 2) // 4) for r in range(ROWS)]
    first_group = np.cumsum([0] + groups).tolist()
    NPC, NG = first_piece[-1], first_group[-1]
    assert NPC % 2 == 0 and NG % 4 == 0 and ROWS % RING == 0
    v_loaded, qk_loaded = p.sem("pv_loaded"), p.sem("qk_loaded")
    z_acc, z_read, scanned, weighed = p.sem("z_acc"), p.sem("z_read"), p.sem("scanned"), p.sem("weighed")
    turned, evacuated, av_done = p.sem("A_turned"), p.sem("AT_evacuated"), p.sem("av_done")
    o_copied, o_stored, filled = p.sem("po_copied"), p.sem("po_stored"), p.sem("pa_filled")
    ready = p.sem("pa_bias_ready")
    with ExitStack() as st:
        def sb(name, *shape):
            return p.sb("f_" + name, list(shape), stack=st)

        v = sb("v", P, ROWS + 1, HALF + SD)
        q, k = sb("q", P, SEQ), sb("k", P, N_META + SEQ)
        keep = [sb(f"keep{i}", P, N_META + SEQ) for i in range(RING)]
        a = [sb(f"a{i}", P, W) for i in range(RING)]
        x = [sb(f"x{i}", P, N_META + SEQ + 1) for i in range(2)]
        at = [sb(f"at{i}", P, 512) for i in range(4)]
        ob, ones = sb("ob", P, ROWS, SD), sb("ones", P, N_META + SEQ)
        block = p.block(st)
        Z_BANK, T_BANK, O_BANK = 0, 4, 7
        L = N_META + SEQ

        SCAN_AT = 2
        AHEAD = 2

        def pair_columns(h):
            return ds(SD * h, P)

        def at_row(h, r):
            return (h, r) if r >= 0 else (h - 1, r + ROWS)

        def wait(eng, sem, n):
            if not isinstance(n, int) or n > 0:
                eng.wait_ge(sem, START + n)

        def over_heads(eng, step, flush):
            for r in range(ROWS):
                step(0, r)
            with eng.Fori(1, SH) as h:
                for r in range(ROWS):
                    step(h, r)
            for r in range(ROWS - LAG, ROWS):
                flush(SH - 1, r)

        @block.sync
        def _(sp):
            sp.wait_ge(filled, START + 1)
            sp.dma_start(v[M0:P, 0, 0:HALF], p.io["v_prompt"][0, 0, 0:N_META].rearrange("l h d -> l (h d)")).then_inc(v_loaded, 16)
            sp.dma_start(v[:, 1:, 0:HALF], p.io["v_prompt"][0, 0, N_META:].rearrange("(t p) h d -> p t (h d)", p=P)).then_inc(v_loaded, 16)

            def load(h, pair, half):
                wait(sp, z_acc, NPC * h)
                sp.dma_start(q[0:SD, :], p.chan[ds(pair + 12, 1), half * SD:half * SD + SD, P:TOK].rearrange("a p n -> (a p) n")).then_inc(qk_loaded, 16)
                sp.dma_start(k[0:SD, :], p.chan[ds(pair + 16, 1), half * SD:half * SD + SD, M0:TOK].rearrange("a p n -> (a p) n")).then_inc(qk_loaded, 16)

            def store(h):
                sp.wait_ge(o_copied, START + ROWS * (h + 1))
                sp.dma_start(p.o_rows[1:, :, ds(HALF + SD * h, SD)].rearrange("t p n -> p t n"), ob[:, :, :]).then_inc(o_stored, 16)

            load(0, 0, 0)
            load(1, 0, 1)
            store(0)
            with sp.Fori(1, PAIRS) as j:
                load(2 * j, j, 0)
                store(2 * j - 1)
                load(2 * j + 1, j, 1)
                store(2 * j)
            store(SH - 1)
            sp.wait_ge(o_stored, START + 16 * SH)

        @block.tensor
        def _(pe):
            def scores(h, r):
                if r == 0:
                    pe.wait_ge(qk_loaded, START + 32 * (h + 1))
                    pe.wait_ge(ready, START + h + 3)
                for i, (c0, c1) in enumerate(pieces[r]):
                    n = first_piece[r] + i
                    wait(pe, z_read, NPC * h + n - 1)
                    for lo in range(c0, c1, 512):
                        hi = min(lo + 512, c1)
                        bank = ps[:, Z_BANK + 2 * (n % 2) + (lo - c0) // 512, :]
                        last = hi == pieces[r][-1][1]
                        m = pe.matmul(bank[:, 0:hi - lo], q[:, r * P:(r + 1) * P], k[:, lo:hi], start=True, stop=not last)
                        if last:
                            cut = max(lo, c1 - P)
                            if cut > c1 - P:
                                pe.matmul(ps[:, Z_BANK + 2 * (n % 2), lo - c0 - (cut - c1 + P):512], p.ident, p.con[:, C_NM:C_NM + cut - c1 + P], start=False, stop=True, skip_group_check=True)
                            m = pe.matmul(bank[:, cut - lo:hi - lo], p.ident, p.con[:, C_NM + P - (c1 - cut):C_NM + P], start=False, stop=True)
                    m.then_inc(z_acc, 1)

            row_of = [r for r in range(ROWS) for _ in range(groups[r])]

            def turn(h, n):
                h, n = (h, n) if n < NG else (h + 1, n - NG)
                r = row_of[n]
                g = n - first_group[r]
                if g == 0:
                    pe.wait_ge(weighed, START + ROWS * h + r + 1)
                if n >= 3 or not isinstance(h, int) or h > 0:
                    hh, mm = (h, n - 3) if n >= 3 else (h - 1, max(m for m in range(NG) if m % 3 == n))
                    pe.wait_ge(evacuated, START + NG * hh + mm + 1)
                c = W - L + (L - N_META - P * (r + 1)) - M0
                for j in range(min(4, r + 2 - 4 * g)):
                    b = 4 * g + j
                    m = pe.transpose(ps[:, T_BANK + n % 3, j * P:(j + 1) * P], a[r % RING][:, c + b * P:c + (b + 1) * P], p.ident)
                m.then_inc(turned, 1)

            def values(h, r, g):
                n = first_group[r] + g
                pe.wait_ge(evacuated, START + NG * h + n + 1)
                if g == 0:
                    wait(pe, o_copied, ROWS * h + r - 1)
                for j in range(min(4, r + 2 - 4 * g)):
                    b = 4 * g + j
                    m = pe.matmul(ps[:, O_BANK, P * (r % 2):P * (r % 2) + P], at[n % 4][:, j * P:(j + 1) * P],
                                  v[:, b, pair_columns(h)], start=(b == 0), stop=(b == r + 1))
                m.then_inc(av_done, 1)

            def second(h, r):
                for g in range(groups[r]):
                    n = first_group[r] + g
                    if isinstance(h, int) and h == 0 and n == 0:
                        turn(h, 0)
                        turn(h, 1)
                    if n + AHEAD < NG or not (isinstance(h, int) and h == SH - 1):
                        turn(h, n + AHEAD)
                    values(h, r, g)

            def step(h, r):
                scores(h, r)
                if not isinstance(h, int) or r >= LAG:
                    second(*at_row(h, r - LAG))

            pe.wait_ge(v_loaded, START + 32)
            over_heads(pe, step, second)

        @block.scalar
        def _(act):
            def gates(h, r):
                off = L - pieces[r][-1][1]
                for i, (c0, c1) in enumerate(pieces[r]):
                    n = first_piece[r] + i
                    act.wait_ge(z_acc, START + NPC * h + n + 1)
                    if i == 0:
                        wait(act, scanned, ROWS * h + r - RING + 1)
                        hh, rr = at_row(h, r - RING)
                        if not isinstance(hh, int) or hh >= 0:
                            act.wait_ge(turned, START + NG * hh + first_group[rr + 1])
                    z = ps[:, Z_BANK + 2 * (n % 2):Z_BANK + 2 * (n % 2) + 2, :].rearrange("p a n -> p (a n)")[:, 0:c1 - c0]
                    act.activation(keep[r % RING][:, off + c0:off + c1], z, ACT.Sigmoid, scale=-SD ** -0.5)
                    act.activation(a[r % RING][:, M0 + off + c0:M0 + off + c1], z, ACT.Sigmoid, scale=SD ** -0.5).then_inc(z_read, 1)

            over_heads(act, gates, lambda h, r: None)

        @block.vector
        def _(dve):
            def scan(h, r):
                n = pieces[r][-1][1]
                dve.wait_ge(z_read, START + NPC * h + first_piece[r + 1])
                wait(dve, weighed, ROWS * h + r - 1)
                out, src = x[r % 2][:, L - n:L], keep[r % RING][:, L - n:L]
                dve.tensor_tensor_scan(out[:, ::-1], src[:, ::-1], src[:, ::-1], 1.0, ALU.mult, ALU.bypass).then_inc(scanned, 1)

            def second(h, r, late):
                for g in range(groups[r]):
                    if g == min(SCAN_AT, groups[r] - 1):
                        late()
                    n = first_group[r] + g
                    dve.wait_ge(turned, START + NG * h + n + 1)
                    wait(dve, av_done, NG * h + n - 3)
                    nb = min(4, r + 2 - 4 * g) * P
                    dve.tensor_copy(at[n % 4][:, 0:nb], ps[:, T_BANK + n % 3, 0:nb]).then_inc(evacuated, 1)
                dve.wait_ge(av_done, START + NG * h + first_group[r + 1])
                if r == 0:
                    wait(dve, o_stored, 16 * h)
                dve.tensor_copy(ob[:, r, :], ps[:, O_BANK, P * (r % 2):P * (r % 2) + SD]).then_inc(o_copied, 1)

            def bias_row(h):
                wait(dve, z_acc, NPC * h)
                dve.tensor_scalar(k[SD:SD + 1, :], ones[SD:SD + 1, :], p.small[SD:SD + 1, ds(h + 8, 1)], None, ALU.mult).then_inc(ready, 1)

            def step(h, r):
                def late():
                    if r or not isinstance(h, int):
                        scan(*at_row(h, r - 1))
                if r == 0:
                    bias_row(h)
                if not isinstance(h, int) or r >= LAG:
                    second(*at_row(h, r - LAG), late)
                else:
                    late()

            def flush(h, r):
                second(h, r, lambda: scan(h, ROWS - 1) if r == ROWS - LAG else None)

            dve.memset(v[:, 0, :], 0.0)
            dve.memset(v[:, 1:, HALF:HALF + SD], 0.0)
            dve.memset(q[SD:P, :], 0.0)
            dve.memset(k[SD:P, :], 0.0)
            dve.memset(ones[:, :], 1.0).then_inc(ready, 1)
            dve.wait_ge(ready, START + 1)
            dve.memset(q[SD:SD + 1, :], SD ** 0.5).then_inc(ready, 1)
            for i in range(2):
                dve.memset(x[i][:, L:L + 1], 1.0)
            for i in range(RING - 1):
                dve.memset(a[i][:, :], 0.0)
            dve.memset(a[RING - 1][:, :], 0.0).then_inc(filled, 1)
            over_heads(dve, step, flush)

        @block.gpsimd
        def _(pool):
            def step(h, r):
                n = pieces[r][-1][1]
                pool.wait_ge(scanned, START + ROWS * h + r + 1)
                w = a[r % RING][:, M0 + L - n:M0 + L]
                pool.tensor_tensor(w, w, x[r % 2][:, L - n + 1:L + 1], ALU.mult).then_inc(weighed, 1)

            over_heads(pool, step, lambda h, r: None)


def sample_attention(p):
    nc, ps = p.nc, p.ps
    GP = 4
    G = PAGES // GP
    PAST = PAGE * PAGES
    L = PAST + NS
    N_BANK, O_BANK, Z_BANK = 6, 7, 4
    once_act, zeroed, passed = p.sem("s_once_act"), p.sem("s_zeroed"), p.sem("s_passed")
    once, q_placed, mask_ready = p.sem("s_once"), p.sem("q_placed"), p.sem("mask_ready")
    table, k_loaded, v_loaded = p.sem("table"), [p.sem("k_even_loaded"), p.sem("k_odd_loaded")], [p.sem("v0_loaded"), p.sem("v1_loaded")]
    k_turned, kT_act, kT_dve = p.sem("s_k_turned"), p.sem("kT_by_scalar"), p.sem("kT_by_vector")
    z_acc, gated, hidden, scanned, weighed = p.sem("sz_acc"), p.sem("s_gated"), p.sem("s_hidden"), p.sem("s_scanned"), p.sem("s_weighed")
    a_turned, at_act, at_dve = p.sem("s_a_turned"), p.sem("s_at_scalar"), p.sem("s_at_vector")
    av_done, oT_placed, o_turned, o_out, stored = p.sem("s_av_done"), p.sem("oT_placed"), p.sem("so_turned"), p.sem("so_out"), p.sem("so_stored")
    with ExitStack() as st:
        def sb(name, *shape, dt=F32):
            return p.sb("j_" + name, list(shape), dt, stack=st)

        pages = sb("pages", 1, SEQS * PAGES, dt=I32)
        qs, ks, vs = sb("qs", P, PAIRS, NS), sb("ks", P, PAIRS, NS), sb("vs", NS, HALF)
        qb = [sb(f"qb{s}", P, PAIRS * 80) for s in range(2)]
        kp = [sb(f"kp{b}", P, GP, HALF) for b in range(2)]
        kT = sb("kT", P, PAIRS, HALF)
        v = sb("v", P, 2, PAGES, HALF)
        keep, a, x = sb("keep", P, L), sb("a", P, L), sb("x", P, L + 1)
        mask, unmask = sb("mask", P, NS), sb("unmask", P, NS)
        at = sb("at", P, PAGES + 1, P)
        oT, ob = sb("oT", P, PAIRS, NS), sb("ob", NS, HALF)
        bias = sb("bias", P, 2)
        block = p.block(st)

        @block.sync
        def _(sp):
            sp.dma_start(pages[:, :], p.io["page_table"].rearrange("b n -> (b n)").rearrange("(a n) -> a n", a=1)).then_inc(table, 16)
            sp.dma_start(qs[:, :, :], p.chan[12:16, :, 0:NS].rearrange("c p n -> p c n")).then_inc(once, 16)
            sp.dma_start(ks[:, :, :], p.chan[16:20, :, 0:NS].rearrange("c p n -> p c n")).then_inc(once, 16)
            sp.dma_start(vs[:, :], p.io["v_sample"][0].rearrange("b t h d -> (b t) (h d)")).then_inc(once, 16)
            for i in range(2 * SH):
                sp.dma_start(bias[STEPS * i:STEPS * i + STEPS, 0:1], p.io["sb_bias"][0, i % SH:i % SH + 1].partition_broadcast(STEPS)).then_inc(once, 16)
            sp.wait_ge(table, START + 16)
            with sp.Fori(0, SEQS // 2) as it:
                for g in range(G):
                    for s in range(2):
                        n = 2 * g + s
                        with sp.Fori(0, GP) as j:
                            page = sp.value_load(pages[0:1, ds(2 * PAGES * it + PAGES * s + GP * g + j, 1)], min_val=0, max_val=p.n_phys - 1)
                            sp.wait_ge(av_done, START + 2 * it)
                            sp.sem_inc(passed, 1)
                            sp.wait_ge(k_turned, START + 2 * G * it + max(n - 1, 0))
                            sp.sem_inc(passed, 1)
                            sp.dma_start(kp[n % 2][:, ds(j, 1), :], p.io["cache_k"][0, ds(page, 1)].rearrange("a t h d -> t a (h d)")).then_inc(k_loaded[n % 2], 16)
                            sp.dma_start(v[:, s, ds(GP * g + j, 1), :], p.io["cache_v"][0, ds(page, 1)].rearrange("a t h d -> t a (h d)")).then_inc(v_loaded[s], 16)
            sp.wait_ge(o_out, START + 1)
            sp.dma_start(p.o_rows[0][0:NS, HALF:D], ob[:, :]).then_inc(stored, 16)
            sp.wait_ge(stored, START + 16)

        @block.tensor
        def _(pe):
            with pe.Fori(0, SEQS // 2) as it:
                def evacuated(n):
                    pe.wait_ge(kT_act, START + 2 * n)
                    pe.wait_ge(kT_dve, START + 2 * n)

                for g in range(G):
                    for s in range(2):
                        n = 2 * g + s
                        pe.wait_ge(k_loaded[n % 2], START + 64 * G * it + 64 * g + 64)
                        if n == 0:
                            pe.wait_ge(at_act, START + 3 * it)
                            pe.wait_ge(at_dve, START + 2 * it)
                        evacuated(2 * G * it + n)
                        for c in range(PAIRS):
                            for j in range(GP):
                                m = pe.transpose(ps[:, c, j * PAGE:(j + 1) * PAGE], kp[n % 2][:, j, c * P:(c + 1) * P], p.ident)
                        m.then_inc(k_turned, 1)
                        if n == 0:
                            pe.wait_ge(q_placed, START + 2 * it + 2)
                        if s == 0:
                            pe.wait_ge(gated, START + 5 * it + max(g - 1, 0))
                        evacuated(2 * G * it + n + 1)
                        for c in range(PAIRS):
                            m = pe.matmul(ps[NS * s:NS * s + NS, Z_BANK + g % 2, :], qb[s][:, NS * c:NS * c + NS], kT[:, c, :],
                                          start=(c == 0), stop=(c == PAIRS - 1))
                        m.then_inc(z_acc, 1)
                pe.wait_ge(gated, START + 5 * it + G - 1)
                for s in range(2):
                    for c in range(PAIRS):
                        m = pe.matmul(ps[NS * s:NS * s + NS, Z_BANK, 0:NS], qb[s][:, NS * c:NS * c + NS], ks[:, c, :],
                                      start=(c == 0), stop=(c == PAIRS - 1))
                    m.then_inc(z_acc, 1)
                pe.wait_ge(weighed, START + it + 1)
                for c in range(4):
                    for j in range(4):
                        b = 4 * c + j
                        m = pe.transpose(ps[:, c, j * P:(j + 1) * P], a[:, b * P:(b + 1) * P], p.ident)
                    m.then_inc(a_turned, 1)
                pe.transpose(ps[0:NS, N_BANK, 0:P], a[:, PAST:L], p.ident).then_inc(a_turned, 1)
                pe.wait_ge(at_act, START + 3 * it + 3)
                pe.wait_ge(at_dve, START + 2 * it + 2)
                pe.wait_ge(oT_placed, START + 2 * it)
                for s in range(2):
                    pe.wait_ge(v_loaded[s], START + 16 * PAGES * (it + 1))
                    for c in range(PAIRS):
                        cols = slice(NS * s + 16 * c, NS * s + 16 * c + 16)
                        for b in range(PAGES):
                            pe.matmul(ps[:, O_BANK, cols], v[:, s, b, P * c:P * c + P], at[:, b, cols], start=(b == 0), stop=False)
                        m = pe.matmul(ps[:, O_BANK, cols], vs[:, P * c:P * c + P], at[0:NS, PAGES, cols], start=False, stop=True)
                    m.then_inc(av_done, 1)
            pe.wait_ge(oT_placed, START + SEQS)
            for c in range(PAIRS):
                m = pe.transpose(ps[0:NS, N_BANK, c * P:(c + 1) * P], oT[:, c, :], p.ident)
            m.then_inc(o_turned, 1)

        @block.scalar
        def _(act):
            act.wait_ge(once, START + 16 * (3 + 2 * SH))
            act.activation(bias[:, 1:2], bias[:, 0:1], ACT.Copy, scale=-1.0).then_inc(once_act, 1)
            act.wait_ge(once_act, START + 1)

            def gates(it, g, c0, w):
                act.wait_ge(z_acc, START + 10 * it + 2 * g + 2)
                if g == 0:
                    act.wait_ge(weighed, START + it)
                    act.wait_ge(a_turned, START + 5 * it)
                z = ps[:, Z_BANK + g % 2, 0:w]
                act.activation(keep[:, c0:c0 + w], z, ACT.Sigmoid, scale=-SD ** -0.5, bias=bias[:, 1:2])
                act.activation(a[:, c0:c0 + w], z, ACT.Sigmoid, scale=SD ** -0.5, bias=bias[:, 0:1]).then_inc(gated, 1)

            with act.Fori(0, SEQS // 2) as it:
                for g in range(G):
                    for s in range(2):
                        n = 2 * g + s
                        act.wait_ge(k_turned, START + 2 * G * it + n + 1)
                        if n:
                            act.wait_ge(z_acc, START + 10 * it + n)
                        else:
                            act.wait_ge(z_acc, START + 10 * it)
                        for c in (0, 1):
                            act.activation(kT[:, c, :], ps[:, c, :], ACT.Copy).then_inc(kT_act, 1)
                    gates(it, g, 512 * g, 512)
                gates(it, G, PAST, NS)
                for c in (0, 1):
                    act.wait_ge(a_turned, START + 5 * it + c + 1)
                    act.wait_ge(av_done, START + 2 * it)
                    act.activation(at[:, 4 * c:4 * c + 4, :].rearrange("p b n -> p (b n)"), ps[:, c, :], ACT.Copy).then_inc(at_act, 1)
                act.wait_ge(a_turned, START + 5 * it + 5)
                act.activation(at[0:NS, PAGES, :], ps[0:NS, N_BANK, 0:P], ACT.Copy).then_inc(at_act, 1)
            act.wait_ge(o_turned, START + 1)
            act.activation(ob[:, :], ps[0:NS, N_BANK, :], ACT.Copy).then_inc(o_out, 1)

        @block.vector
        def _(dve):
            for s in range(2):
                dve.memset(qb[s][:, :], 0.0).then_inc(zeroed, 1)
            dve.memset(x[:, L:L + 1], 1.0).then_inc(zeroed, 1)
            dve.wait_ge(zeroed, START + 3)
            dve.wait_ge(once, START + 16 * (3 + 2 * SH))
            with dve.Fori(0, SEQS // 2) as it:
                dve.wait_ge(z_acc, START + 10 * it)
                for s in range(2):
                    src = qs[:, :, ds(2 * STEPS * it + STEPS * s, STEPS)]
                    to = qb[s][:, :].rearrange("p (c n) -> p c n", n=80)
                    dve.tensor_copy(to[0:SD, :, 0:STEPS], src[0:SD])
                    dve.tensor_copy(to[SD:P, :, STEPS:2 * STEPS], src[SD:P]).then_inc(q_placed, 1)
                dve.tensor_copy(mask[:, :], p.con[:, ds(C_MB + 48 - 2 * STEPS * it, NS)]).then_inc(mask_ready, 1)
                dve.wait_ge(mask_ready, START + 2 * it + 1)
                dve.tensor_scalar(unmask[:, :], mask[:, :], -1.0, 1.0, ALU.mult, ALU.add).then_inc(mask_ready, 1)
                for n in range(2 * G):
                    dve.wait_ge(k_turned, START + 2 * G * it + n + 1)
                    dve.wait_ge(z_acc, START + 10 * it + n)
                    for c in (2, 3):
                        dve.tensor_copy(kT[:, c, :], ps[:, c, :]).then_inc(kT_dve, 1)
                dve.wait_ge(gated, START + 5 * it + 5)
                dve.wait_ge(mask_ready, START + 2 * it + 2)
                dve.tensor_tensor(keep[:, PAST:L], keep[:, PAST:L], unmask[:, :], ALU.max).then_inc(hidden, 1)
                dve.tensor_tensor(a[:, PAST:L], a[:, PAST:L], mask[:, :], ALU.mult).then_inc(hidden, 1)
                dve.wait_ge(hidden, START + 2 * it + 2)
                dve.wait_ge(weighed, START + it)
                dve.tensor_tensor_scan(x[:, 0:L][:, ::-1], keep[:, ::-1], keep[:, ::-1], 1.0, ALU.mult, ALU.bypass).then_inc(scanned, 1)
                dve.wait_ge(scanned, START + it + 1)
                dve.tensor_tensor(a[:, :], a[:, :], x[:, 1:L + 1], ALU.mult).then_inc(weighed, 1)
                for c in (2, 3):
                    dve.wait_ge(a_turned, START + 5 * it + c + 1)
                    dve.wait_ge(av_done, START + 2 * it)
                    dve.tensor_copy(at[:, 4 * c:4 * c + 4, :].rearrange("p b n -> p (b n)"), ps[:, c, :]).then_inc(at_dve, 1)
                for s in range(2):
                    dve.wait_ge(av_done, START + 2 * it + 2)
                    src = ps[:, O_BANK, NS * s:NS * s + NS].rearrange("p (c n) -> p c n", n=16)
                    to = oT[:, :, ds(2 * STEPS * it + STEPS * s, STEPS)]
                    dve.tensor_copy(to[0:SD], src[0:SD, :, 0:STEPS])
                    dve.tensor_copy(to[SD:P], src[SD:P, :, STEPS:2 * STEPS]).then_inc(oT_placed, 1)


def merge(p):
    nc, io, ps = p.nc, p.io, p.ps
    loaded, g_once = [p.sem("m_even_loaded"), p.sem("m_odd_loaded")], p.sem("m_rows_loaded")
    names = ("once", "zeroed", "squares", "mean_sq", "rms", "gated", "mixed", "turned", "mT_ready", "y_acc", "summed",
             "stats", "var", "rstd", "normed", "gained", "biased", "junked")
    s = {n: p.sem("m_" + n) for n in names}
    stored = [p.sem("y_even_stored"), p.sem("y_odd_stored")]
    with ExitStack() as st:
        def sb(name, *shape):
            return p.sb("m_" + name, list(shape), stack=st)

        w = sb("w", P, KC, D)
        gn, lng, lnb = sb("gn", P, DK), sb("lng", P, D), sb("lnb", P, D)
        o, gt, hh, mix, yb = ([sb(f"{n}{b}", P, D) for b in range(2)] for n in ("o", "gt", "hh", "mix", "yb"))
        mT = [sb(f"mT{b}", P, KC, P) for b in range(2)]
        junk, ss, rs = sb("junk", P, GH, DK), sb("ss", P, 4), sb("rs", P, 4)
        st6, mv = sb("st6", P, 2, 6), sb("mv", P, 4)
        block = p.block(st)

        def after(eng, sem, n):
            if not isinstance(n, int) or n > 0:
                eng.wait_ge(sem, START + n)

        @block.sync
        def _(sp):
            def load(t, b):
                if not isinstance(t, int) or t >= 2:
                    sp.wait_ge(s["mixed"], START + t - 1)
                    sp.wait_ge(s["summed"], START + t - 1)
                for dst, src in ((o[b], p.o_rows), (gt[b], p.gates), (hh[b], p.h_rows)):
                    sp.dma_start(dst[:, :], src[ds(t, 1)].rearrange("a p d -> (a p) d")).then_inc(loaded[b], 16)

            def store(t, b):
                sp.wait_ge(s["biased"], START + t + 1)
                sp.dma_start(io["y_prompt"][0, ds((t - 1) * P, P), :], yb[b][:, :]).then_inc(stored[b], 16)

            sp.wait_ge(s["zeroed"], START + 1)
            for dst, src in ((o[0], p.o_rows), (gt[0], p.gates), (hh[0], p.h_rows)):
                n = NS if dst is o[0] else P
                sp.dma_start(dst[0:n, :], src[0][0:n, :]).then_inc(loaded[0], 16)
            sp.dma_start(gn[:, :], row(io["gdn_norm_g"][0])).then_inc(g_once, 16)
            sp.dma_start(lng[:, :], row(io["ln_out_g"][0])).then_inc(g_once, 16)
            sp.dma_start(lnb[:, :], row(io["ln_out_b"][0])).then_inc(g_once, 16)
            sp.dma_start(w[:, :, :], io["w_out"][0].rearrange("(c p) n -> p c n", p=P)).then_inc(s["once"], 16)
            load(1, 1)
            sp.wait_ge(s["biased"], START + 1)
            sp.dma_start(io["y_sample"].rearrange("b t d -> (b t) d"), yb[0][0:NS, :]).then_inc(stored[0], 16)
            with sp.Fori(0, (NT - 1) // 2 - 1) as i:
                load(2 * i + 2, 0)
                store(2 * i + 1, 1)
                load(2 * i + 3, 1)
                store(2 * i + 2, 0)
            load(NT - 1, 0)
            store(NT - 2, 1)
            store(NT - 1, 0)
            sp.wait_ge(stored[0], START + 16 * (NT // 2 + 1))
            sp.wait_ge(stored[1], START + 16 * (NT // 2))

        @block.tensor
        def _(pe):
            def turn(t, b):
                pe.wait_ge(s["mixed"], START + t + 1)
                after(pe, s["mT_ready"], t)
                for c in range(KC):
                    m = pe.transpose(ps[:, c // 4, (c % 4) * P:(c % 4 + 1) * P], mix[b][:, c * P:(c + 1) * P], p.ident)
                m.then_inc(s["turned"], 1)

            def products(t, b):
                pe.wait_ge(s["mT_ready"], START + t + 1)
                if not isinstance(t, int) or t >= 2:
                    pe.wait_ge(s["summed"], START + t)
                for f in range(2):
                    for c in range(KC):
                        m = pe.matmul(ps[:, 2 + 2 * b + f, :], mT[b][:, c, :], w[:, c, 512 * f:512 * f + 512], start=(c == 0), stop=(c == KC - 1))
                m.then_inc(s["y_acc"], 1)

            turn(0, 0)
            pe.wait_ge(s["once"], START + 16)
            with pe.Fori(0, (NT - 1) // 2) as i:
                turn(2 * i + 1, 1)
                products(2 * i, 0)
                turn(2 * i + 2, 0)
                products(2 * i + 1, 1)
            products(NT - 1, 0)

        def pipelined(eng, first, second):
            first(0, 0, 48)
            with eng.Fori(0, (NT - 1) // 2) as i:
                first(2 * i + 1, 1, 48 * i + 48)
                second(2 * i, 0, 16 * i)
                first(2 * i + 2, 0, 48 * i + 96)
                second(2 * i + 1, 1, 16 * i)
            second(NT - 1, 0, 16 * (NT // 2))

        @block.scalar
        def _(act):
            def first(t, b, ld):
                act.wait_ge(loaded[b], START + ld)
                after(act, s["rms"], t)
                for h in range(GH):
                    m = act.activation(junk[:, h, :], o[b][:, h * DK:(h + 1) * DK], ACT.Square, accum_out=ss[:, h:h + 1])
                m.then_inc(s["squares"], 1)
                act.wait_ge(s["turned"], START + t + 1)
                if not isinstance(t, int) or t >= 2:
                    act.wait_ge(s["y_acc"], START + t - 1)
                for f in range(2):
                    m = act.activation(mT[b][:, 4 * f:4 * f + 4, :].rearrange("p c n -> p (c n)"), ps[:, f, :], ACT.Copy)
                m.then_inc(s["mT_ready"], 1)

            pipelined(act, first, lambda t, b, n: None)

        @block.vector
        def _(dve):
            def first(t, b, ld):
                dve.wait_ge(s["squares"], START + t + 1)
                dve.tensor_scalar(rs[:, :], ss[:, :], 1.0 / DK, RMS_EPS, ALU.mult, ALU.add).then_inc(s["mean_sq"], 1)
                dve.wait_ge(s["rms"], START + t + 1)
                dve.wait_ge(s["gated"], START + t + 1)
                if not isinstance(t, int) or t >= 2:
                    dve.wait_ge(s["turned"], START + t - 1)
                for h in range(GH):
                    c = slice(h * DK, (h + 1) * DK)
                    dve.scalar_tensor_tensor(out=mix[b][:, c], in0=o[b][:, c], scalar=rs[:, h:h + 1], in1=gt[b][:, c], op0=ALU.mult, op1=ALU.mult)
                dve.tensor_tensor(mix[b][:, HALF:D], o[b][:, HALF:D], gt[b][:, HALF:D], ALU.mult).then_inc(s["mixed"], 1)

            def second(t, b, before):
                dve.wait_ge(s["y_acc"], START + t + 1)
                if not isinstance(t, int) or t >= 2:
                    dve.wait_ge(stored[b], START + before)
                for f in range(2):
                    c = slice(512 * f, 512 * f + 512)
                    dve.scalar_tensor_tensor(out=yb[b][:, c], in0=hh[b][:, c], scalar=ALPHA, in1=ps[:, 2 + 2 * b + f, :], op0=ALU.mult, op1=ALU.add).then_inc(s["junked"], 1)
                dve.wait_ge(s["junked"], START + 2 * t + 2)
                dve.tensor_copy(mv[:, 3:4], yb[b][:, 0:1]).then_inc(s["summed"], 1)
                dve.bn_stats(st6[:, 0, :], yb[b][:, 0:512]).then_inc(s["stats"], 1)
                dve.bn_stats(st6[:, 1, :], yb[b][:, 512:1024]).then_inc(s["stats"], 1)
                dve.wait_ge(s["stats"], START + 3 * t + 2)
                dve.tensor_copy(mv[:, 2:3], st6[:, 1, 0:1])
                dve.bn_aggr(mv[:, 0:2], st6[:, :, :].rearrange("p a b -> p (a b)")).then_inc(s["stats"], 1)
                dve.wait_ge(s["stats"], START + 3 * t + 3)
                dve.tensor_scalar(mv[:, 2:3], mv[:, 1:2], LN_EPS, None, ALU.add).then_inc(s["var"], 1)
                dve.wait_ge(s["rstd"], START + t + 1)
                dve.tensor_scalar(yb[b][:, :], yb[b][:, :], mv[:, 0:1], mv[:, 3:4], ALU.subtract, ALU.mult).then_inc(s["normed"], 1)

            pipelined(dve, first, second)

        @block.gpsimd
        def _(pool):
            pool.memset(o[0][NS:P, :], 0.0).then_inc(s["zeroed"], 1)
            pool.wait_ge(g_once, START + 48)

            def first(t, b, ld):
                pool.wait_ge(s["mean_sq"], START + t + 1)
                pool.tensor_tensor(rs[:, :], rs[:, :], p.con[:, C_MH:C_MH + 1].broadcast_to([P, 4]), ALU.pow).then_inc(s["rms"], 1)
                pool.wait_ge(loaded[b], START + ld)
                v = gt[b][:, 0:HALF].rearrange("p (h n) -> p h n", h=GH)
                pool.tensor_tensor(v, v, gn[:, :].unsqueeze(1).broadcast_to([P, GH, DK]), ALU.mult).then_inc(s["gated"], 1)

            def second(t, b, before):
                pool.wait_ge(s["var"], START + t + 1)
                pool.tensor_tensor(mv[:, 3:4], mv[:, 2:3], p.con[:, C_MH:C_MH + 1], ALU.pow).then_inc(s["rstd"], 1)
                pool.wait_ge(s["normed"], START + t + 1)
                pool.tensor_tensor(yb[b][:, :], yb[b][:, :], lng[:, :], ALU.mult).then_inc(s["gained"], 1)
                pool.wait_ge(s["gained"], START + t + 1)
                pool.tensor_tensor(yb[b][:, :], yb[b][:, :], lnb[:, :], ALU.add).then_inc(s["biased"], 1)

            pipelined(pool, first, second)



def build(nc, io, debug=False, stages=99):
    with ExitStack() as stack:
        p = Program(nc, io, stack, debug)
        p.run(setup)
        with ExitStack() as st:
            hT = p.sb("hT", [P, KC, TOK], stack=st)
            p.run(token_major, hT)
            if stages >= 2:
                p.run(channel_major, hT)
            if stages >= 3:
                p.run(attention_heads, hT)
        later = [(4, delta_gates), (4, conv_states), (4, delta_net), (4, sample_delta),
                 (5, prompt_attention), (6, sample_attention), (7, merge)]
        for n, stage in later:
            if stages >= n:
                p.run(stage)


_INS = ["x_prompt", "x_sample", "cache_k", "cache_v", "page_table", "state_gdn", "state_conv", "meta_tokens",
        "ln_in_g", "ln_in_b", "w_in", "conv_w", "a_log", "dt_bias", "gdn_norm_g", "sb_bias", "w_out", "ln_out_g", "ln_out_b"]
_OUTS = [("y_prompt", (1, SEQ, D)), ("y_sample", (SEQS, STEPS, D)),
         ("k_prompt", (1, 1, N_META + SEQ, SH, SD)), ("v_prompt", (1, 1, N_META + SEQ, SH, SD)),
         ("k_sample", (1, SEQS, STEPS, SH, SD)), ("v_sample", (1, SEQS, STEPS, SH, SD)),
         ("gdn_prompt", (1, 1, GH, DK, DK)), ("gdn_sample", (1, SEQS, GH, DK, DK)),
         ("conv_prompt", (1, 1, CONV - 1, 3 * HALF)), ("conv_sample", (1, SEQS, CONV - 1, 3 * HALF))]


def kernel(**inputs):
    import numpy as _np
    import concourse.bacc as _bacc
    from concourse import mybir as _mybir
    from concourse.bass_utils import run_bass_kernel_spmd as _run

    nc = _bacc.Bacc("TRN2", target_bir_lowering=False, num_devices=1)
    arrays, io = {}, {}
    for name in _INS:
        arrays[name] = _np.ascontiguousarray(inputs[name])
    arrays["consts"] = shape_constants()
    for name, a in arrays.items():
        io[name] = nc.dram_tensor(name, a.shape, _mybir.dt.from_np(a.dtype), kind="ExternalInput").ap()
    for name, shape in _OUTS:
        io[name] = nc.dram_tensor(name, shape, F32, kind="ExternalOutput").ap()
    build(nc, io)
    r = _run(nc, [arrays], core_ids=[0])
    return tuple(r.results[0][name] for name, _ in _OUTS)
```

```python
from contextlib import ExitStack

import numpy as np

import concourse.bass as bass
from concourse import mybir

F32 = mybir.dt.float32
I32 = mybir.dt.int32
ALU = mybir.AluOpType
ACT = mybir.ActivationFunctionType
ds = bass.ds

P = 128
D = 1024
KC = D // P
SEQ, N_META = 2048, 16
SEQS, STEPS = 8, 8
NS = SEQS * STEPS
NT = 1 + SEQ // P
TOK = NT * P
M0 = P - N_META
GH, DK = 4, 128
SH, SD = 8, 64
PAIRS = SH // 2
HALF = 512
CONV = 4
CB = 12
PAGE, PAGES = 128, 16
COL_ZG, COL_AB, COL_Q, COL_K, COL_V, COL_ZS = 1536, 2048, 2056, 2568, 3080, 3592
ALPHA = 2.0 ** 0.25
LN_EPS, RMS_EPS, L2_EPS = 1e-5, 1e-6, 1e-6
CHUNKS = [(0, 512), (512, 512), (1024, 512), (1536, 512), (2048, 128)]
START = 1
LEVELS = 7

C_ID, C_UT, C_ONE, C_LM, C_U8, C_MB = 0, P, 2 * P, 3 * P, (3 + LEVELS) * P, (3 + LEVELS) * P + NS
C_MH = C_MB + 112
C_NM = C_MH + 1
C_W = C_NM + P


def shape_constants():
    i, j = np.arange(P)[:, None], np.arange(P)[None, :]
    parts = [i == j, i <= j, np.ones((P, P))]
    for l in range(LEVELS):
        s = 1 << l
        parts.append((i // (2 * s) == j // (2 * s)) & (i // s % 2 == 1) & (j // s % 2 == 0))
    parts.append(((i // STEPS == j // STEPS) & (i <= j))[:, :NS])
    c = np.arange(112)[None, :] - 48
    parts.append((c // STEPS == i // NS) & (c >= 0) & (c % STEPS < i % STEPS))
    parts.append(np.full((P, 1), -0.5))
    parts.append(np.where(j >= i, -1e30, 0.0))
    return np.concatenate([np.asarray(p, np.float32) for p in parts], axis=1)


class Program:

    def __init__(self, nc, io, stack, debug):
        self.nc, self.io, self.stack = nc, io, stack
        kind = "ExternalOutput" if debug else "Internal"

        def scratch(name, shape):
            return nc.dram_tensor(name, shape, F32, kind=kind).ap()

        self.h_rows = scratch("h_rows", (NT, P, D))
        self.gates = scratch("gates", (NT, P, D))
        self.chan = scratch("chan", (20, P, TOK))
        self.o_rows = scratch("o_rows", (NT, P, D))
        self.ps = stack.enter_context(nc.psum_tensor("ps", [P, 8, 512], F32))
        self.con = self.sb("con", [P, C_W])
        self.ab = self.sb("ab", [P, NT, 8])
        self.lnT = self.sb("lnT", [P, 16])
        self.rows28 = self.sb("rows28", [28, CB, P])
        self.sc = self.sb("sc", [P, CB, 28])
        self.tails = self.sb("tails", [P, CB, 27])
        self.small = self.sb("small", [P, 64])
        self.g = self.sb("g", [P, NT, GH])
        self.g_s = self.sb("g_s", [P, GH])
        self.beta = self.sb("beta", [P, NT, GH])
        self.ident = self.con[:, C_ID:C_ID + P]
        self.utri = self.con[:, C_UT:C_UT + P]
        self.ones = self.con[:, C_ONE:C_ONE + P]

    def sb(self, name, shape, dt=F32, stack=None):
        return (stack or self.stack).enter_context(self.nc.sbuf_tensor(name, shape, dt))

    def sem(self, name):
        self.stage_sems.append(self.nc.alloc_semaphore(name=name))
        return self.stage_sems[-1]

    def block(self, stack):
        for s in self.stage_sems:
            self.nc.gpsimd.sem_inc(s, START)
        self.nc.all_engine_barrier()
        return stack.enter_context(self.nc.Block())

    def run(self, stage, *args):
        self.stage_sems = []
        stage(self, *args)
        self.nc.clear_and_free_semaphores(self.stage_sems)


def row(ap, n=P):
    return ap.partition_broadcast(n)


def setup(p):
    nc, io = p.nc, p.io
    loaded, turned, copied = p.sem("su_loaded"), p.sem("su_turned"), p.sem("su_copied")
    with ExitStack() as st:
        ln16 = p.sb("ln16", [16, P], stack=st)
        block = p.block(st)

        @block.sync
        def _(sp):
            sp.dma_start(p.con[:, :], io["consts"]).then_inc(loaded, 16)
            sp.dma_start(p.rows28[0:24, :, :], io["state_conv"][0].rearrange("b i (c p) -> (b i) c p", p=P)).then_inc(loaded, 16)
            sp.dma_start(p.rows28[24:28, :, :], io["conv_w"][0].rearrange("i (c p) -> i c p", p=P)).then_inc(loaded, 16)
            sp.dma_start(ln16[0:8, :], io["ln_in_g"].rearrange("(c p) -> c p", p=P)).then_inc(loaded, 16)
            sp.dma_start(ln16[8:16, :], io["ln_in_b"].rearrange("(c p) -> c p", p=P)).then_inc(loaded, 16)
            sp.dma_start(p.small[:, 0:4], row(io["a_log"][0])).then_inc(loaded, 16)
            sp.dma_start(p.small[:, 4:8], row(io["dt_bias"][0])).then_inc(loaded, 16)
            sp.dma_start(p.small[:, 8:16], row(io["sb_bias"][0])).then_inc(loaded, 16)

        @block.tensor
        def _(pe):
            pe.wait_ge(loaded, START + 16 * 8)
            for c in range(CB):
                pe.transpose(p.ps[:, 0, 28 * c:28 * c + 28], p.rows28[:, c, :], p.con[0:28, 0:28])
            pe.transpose(p.ps[:, 1, 0:16], ln16[:, :], p.con[0:16, 0:16]).then_inc(turned, 1)

        @block.vector
        def _(dve):
            dve.wait_ge(turned, START + 1)
            dve.tensor_copy(p.sc[:, :, :].rearrange("p c i -> p (c i)"), p.ps[:, 0, 0:28 * CB]).then_inc(copied, 1)
            dve.tensor_copy(p.lnT[:, :], p.ps[:, 1, 0:16]).then_inc(copied, 1)
            dve.tensor_scalar(p.small[:, 16:24], p.small[:, 8:16], -1.0, None, ALU.mult).then_inc(copied, 1)
            dve.wait_ge(copied, START + 3)


def token_major(p, hT):
    nc, io, ps = p.nc, p.io, p.ps
    x_loaded = [p.sem("x_even_loaded"), p.sem("x_odd_loaded")]
    w_loaded, g_loaded = [p.sem(n + "_weights_loaded") for n in ("v", "zg", "zs", "ab")], p.sem("g_loaded")
    padded = p.sem("padded")
    stats, centred, rooted, normed = p.sem("stats"), p.sem("centred"), p.sem("rooted"), p.sem("normed")
    turned, evacuated = p.sem("x_turned"), p.sem("xT_evacuated")
    v_acc, zg_acc, zs_acc, ab_acc = p.sem("v_acc"), p.sem("zg_acc"), p.sem("zs_acc"), p.sem("ab_acc")
    v_out, zg_out, zs_out, ab_out = p.sem("v_out"), p.sem("zg_out"), p.sem("zs_out"), p.sem("ab_out")
    scaled, shifted, kept = p.sem("h_scaled"), p.sem("h_shifted"), p.sem("hT_kept")
    h_stored = p.sem("h_stored")
    v_stored = [p.sem("v_even_stored"), p.sem("v_odd_stored")]
    g_stored = [p.sem("g_even_stored"), p.sem("g_odd_stored")]
    w = io["w_in"][0].rearrange("(c p) n -> p c n", p=P)
    v_p = io["v_prompt"][0, 0].rearrange("l h d -> l (h d)")
    v_s = io["v_sample"][0].rearrange("b t h d -> (b t) (h d)")
    with ExitStack() as st:
        wt = p.sb("wt", [P, KC, 1536], stack=st)
        wab = p.sb("wab", [P, KC, 8], stack=st)
        xin = p.sb("xin", [P, 2, D], stack=st)
        xh = p.sb("xh", [P, 2, D], stack=st)
        hg = p.sb("hg", [P, D], stack=st)
        gain = p.sb("gain", [P, 2, D], stack=st)
        cur = [p.sb(f"hT_now{i}", [P, KC, P], stack=st) for i in range(2)]
        vb = p.sb("vb", [P, 2, 512], stack=st)
        gb = p.sb("gb", [P, 2, D], stack=st)
        st6 = p.sb("st6", [P, 2, 6], stack=st)
        mv = p.sb("mv", [P, 4], stack=st)
        block = p.block(st)

        @block.sync
        def _(sp):
            def load(t, b):
                if not isinstance(t, int) or t >= 2:
                    sp.wait_ge(normed, START + t - 1)
                sp.dma_start(xin[:, b, :], io["x_prompt"][0, ds((t - 1) * P, P), :]).then_inc(x_loaded[b], 16)

            def store(t, b):
                sp.wait_ge(shifted, START + t + 1)
                sp.dma_start(p.h_rows[ds(t, 1)].rearrange("a p d -> (a p) d"), hg[:, :]).then_inc(h_stored, 16)
                sp.wait_ge(v_out, START + t + 1)
                sp.dma_start(v_p[ds(t * P - M0, P), :], vb[:, b, :]).then_inc(v_stored[b], 16)
                sp.wait_ge(zs_out, START + t + 1)
                sp.dma_start(p.gates[ds(t, 1)].rearrange("a p d -> (a p) d"), gb[:, b, :]).then_inc(g_stored[b], 16)

            sp.dma_start(xin[0:NS, 0, :], io["x_sample"].rearrange("b t d -> (b t) d")).then_inc(x_loaded[0], 16)
            sp.dma_start(xin[M0:P, 0, :], io["meta_tokens"]).then_inc(x_loaded[0], 16)
            sp.dma_start(gain[:, 0, :], row(io["ln_in_g"])).then_inc(g_loaded, 16)
            sp.dma_start(gain[:, 1, :], row(io["ln_in_b"])).then_inc(g_loaded, 16)
            load(1, 1)
            for i, col in enumerate((COL_V, COL_ZG, COL_ZS)):
                sp.dma_start(wt[:, :, 512 * i:512 * i + 512], w[:, :, col:col + 512]).then_inc(w_loaded[i], 16)
            sp.dma_start(wab[:, :, :], w[:, :, COL_AB:COL_AB + 8]).then_inc(w_loaded[3], 16)
            load(2, 0)
            sp.wait_ge(shifted, START + 1)
            sp.dma_start(p.h_rows[0], hg[:, :]).then_inc(h_stored, 16)
            sp.wait_ge(v_out, START + 1)
            sp.dma_start(v_s, vb[0:NS, 0, :]).then_inc(v_stored[0], 16)
            sp.dma_start(v_p[0:N_META, :], vb[M0:P, 0, :]).then_inc(v_stored[0], 16)
            sp.wait_ge(zs_out, START + 1)
            sp.dma_start(p.gates[0], gb[:, 0, :]).then_inc(g_stored[0], 16)
            with sp.Fori(0, (NT - 1) // 2 - 1) as i:
                load(2 * i + 3, 1)
                store(2 * i + 1, 1)
                load(2 * i + 4, 0)
                store(2 * i + 2, 0)
            store(NT - 2, 1)
            store(NT - 1, 0)
            sp.wait_ge(h_stored, START + 16 * NT)
            sp.wait_ge(v_stored[0], START + 16 * (NT // 2 + 2))
            sp.wait_ge(v_stored[1], START + 16 * (NT // 2))
            sp.wait_ge(g_stored[0], START + 16 * (NT // 2 + 1))
            sp.wait_ge(g_stored[1], START + 16 * (NT // 2))

        @block.gpsimd
        def _(pool):
            pool.memset(xin[NS:M0, 0, :], 0.0).then_inc(padded, 1)
            pool.wait_ge(padded, START + 1)
            pool.memset(cur[0][:, :, NS:M0], 0.0).then_inc(padded, 1)

            def rows(t, b):
                pool.wait_ge(centred, START + t + 1)
                pool.tensor_tensor(mv[:, 3:4], mv[:, 2:3], p.con[:, C_MH:C_MH + 1], ALU.pow).then_inc(rooted, 1)
                pool.wait_ge(normed, START + t + 1)
                pool.wait_ge(h_stored, START + 16 * t)
                pool.tensor_tensor(hg[:, :], xh[:, b, :], gain[:, 0, :], ALU.mult).then_inc(scaled, 1)
                pool.wait_ge(scaled, START + t + 1)
                pool.tensor_tensor(hg[:, :], hg[:, :], gain[:, 1, :], ALU.add).then_inc(shifted, 1)
                pool.wait_ge(evacuated, START + t + 1)
                pool.tensor_copy(hT[:, :, ds(t * P, P)], cur[b][:, :, :]).then_inc(kept, 1)

            pool.wait_ge(g_loaded, START + 32)
            rows(0, 0)
            with pool.Fori(0, (NT - 1) // 2) as i:
                rows(2 * i + 1, 1)
                rows(2 * i + 2, 0)

        @block.vector
        def _(dve):
            def norm(t, b, loaded):
                dve.wait_ge(x_loaded[b], START + loaded)
                if not (isinstance(t, int) and t == 0):
                    dve.wait_ge(normed, START + t)
                dve.bn_stats(st6[:, 0, :], xin[:, b, 0:512]).then_inc(stats, 1)
                dve.bn_stats(st6[:, 1, :], xin[:, b, 512:1024]).then_inc(stats, 1)
                dve.wait_ge(stats, START + 3 * t + 2)
                dve.tensor_copy(mv[:, 2:3], st6[:, 1, 0:1])
                dve.bn_aggr(mv[:, 0:2], st6[:, :, :].rearrange("p a b -> p (a b)")).then_inc(stats, 1)
                dve.wait_ge(stats, START + 3 * t + 3)
                dve.tensor_scalar(mv[:, 2:3], mv[:, 1:2], LN_EPS, None, ALU.add).then_inc(centred, 1)
                dve.wait_ge(rooted, START + t + 1)
                if not (isinstance(t, int) and t < 2):
                    dve.wait_ge(shifted, START + t - 1)
                    dve.wait_ge(turned, START + t - 1)
                dve.tensor_scalar(xh[:, b, :], xin[:, b, :], mv[:, 0:1], mv[:, 3:4], ALU.subtract, ALU.mult).then_inc(normed, 1)

            def logits(t):
                dve.wait_ge(ab_acc, START + t + 1)
                dve.tensor_copy(p.ab[:, ds(t, 1), :].rearrange("p a b -> p (a b)"), ps[:, 5, 0:8]).then_inc(ab_out, 1)

            dve.wait_ge(padded, START + 1)
            norm(0, 0, 32)
            norm(1, 1, 16)
            with dve.Fori(0, (NT - 3) // 2) as i:
                norm(2 * i + 2, 0, 16 * i + 48)
                logits(2 * i)
                norm(2 * i + 3, 1, 16 * i + 32)
                logits(2 * i + 1)
            norm(NT - 1, 0, 8 * (NT - 3) + 48)
            for t in range(NT - 3, NT):
                logits(t)
            dve.wait_ge(ab_out, START + NT)

        @block.tensor
        def _(pe):
            def turn(t, b):
                pe.wait_ge(normed, START + t + 1)
                pe.wait_ge(evacuated, START + t)
                for c in range(KC):
                    m = pe.transpose(ps[:, c // 4, (c % 4) * P:(c % 4 + 1) * P], xh[:, b, c * P:(c + 1) * P], p.ident)
                m.then_inc(turned, 1)

            def products(t, b):
                pe.wait_ge(evacuated, START + t + 1)
                for g, (done, acc) in enumerate(((v_out, v_acc), (zg_out, zg_acc), (zs_out, zs_acc))):
                    if isinstance(t, int) and t == 0:
                        pe.wait_ge(w_loaded[g], START + 16)
                    else:
                        pe.wait_ge(done, START + t)
                    for c in range(KC):
                        m = pe.matmul(ps[:, 2 + g, :], cur[b][:, c, :], wt[:, c, 512 * g:512 * g + 512],
                                      start=(c == 0), stop=(c == KC - 1))
                    m.then_inc(acc, 1)
                if isinstance(t, int) and t == 0:
                    pe.wait_ge(w_loaded[3], START + 16)
                else:
                    pe.wait_ge(ab_out, START + t)
                for c in range(KC):
                    m = pe.matmul(ps[:, 5, 0:8], cur[b][:, c, :], wab[:, c, :], start=(c == 0), stop=(c == KC - 1))
                m.then_inc(ab_acc, 1)

            turn(0, 0)
            turn(1, 1)
            products(0, 0)
            with pe.Fori(0, (NT - 1) // 2 - 1) as i:
                turn(2 * i + 2, 0)
                products(2 * i + 1, 1)
                turn(2 * i + 3, 1)
                products(2 * i + 2, 0)
            turn(NT - 1, 0)
            products(NT - 2, 1)
            products(NT - 1, 0)

        @block.scalar
        def _(act):
            def evacuate(t, b):
                act.wait_ge(turned, START + t + 1)
                first = isinstance(t, int) and t == 0
                if first:
                    act.wait_ge(padded, START + 2)
                else:
                    if not (isinstance(t, int) and t < 2):
                        act.wait_ge(ab_acc, START + t - 1)
                        act.wait_ge(kept, START + t - 1)
                for c in range(KC):
                    for lo, hi in ((0, NS), (M0, P)) if first else ((0, P),):
                        a = act.activation(cur[b][:, c, lo:hi], ps[:, c // 4, (c % 4) * P + lo:(c % 4) * P + hi],
                                           ACT.Identity, scale=p.lnT[:, c:c + 1], bias=p.lnT[:, 8 + c:9 + c])
                a.then_inc(evacuated, 1)

            def outputs(t, b, v_before, g_before):
                act.wait_ge(v_acc, START + t + 1)
                if not (isinstance(t, int) and t < 2):
                    act.wait_ge(v_stored[b], START + v_before)
                    act.wait_ge(g_stored[b], START + g_before)
                act.activation(vb[:, b, :], ps[:, 2, :], ACT.Copy).then_inc(v_out, 1)
                act.wait_ge(zg_acc, START + t + 1)
                act.activation(gb[:, b, 0:512], ps[:, 3, :], ACT.Silu).then_inc(zg_out, 1)
                act.wait_ge(zs_acc, START + t + 1)
                act.activation(gb[:, b, 512:1024], ps[:, 4, :], ACT.Silu).then_inc(zs_out, 1)

            evacuate(0, 0)
            evacuate(1, 1)
            outputs(0, 0, 0, 0)
            with act.Fori(0, (NT - 1) // 2 - 1) as i:
                evacuate(2 * i + 2, 0)
                outputs(2 * i + 1, 1, 16 * i, 16 * i)
                evacuate(2 * i + 3, 1)
                outputs(2 * i + 2, 0, 16 * i + 32, 16 * i + 16)
            n = (NT - 1) // 2 - 1
            evacuate(NT - 1, 0)
            outputs(NT - 2, 1, 16 * n, 16 * n)
            outputs(NT - 1, 0, 16 * n + 32, 16 * n + 16)


def channel_major(p, hT):
    nc, io, ps = p.nc, p.io, p.ps
    w = io["w_in"][0].rearrange("(c p) n -> p c n", p=P)
    w_in, acc, evac = [p.sem(f"cw{k}_loaded") for k in range(3)], p.sem("c_acc"), p.sem("c_evacuated")
    smp, conv, silu = p.sem("smp_ready"), p.sem("conv_step"), p.sem("c_silu")
    tailed, squared, summed = p.sem("tailed"), p.sem("squared"), p.sem("summed")
    rooted, inverted, scaled, stored = p.sem("c_rooted"), p.sem("inverted"), p.sem("c_scaled"), p.sem("c_stored")
    zeroed, epsd = p.sem("c_zeroed"), p.sem("epsd")
    v_stored = p.sem("cv_stored")
    with ExitStack() as st:
        wc = [p.sb(f"wc{k}", [P, KC, P], stack=st) for k in range(3)]
        pre = [p.sb(f"pre{k}", [P, TOK], stack=st) for k in range(3)]
        y = [p.sb(f"y{k}", [P, TOK], stack=st) for k in range(3)]
        sq = p.sb("sq", [P, TOK], stack=st)
        nrm = p.sb("nrm", [P, TOK], stack=st)
        xs = p.sb("xs", [P, SEQS, 11], stack=st)
        eps = p.sb("eps", [P, 2], stack=st)
        block = p.block(st)
        COLS = (0, 512, 1024)

        @block.sync
        def _(sp):
            def load(h, k):
                sp.dma_start(wc[k][:, :, :], w[:, :, ds(h * P + COLS[k], P)]).then_inc(w_in[k], 16)

            def store(h, k):
                done = stored
                if k < 2:
                    sp.wait_ge(scaled, START + 2 * h + k + 1)
                else:
                    sp.wait_ge(silu, START + 3 * h + 3)
                    done = v_stored
                sp.dma_start(p.chan[ds(h + 4 * k, 1)].rearrange("a p n -> (a p) n"), y[k][:, :]).then_inc(done, 16)

            for k in range(3):
                load(0, k)
            with sp.Fori(0, GH - 1) as h:
                for k in range(3):
                    sp.wait_ge(acc, START + 15 * h + 5 * (k + 1))
                    load(h + 1, k)
                for k in range(3):
                    store(h, k)
            for k in range(3):
                store(GH - 1, k)
            sp.wait_ge(stored, START + 16 * 8)
            sp.wait_ge(v_stored, START + 16 * 4)

        @block.tensor
        def _(pe):
            def products(h, k):
                pe.wait_ge(w_in[k], START + 16 * h + 16)
                for ci, (c0, n) in enumerate(CHUNKS):
                    if k:
                        pe.wait_ge(evac, START + 15 * h + 5 * (k - 1) + ci + 1)
                    else:
                        pe.wait_ge(evac, START + 15 * h)
                    for c in range(KC):
                        m = pe.matmul(ps[:, ci, 0:n], wc[k][:, c, :], hT[:, c, c0:c0 + n], start=(c == 0), stop=(c == KC - 1))
                    m.then_inc(acc, 1)

            def sums(h, k):
                pe.wait_ge(squared, START + 2 * h + k + 1)
                for ci, (c0, n) in enumerate(CHUNKS):
                    pe.wait_ge(rooted, START + 10 * h + 5 * k + max(ci - 2, 0))
                    pe.matmul(ps[:, 5 + ci % 3, 0:n], p.ones, sq[:, c0:c0 + n], start=True, stop=True).then_inc(summed, 1)

            with pe.Fori(0, GH) as h:
                products(h, 0)
                products(h, 1)
                sums(h, 0)
                products(h, 2)
                sums(h, 1)

        @block.scalar
        def _(act):
            def evacuate(h, k, between=None):
                for ci, (c0, n) in enumerate(CHUNKS):
                    if ci == 3 and between:
                        between()
                    act.wait_ge(acc, START + 15 * h + 5 * k + ci + 1)
                    if ci == 0:
                        act.wait_ge(tailed, START + 3 * h + k)
                    act.activation(pre[k][:, c0:c0 + n], ps[:, ci, 0:n], ACT.Copy).then_inc(evac, 1)

            def swish(h, k):
                act.wait_ge(conv, START + 8 * (3 * h + k + 1))
                act.activation(y[k][:, 0:NS], y[k][:, 0:NS], ACT.Silu)
                act.activation(y[k][:, M0:TOK], y[k][:, M0:TOK], ACT.Silu).then_inc(silu, 1)

            def root(h, k):
                for ci, (c0, n) in enumerate(CHUNKS):
                    act.wait_ge(summed, START + 10 * h + 5 * k + ci + 1)
                    if ci == 0:
                        act.wait_ge(scaled, START + 2 * h + k)
                    act.activation(nrm[:, c0:c0 + n], ps[:, 5 + ci % 3, 0:n], ACT.Sqrt,
                                   scale=float(DK) if k == 0 else 1.0, bias=eps[:, k:k + 1]).then_inc(rooted, 1)

            act.wait_ge(epsd, START + 2)
            with act.Fori(0, GH) as h:
                evacuate(h, 0)
                evacuate(h, 1, lambda: swish(h, 0))
                root(h, 0)
                evacuate(h, 2, lambda: swish(h, 1))
                root(h, 1)
                swish(h, 2)

        @block.vector
        def _(dve):
            for k in range(3):
                dve.memset(y[k][:, NS:M0], 0.0).then_inc(zeroed, 1)
            dve.memset(eps[:, 0:1], L2_EPS * DK).then_inc(epsd, 1)
            dve.memset(eps[:, 1:2], L2_EPS).then_inc(epsd, 1)
            dve.wait_ge(zeroed, START + 3)

            def convolve(h, k):
                n = 3 * h + k
                wt = [p.sc[:, ds(h + 4 * k, 1), 24 + i:25 + i].rearrange("p a b -> p (a b)") for i in range(CONV)]
                dve.wait_ge(evac, START + 5 * (n + 1))
                if k < 2:
                    dve.wait_ge(stored, START + 32 * h)
                else:
                    dve.wait_ge(v_stored, START + 16 * h)
                dve.wait_ge(tailed, START + n)
                dve.tensor_copy(xs[:, :, 0:3], p.sc[:, ds(h + 4 * k, 1), 0:24].rearrange("p a (b i) -> p (a b) i", i=3)).then_inc(smp, 1)
                dve.tensor_copy(xs[:, :, 3:11], pre[k][:, 0:NS].rearrange("p (b t) -> p b t", t=STEPS)).then_inc(smp, 1)
                dve.wait_ge(smp, START + 2 * (n + 1))
                ys = y[k][:, 0:NS].rearrange("p (b t) -> p b t", t=STEPS)
                for i in range(CONV):
                    src, srcs = pre[k][:, M0 - 3 + i:TOK - 3 + i], xs[:, :, i:i + STEPS]
                    if i == 0:
                        dve.tensor_scalar(y[k][:, M0:TOK], src, wt[i], None, ALU.mult).then_inc(conv, 1)
                        dve.tensor_scalar(ys, srcs, wt[i], None, ALU.mult).then_inc(conv, 1)
                    else:
                        dve.wait_ge(conv, START + 8 * n + 2 * i)
                        dve.scalar_tensor_tensor(out=y[k][:, M0:TOK], in0=src, scalar=wt[i], in1=y[k][:, M0:TOK], op0=ALU.mult, op1=ALU.add).then_inc(conv, 1)
                        dve.scalar_tensor_tensor(out=ys, in0=srcs, scalar=wt[i], in1=ys, op0=ALU.mult, op1=ALU.add).then_inc(conv, 1)
                dve.tensor_copy(p.tails[:, ds(h + 4 * k, 1), 0:24].rearrange("p a (b i) -> p (a b) i", i=3), xs[:, :, STEPS:STEPS + 3])
                dve.tensor_copy(p.tails[:, ds(h + 4 * k, 1), 24:27].rearrange("p a b -> p (a b)"), pre[k][:, TOK - 3:TOK]).then_inc(tailed, 1)

            def scale(h, k):
                dve.wait_ge(rooted, START + 10 * h + 5 * (k + 1))
                dve.reciprocal(nrm[:, :], nrm[:, :]).then_inc(inverted, 1)
                dve.wait_ge(inverted, START + 2 * h + k + 1)
                dve.tensor_tensor(y[k][:, :], y[k][:, :], nrm[:, :], ALU.mult).then_inc(scaled, 1)

            with dve.Fori(0, GH) as h:
                convolve(h, 0)
                convolve(h, 1)
                scale(h, 0)
                convolve(h, 2)
                scale(h, 1)

        @block.gpsimd
        def _(pool):
            pool.wait_ge(zeroed, START + 3)

            def square(h, k):
                pool.wait_ge(silu, START + 3 * h + k + 1)
                if k:
                    pool.wait_ge(summed, START + 10 * h + 5)
                else:
                    pool.wait_ge(summed, START + 10 * h)
                pool.tensor_tensor(sq[:, :], y[k][:, :], y[k][:, :], ALU.mult).then_inc(squared, 1)

            with pool.Fori(0, GH) as h:
                square(h, 0)
                square(h, 1)


def attention_heads(p, hT):
    nc, io, ps = p.nc, p.io, p.ps
    w = io["w_in"][0].rearrange("(c p) n -> p c n", p=P)
    w_in, acc, evac, stored = [p.sem(f"aw{k}_loaded") for k in range(2)], p.sem("a_acc"), p.sem("a_evac"), p.sem("a_stored")
    turned, out, k_stored = p.sem("k_turned"), p.sem("k_out"), p.sem("k_stored")
    k_p = io["k_prompt"][0, 0].rearrange("l h d -> l (h d)")
    k_s = io["k_sample"][0].rearrange("b t h d -> (b t) (h d)")
    groups = [(g, min(4, NT - 4 * g)) for g in range(5)]
    with ExitStack() as st:
        wc = [p.sb(f"wa{k}", [P, KC, P], stack=st) for k in range(2)]
        y = [p.sb(f"ya{k}", [P, TOK], stack=st) for k in range(2)]
        kr = p.sb("kr", [P, NT, P], stack=st)
        block = p.block(st)

        @block.sync
        def _(sp):
            def load(h, k):
                sp.dma_start(wc[k][:, :, :], w[:, :, ds(h * P + (COL_Q, COL_K)[k], P)]).then_inc(w_in[k], 16)

            def store(h):
                sp.wait_ge(evac, START + 10 * h + 10)
                sp.dma_start(p.chan[ds(h + 12, 1)].rearrange("a p n -> (a p) n"), y[0][:, :]).then_inc(stored, 16)
                sp.dma_start(p.chan[ds(h + 16, 1)].rearrange("a p n -> (a p) n"), y[1][:, :]).then_inc(stored, 16)
                sp.wait_ge(out, START + 5 * h + 5)
                cols = ds(h * P, P)
                sp.dma_start(k_p[N_META:, cols].rearrange("(t p) n -> p t n", p=P), kr[:, 1:, :]).then_inc(k_stored, 16)
                sp.dma_start(k_p[0:N_META, cols], kr[M0:P, 0, :]).then_inc(k_stored, 16)
                sp.dma_start(k_s[:, cols], kr[0:NS, 0, :]).then_inc(k_stored, 16)

            for k in range(2):
                load(0, k)
            with sp.Fori(0, PAIRS - 1) as h:
                for k in range(2):
                    sp.wait_ge(acc, START + 10 * h + 5 * (k + 1))
                    load(h + 1, k)
                store(h)
            store(PAIRS - 1)
            sp.wait_ge(stored, START + 16 * 8)
            sp.wait_ge(k_stored, START + 48 * 4)

        @block.tensor
        def _(pe):
            with pe.Fori(0, PAIRS) as h:
                for k in range(2):
                    pe.wait_ge(w_in[k], START + 16 * h + 16)
                    for ci, (c0, n) in enumerate(CHUNKS):
                        pe.wait_ge(evac, START + (10 * h + (ci + 1 if k else 0)))
                        for c in range(KC):
                            m = pe.matmul(ps[:, ci, 0:n], wc[k][:, c, :], hT[:, c, c0:c0 + n], start=(c == 0), stop=(c == KC - 1))
                        m.then_inc(acc, 1)
                pe.wait_ge(evac, START + 10 * h + 10)
                for g, n in groups:
                    pe.wait_ge(out, START + 5 * h + max(g - 2, 0))
                    for j in range(n):
                        m = pe.transpose(ps[:, 5 + g % 3, j * P:(j + 1) * P], y[1][:, (4 * g + j) * P:(4 * g + j + 1) * P], p.ident)
                    m.then_inc(turned, 1)

        @block.scalar
        def _(act):
            with act.Fori(0, PAIRS) as h:
                for k in range(2):
                    for ci, (c0, n) in enumerate(CHUNKS):
                        act.wait_ge(acc, START + 10 * h + 5 * k + ci + 1)
                        if ci == 0:
                            act.wait_ge(stored, START + 32 * h)
                            act.wait_ge(turned, START + 5 * h)
                        act.activation(y[k][:, c0:c0 + n], ps[:, ci, 0:n], ACT.Copy).then_inc(evac, 1)

        @block.vector
        def _(dve):
            with dve.Fori(0, PAIRS) as h:
                for g, n in groups:
                    dve.wait_ge(turned, START + 5 * h + g + 1)
                    if g == 0:
                        dve.wait_ge(k_stored, START + 48 * h)
                    dve.tensor_copy(kr[:, 4 * g:4 * g + n, :].rearrange("p a b -> p (a b)"), ps[:, 5 + g % 3, 0:n * P]).then_inc(out, 1)


def delta_gates(p):
    nc = p.nc
    d, a = p.sem("dg_vector"), p.sem("dg_scalar")
    shape = [P, NT, GH]
    with ExitStack() as st:
        x, ax, e, sp, eb = [p.sb(n, shape, stack=st) for n in ("g_x", "g_ax", "g_e", "g_sp", "g_eb")]
        ea = p.sb("g_ea", [P, GH], stack=st)
        one = p.sb("g_one", [P, 1], stack=st)
        before = p.sb("g_before", [P, 1], stack=st)
        block = p.block(st)

        @block.vector
        def _(dve):
            dve.memset(one[:, :], 1.0).then_inc(d, 1)
            dve.tensor_tensor(x[:, :, :], p.ab[:, :, 0:4], p.small[:, 4:8].unsqueeze(1).broadcast_to(shape), ALU.add).then_inc(d, 1)
            dve.tensor_scalar(before[:, :], p.utri[:, M0 - 1:M0], -1.0, 1.0, ALU.mult, ALU.add).then_inc(d, 1)
            dve.wait_ge(d, START + 3)
            dve.tensor_scalar(ax[:, :, :], x[:, :, :], -1.0, None, ALU.mult).then_inc(d, 1)
            dve.wait_ge(d, START + 4)
            dve.tensor_tensor(ax[:, :, :], ax[:, :, :], x[:, :, :], ALU.max).then_inc(d, 1)
            dve.wait_ge(a, START + 4)
            dve.scalar_tensor_tensor(out=sp[:, :, :], in0=x[:, :, :], scalar=0.0, in1=sp[:, :, :], op0=ALU.max, op1=ALU.add).then_inc(d, 1)
            dve.tensor_scalar(eb[:, :, :], eb[:, :, :], 1.0, None, ALU.add).then_inc(d, 1)
            dve.wait_ge(d, START + 7)
            dve.scalar_tensor_tensor(out=p.g[:, :, :], in0=sp[:, :, :], scalar=-1.0, in1=ea[:, :].unsqueeze(1).broadcast_to(shape), op0=ALU.mult, op1=ALU.mult).then_inc(d, 1)
            dve.reciprocal(p.beta[:, :, :], eb[:, :, :]).then_inc(d, 1)
            dve.wait_ge(d, START + 9)
            dve.tensor_copy(p.g_s[:, :], p.g[:, 0, :]).then_inc(d, 1)
            dve.wait_ge(d, START + 10)
            dve.tensor_scalar(p.g[:, 0, :], p.g[:, 0, :], before[:, 0:1], None, ALU.mult).then_inc(d, 1)
            dve.wait_ge(d, START + 11)

        @block.scalar
        def _(act):
            act.wait_ge(d, START + 5)
            act.activation(e[:, :, :], ax[:, :, :], ACT.Exp, scale=-1.0).then_inc(a, 1)
            act.activation(ea[:, :], p.small[:, 0:4], ACT.Exp).then_inc(a, 1)
            act.activation(eb[:, :, :], p.ab[:, :, 4:8], ACT.Exp, scale=-1.0).then_inc(a, 1)
            act.wait_ge(a, START + 3)
            act.activation(sp[:, :, :], e[:, :, :], ACT.Ln, bias=one[:, 0:1]).then_inc(a, 1)


def delta_net(p):
    nc, ps = p.nc, p.ps
    loaded = [p.sem("d_even_loaded"), p.sem("d_odd_loaded")]
    names = ("g_spread", "g_now", "G_acc", "kk_acc", "qk_acc", "G_col", "G_diff", "G_clamped", "decays", "edges",
             "E2_masked", "A_ready", "qk_ready", "kv_turned", "kd_ready", "v_ready", "levels_masked", "scaled_by_G",
             "m0_turned", "T_begun", "U_begun", "Ub_ready", "ks_acc", "rhs_ready", "vn_acc", "vn_ready", "o_acc", "o_ready",
             "ds_acc", "state", "o_stored", "zeroed_d", "s_stored")
    s = {n: p.sem("d_" + n) for n in names}
    q_acc, q_out, ut_acc, ut_done = p.sem("Q_acc"), p.sem("Q_out"), p.sem("UT_acc"), p.sem("UT_done")
    LV = 2 * (LEVELS - 1)
    G_BANK, K_BANK, Q_BANK, KS_BANK, VN_BANK, O_BANK = range(6)

    def heads(bank, h=None, n=P):
        v = ps[:, bank, :].rearrange("p (h n) -> p h n", h=GH)
        return v if h is None else v[:, h, :]

    with ExitStack() as st:
        def sb(name, shape=(P, GH, P)):
            return p.sb(name, list(shape), stack=st)

        ld = [sb(f"d_ld{b}", (P, 12, P)) for b in range(2)]
        kE, qE, QK, kd, vt, Ub = ([sb(f"d_{n}{b}") for b in range(2)] for n in ("kE", "qE", "QK", "kd", "vt", "Ub"))
        last = [sb(f"d_last{b}", (P, GH)) for b in range(2)]
        gB, dif, E1, E2, EG, A = (sb("d_" + n) for n in ("gB", "dif", "E1", "E2", "EG", "A"))
        ML = [sb(f"d_ML{b}", (P, LEVELS, GH, P)) for b in range(2)]
        UT = [sb(f"d_UT{g}", (P, 2, 2, P)) for g in range(2)]
        Qs = [sb(f"d_Qs{g}", (P, 2, P)) for g in range(2)]
        gc, Gc, beta = sb("d_gc", (P, GH)), sb("d_Gc", (P, GH)), [sb(f"d_beta{b}", (P, GH)) for b in range(2)]
        rhs, Vn, ob, S = sb("d_rhs"), sb("d_Vn"), sb("d_ob"), sb("d_S")
        bc = [P, GH, P]
        chan = p.chan[0:12].rearrange("c p n -> p c n")
        block = p.block(st)

        def after(eng, what, value):
            if not isinstance(value, int) or value > 0:
                eng.wait_ge(s[what], START + value)

        def over_tiles(front, turn, state):
            def run(eng):
                front(0, 0, 16)
                turn(0, 0, (1, 1, 16), None)
                with eng.Fori(0, (NT - 3) // 2) as i:
                    turn(2 * i + 1, 1, (2 * i + 2, 0, 16 * i + 32), (2 * i, 0))
                    turn(2 * i + 2, 0, (2 * i + 3, 1, 16 * i + 32), (2 * i + 1, 1))
                turn(NT - 2, 1, (NT - 1, 0, 8 * (NT + 1)), (NT - 3, 0))
                turn(NT - 1, 0, None, (NT - 2, 1))
                state(NT - 1, 0)
            return run

        @block.sync
        def _(sp):
            sp.wait_ge(s["zeroed_d"], START + 2)
            sp.dma_start(ld[0][:, :, M0:P], chan[:, :, M0:P]).then_inc(loaded[0], 16)
            sp.dma_start(ld[1][:, :, :], chan[:, :, P:2 * P]).then_inc(loaded[1], 16)

            def load(t, b):
                sp.wait_ge(s["kv_turned"], START + t - 1)
                sp.wait_ge(s["scaled_by_G"], START + t - 1)
                sp.dma_start(ld[b][:, :, :], chan[:, :, ds(t * P, P)]).then_inc(loaded[b], 16)

            def store(t):
                sp.wait_ge(s["o_ready"], START + t + 1)
                sp.dma_start(p.o_rows[ds(t, 1)].rearrange("a p n -> (a p) n")[:, 0:HALF],
                             ob[:, :, :].rearrange("p h n -> p (h n)")).then_inc(s["o_stored"], 16)

            with sp.Fori(0, (NT - 1) // 2 - 1) as i:
                load(2 * i + 2, 0)
                store(2 * i)
                load(2 * i + 3, 1)
                store(2 * i + 1)
            load(NT - 1, 0)
            for t in (NT - 3, NT - 2, NT - 1):
                store(t)
            sp.wait_ge(s["state"], START + NT + 1)
            sp.dma_start(p.io["gdn_prompt"][0, 0].rearrange("h k v -> k h v"), S[:, :, :]).then_inc(s["s_stored"], 16)
            sp.wait_ge(s["o_stored"], START + 16 * NT)
            sp.wait_ge(s["s_stored"], START + 16)

        @block.tensor
        def _(pe):
            def begin_g(t, b, ld_count):
                pe.wait_ge(s["g_spread"], START + t + 1)
                after(pe, "edges", t)
                after(pe, "v_ready", t)
                for h in range(GH):
                    pe.matmul(heads(G_BANK, h), gB[:, h, :], p.utri, start=True, stop=True)
                pe.matmul(ps[:, Q_BANK, 0:GH], p.utri, gc[:, :], start=True, stop=True).then_inc(s["G_acc"], 1)

            def begin_kk(t, b, ld_count):
                pe.wait_ge(loaded[b], START + ld_count)
                after(pe, "kd_ready", t)
                for h in range(GH):
                    m = pe.matmul(heads(K_BANK, h), ld[b][:, GH + h, :], ld[b][:, GH + h, :], start=True, stop=True)
                m.then_inc(s["kk_acc"], 1)

            def begin_qk(t, b, ld_count):
                pe.wait_ge(s["G_col"], START + t + 1)
                for h in range(GH):
                    m = pe.matmul(heads(Q_BANK, h), ld[b][:, GH + h, :], ld[b][:, h, :], start=True, stop=True)
                m.then_inc(s["qk_acc"], 1)

            def turn_kv(t, b, ld_count=None):
                pe.wait_ge(s["A_ready"], START + t + 1)
                pe.wait_ge(s["qk_ready"], START + t + 1)
                for h in range(GH):
                    pe.transpose(heads(K_BANK, h), ld[b][:, GH + h, :], p.ident)
                    m = pe.transpose(heads(Q_BANK, h), ld[b][:, 2 * GH + h, :], p.ident)
                m.then_inc(s["kv_turned"], 1)

            def turn_m0(t, b, ld_count=None):
                pe.wait_ge(s["levels_masked"], START + LEVELS * t + 1)
                after(pe, "vn_ready", t - 1)
                for h in range(GH):
                    m = pe.transpose(heads(VN_BANK, h), ML[b][:, 0, h, :], p.ident)
                m.then_inc(s["m0_turned"], 1)

            def level_q(t, b, l):
                pe.wait_ge(s["levels_masked"], START + LEVELS * t + l + 1)
                for g in range(2):
                    if l == 1:
                        if not isinstance(t, int) or t:
                            pe.wait_ge(ut_done, START + LV * t)
                        pe.wait_ge(s["U_begun"], START + 2 * t + g + 1)
                    if l > 1:
                        pe.wait_ge(ut_done, START + LV * t + 2 * (l - 2) + g + 1)
                    for h in range(2):
                        m = pe.matmul(ps[:, 6 + g, h * P:(h + 1) * P], ML[b][:, l, 2 * g + h, :], UT[g][:, 1, h, :], start=True, stop=True)
                    m.then_inc(q_acc, 1)

            def level_ut(t, l):
                if l == 1:
                    pe.wait_ge(s["T_begun"], START + t + 1)
                for g in range(2):
                    pe.wait_ge(q_out, START + LV * t + 2 * (l - 1) + g + 1)
                    for h in range(2):
                        m = pe.matmul(ps[:, 6 + g, (2 + h) * P:(3 + h) * P], UT[g][:, 0, h, :], Qs[g][:, h, :], start=True, stop=True)
                    if l < LEVELS - 1:
                        for h in range(2):
                            m = pe.matmul(ps[:, 6 + g, h * P:(h + 1) * P], Qs[g][:, h, :], UT[g][:, 0, h, :], start=True, stop=True)
                    m.then_inc(ut_acc, 1)

            def state_ks(t, b):
                pe.wait_ge(s["state"], START + t + 1)
                pe.wait_ge(s["scaled_by_G"], START + t + 1)
                for h in range(GH):
                    m = pe.matmul(heads(KS_BANK, h), kE[b][:, h, :], S[:, h, :], start=True, stop=True)
                m.then_inc(s["ks_acc"], 1)

            def state_vn(t, b):
                pe.wait_ge(s["rhs_ready"], START + t + 1)
                pe.wait_ge(s["Ub_ready"], START + t + 1)
                for h in range(GH):
                    m = pe.matmul(heads(VN_BANK, h), Ub[b][:, h, :], rhs[:, h, :], start=True, stop=True)
                m.then_inc(s["vn_acc"], 1)

            def state_update(t, b):
                pe.wait_ge(s["vn_ready"], START + t + 1)
                for h in range(GH):
                    m = pe.matmul(heads(KS_BANK, h), kd[b][:, h, :], Vn[:, h, :], start=True, stop=True)
                m.then_inc(s["ds_acc"], 1)

            def outputs(t, b):
                after(pe, "o_ready", t)
                for h in range(GH):
                    pe.matmul(heads(O_BANK, h), qE[b][:, h, :], S[:, h, :], start=True, stop=False)
                    m = pe.matmul(heads(O_BANK, h), QK[b][:, h, :], Vn[:, h, :], start=False, stop=True)
                m.then_inc(s["o_acc"], 1)

            def front(t, b, ld_count):
                for part in (begin_g, begin_kk, begin_qk, turn_kv, turn_m0):
                    part(t, b, ld_count)

            def tile(t, b, ahead, state):
                if state:
                    state_ks(*state)
                for l in range(1, LEVELS):
                    level_q(t, b, l)
                    if ahead and l <= 3:
                        (begin_g, begin_kk, begin_qk)[l - 1](*ahead)
                    if ahead and l == 5:
                        turn_kv(*ahead)
                    if ahead and l == LEVELS - 1:
                        turn_m0(*ahead)
                    level_ut(t, l)
                    if state and l in (2, 3):
                        (state_vn, state_update_and_outputs)[l - 2](*state)

            def state_update_and_outputs(t, b):
                pe.wait_ge(s["vn_ready"], START + t + 1)
                outputs(t, b)
                state_update(t, b)

            def state(t, b):
                state_ks(t, b)
                state_vn(t, b)
                state_update_and_outputs(t, b)

            over_tiles(front, tile, state)(pe)

        @block.vector
        def _(dve):
            def spread(t, b):
                after(dve, "Ub_ready", t - 1)
                after(dve, "G_acc", t)
                dve.tensor_copy(gc[:, :], p.g[:, ds(t, 1), :].rearrange("p a h -> p (a h)")).then_inc(s["g_now"], 1)
                dve.tensor_copy(beta[b][:, :], p.beta[:, ds(t, 1), :].rearrange("p a h -> p (a h)")).then_inc(s["g_now"], 1)
                dve.wait_ge(s["g_now"], START + 2 * t + 2)
                dve.tensor_copy(gB[:, :, :], gc[:, :].unsqueeze(2).broadcast_to(bc)).then_inc(s["g_spread"], 1)

            def decays(t):
                dve.wait_ge(s["G_acc"], START + t + 1)
                dve.tensor_copy(Gc[:, :], ps[:, Q_BANK, 0:GH]).then_inc(s["G_col"], 1)
                dve.wait_ge(s["G_col"], START + t + 1)
                dve.tensor_tensor(dif[:, :, :], heads(G_BANK), Gc[:, :].unsqueeze(2).broadcast_to(bc), ALU.subtract).then_inc(s["G_diff"], 1)
                dve.wait_ge(s["G_diff"], START + t + 1)
                after(dve, "A_ready", t)
                dve.tensor_scalar(E1[:, :, :], dif[:, :, :], 0.0, None, ALU.max).then_inc(s["G_clamped"], 1)
                after(dve, "kd_ready", t)
                dve.tensor_scalar(E2[:, :, :], dif[:, :, :], 0.0, None, ALU.min).then_inc(s["G_clamped"], 1)

            def blocks(t, b):
                after(dve, "levels_masked", LEVELS * t)
                dve.wait_ge(s["decays"], START + t + 1)
                dve.wait_ge(s["kk_acc"], START + t + 1)
                for h in range(GH):
                    m = dve.scalar_tensor_tensor(out=A[:, h, :], in0=heads(K_BANK, h), scalar=beta[b][:, h:h + 1], in1=E1[:, h, :], op0=ALU.mult, op1=ALU.mult)
                m.then_inc(s["A_ready"], 1)

            def decayed_qk(t, b):
                after(dve, "o_acc", t - 1)
                dve.wait_ge(s["E2_masked"], START + t + 1)
                dve.wait_ge(s["qk_acc"], START + t + 1)
                dve.tensor_tensor(QK[b][:, :, :], heads(Q_BANK), E2[:, :, :], ALU.mult).then_inc(s["qk_ready"], 1)

            def decayed_k(t, b):
                after(dve, "ds_acc", t - 1)
                dve.wait_ge(s["kv_turned"], START + t + 1)
                dve.tensor_tensor(kd[b][:, :, :], heads(K_BANK), E2[:, :, P - 1:P].broadcast_to(bc), ALU.mult).then_inc(s["kd_ready"], 1)

            def begin_T(t, b):
                after(dve, "Ub_ready", t)
                eye = p.ident.unsqueeze(1).broadcast_to([P, 2, P])
                dve.wait_ge(s["m0_turned"], START + t + 1)
                for g in range(2):
                    dve.tensor_tensor(UT[g][:, 1, :, :], eye, heads(VN_BANK)[:, 2 * g:2 * g + 2, :], ALU.subtract).then_inc(s["U_begun"], 1)
                dve.wait_ge(s["levels_masked"], START + LEVELS * t + 1)
                for g in range(2):
                    m = dve.tensor_tensor(UT[g][:, 0, :, :], eye, ML[b][:, 0, 2 * g:2 * g + 2, :], ALU.subtract)
                m.then_inc(s["T_begun"], 1)

            def level(t, l):
                for g in range(2):
                    dve.wait_ge(ut_acc, START + LV * t + 2 * (l - 1) + g + 1)
                    if l < LEVELS - 1:
                        v = UT[g][:, :, :, :].rearrange("p u h n -> p (u h n)")
                        dve.tensor_tensor(v, v, ps[:, 6 + g, :], ALU.subtract).then_inc(ut_done, 1)
                    else:
                        v = UT[g][:, 1, :, :].rearrange("p h n -> p (h n)")
                        dve.tensor_tensor(v, v, ps[:, 6 + g, 2 * P:4 * P], ALU.subtract).then_inc(ut_done, 1)

            def finish(t, b):
                dve.wait_ge(ut_done, START + LV * t + LV)
                for g in range(2):
                    m = dve.tensor_tensor(Ub[b][:, 2 * g:2 * g + 2, :], UT[g][:, 1, :, :],
                                          beta[b][:, 2 * g:2 * g + 2].unsqueeze(2).broadcast_to([P, 2, P]), ALU.mult)
                m.then_inc(s["Ub_ready"], 1)

            def state_rhs(t, b):
                dve.wait_ge(s["ks_acc"], START + t + 1)
                dve.wait_ge(s["v_ready"], START + t + 1)
                dve.tensor_tensor(rhs[:, :, :], vt[b][:, :, :], heads(KS_BANK), ALU.subtract).then_inc(s["rhs_ready"], 1)

            def state_update(t, b):
                dve.wait_ge(s["ds_acc"], START + t + 1)
                dve.wait_ge(s["o_acc"], START + t + 1)
                for h in range(GH):
                    m = dve.scalar_tensor_tensor(out=S[:, h, :], in0=S[:, h, :], scalar=last[b][:, h:h + 1], in1=heads(KS_BANK, h), op0=ALU.mult, op1=ALU.add)
                m.then_inc(s["state"], 1)

            def front(t, b, ld_count):
                spread(t, b)
                decays(t)
                for part in (blocks, decayed_qk, decayed_k, begin_T):
                    part(t, b)

            def tile(t, b, ahead, state):
                ahead = ahead and ahead[0:2]
                if ahead:
                    spread(*ahead)
                if state:
                    state_rhs(*state)
                for l in range(1, LEVELS):
                    level(t, l)
                    if l == 1 and ahead:
                        decays(ahead[0])
                    if l == 2 and ahead:
                        blocks(*ahead)
                    if l == 3:
                        if state:
                            state_update(*state)
                        if ahead:
                            decayed_qk(*ahead)
                    if l == 5 and ahead:
                        decayed_k(*ahead)
                finish(t, b)
                if ahead:
                    begin_T(*ahead)

            def state(t, b):
                state_rhs(t, b)
                state_update(t, b)

            dve.memset(S[:, :, :], 0.0).then_inc(s["state"], 1)
            over_tiles(front, tile, state)(dve)

        @block.scalar
        def _(act):
            def decays(t, b):
                act.wait_ge(s["G_clamped"], START + 2 * t + 2)
                act.activation(E1[:, :, :], E1[:, :, :], ACT.Exp, scale=-1.0)
                act.activation(E2[:, :, :], E2[:, :, :], ACT.Exp)
                after(act, "scaled_by_G", t)
                act.activation(EG[:, :, :], heads(G_BANK), ACT.Exp).then_inc(s["decays"], 1)

            def values(t, b):
                if not isinstance(t, int) or t >= 2:
                    act.wait_ge(s["state"], START + t)
                act.activation(last[b][:, :], heads(G_BANK)[:, :, P - 1], ACT.Exp).then_inc(s["edges"], 1)
                act.wait_ge(s["kv_turned"], START + t + 1)
                act.activation(vt[b][:, :, :], heads(Q_BANK), ACT.Copy).then_inc(s["v_ready"], 1)

            def level(t, l):
                for g in range(2):
                    act.wait_ge(q_acc, START + LV * t + 2 * (l - 1) + g + 1)
                    act.activation(Qs[g][:, :, :], ps[:, 6 + g, 0:2 * P].rearrange("p (h n) -> p h n", h=2), ACT.Copy).then_inc(q_out, 1)

            def state_vn(t):
                act.wait_ge(s["vn_acc"], START + t + 1)
                act.activation(Vn[:, :, :], heads(VN_BANK), ACT.Copy).then_inc(s["vn_ready"], 1)

            def outputs(t):
                act.wait_ge(s["o_acc"], START + t + 1)
                after(act, "o_stored", 16 * t)
                act.activation(ob[:, :, :], heads(O_BANK), ACT.Copy).then_inc(s["o_ready"], 1)

            def front(t, b, ld_count):
                decays(t, b)
                values(t, b)

            def tile(t, b, ahead, state):
                for l in range(1, LEVELS):
                    level(t, l)
                    if l == 2:
                        if ahead:
                            decays(*ahead[0:2])
                        if state:
                            state_vn(state[0])
                    if l == 3 and state:
                        outputs(state[0])
                    if l == 5 and ahead:
                        values(*ahead[0:2])

            def state(t, b):
                state_vn(t)
                outputs(t)

            over_tiles(front, tile, state)(act)

        @block.gpsimd
        def _(pool):
            def front(t, b, ld_count):
                pool.wait_ge(s["decays"], START + t + 1)
                pool.tensor_tensor(E2[:, :, :], E2[:, :, :], p.utri.unsqueeze(1).broadcast_to(bc), ALU.mult).then_inc(s["E2_masked"], 1)
                pool.wait_ge(s["A_ready"], START + t + 1)
                for l in range(LEVELS):
                    mask = p.con[:, C_LM + l * P:C_LM + (l + 1) * P].unsqueeze(1).broadcast_to(bc)
                    pool.tensor_tensor(ML[b][:, l, :, :], A[:, :, :], mask, ALU.mult).then_inc(s["levels_masked"], 1)
                    if l == 2:
                        if not isinstance(t, int) or t >= 2:
                            pool.wait_ge(s["o_acc"], START + t - 1)
                        pool.wait_ge(loaded[b], START + ld_count)
                        pool.tensor_tensor(kE[b][:, :, :], ld[b][:, GH:2 * GH, :], EG[:, :, :], ALU.mult)
                        pool.tensor_tensor(qE[b][:, :, :], ld[b][:, 0:GH, :], EG[:, :, :], ALU.mult).then_inc(s["scaled_by_G"], 1)

            pool.memset(ld[0][:, :, 0:M0], 0.0).then_inc(s["zeroed_d"], 1)
            pool.wait_ge(s["zeroed_d"], START + 1)
            pool.memset(ob[:, :, :], 0.0).then_inc(s["zeroed_d"], 1)
            over_tiles(front, lambda t, b, ahead, state: ahead and front(*ahead), lambda t, b: None)(pool)


def conv_states(p):
    nc, ps = p.nc, p.ps
    turned, out, stored = p.sem("cs_turned"), p.sem("cs_out"), p.sem("cs_stored")
    with ExitStack() as st:
        rows = p.sb("cs_rows", [27, CB * P], stack=st)
        block = p.block(st)

        @block.tensor
        def _(pe):
            for c in range(CB):
                m = pe.transpose(ps[0:27, c // 4, (c % 4) * P:(c % 4 + 1) * P], p.tails[:, c, :], p.ident)
            m.then_inc(turned, 1)

        @block.vector
        def _(dve):
            dve.wait_ge(turned, START + 1)
            for c in range(3):
                dve.tensor_copy(rows[:, 512 * c:512 * c + 512], ps[0:27, c, :]).then_inc(out, 1)

        @block.sync
        def _(sp):
            sp.wait_ge(out, START + 3)
            sp.dma_start(p.io["conv_sample"][0].rearrange("b i n -> (b i) n"), rows[0:24, :]).then_inc(stored, 16)
            sp.dma_start(p.io["conv_prompt"][0, 0], rows[24:27, :]).then_inc(stored, 16)
            sp.wait_ge(stored, START + 32)


def sample_delta(p):
    nc, ps = p.nc, p.ps
    names = ("loaded", "spread", "G_acc", "G_col", "dif", "clamped", "decays", "kk_acc", "A_ready", "masked", "E2_masked",
             "QK_ready", "k_turned", "kd_ready", "m0_turned", "T_begun", "Q_acc", "Q_out", "UT_acc", "UT_done", "Ub_ready",
             "scaled", "ks_acc", "rhsT_ready", "rhs_turned", "rhs_ready", "vn_acc", "vn_ready", "oT_acc", "oT_ready",
             "o_turned", "o_ready", "ds_acc", "s_ready", "stored")
    s = {n: p.sem("e_" + n) for n in names}
    u8 = p.con[0:NS, C_U8:C_U8 + NS]
    ident = p.con[0:NS, C_ID:C_ID + NS]
    bc = [NS, GH, NS]
    with ExitStack() as st:
        def sb(name, *shape):
            return p.sb("e_" + name, list(shape), stack=st)

        ld, S = sb("ld", P, 12, NS), sb("S", P, SEQS, GH, P)
        gB, Gc = sb("gB", NS, GH, P), sb("Gc", NS, GH)
        dif, E1, E2, A = (sb(n, NS, GH, NS) for n in ("dif", "E1", "E2", "A"))
        EG, kE, qE = (sb(n, P, GH, NS) for n in ("EG", "kE", "qE"))
        ML, T, U, Qs, QK, Ub = sb("ML", NS, 3, GH, NS), *(sb(n, NS, GH, NS) for n in ("T", "U", "Qs", "QK", "Ub"))
        kd = sb("kd", NS, SEQS, GH, P)
        rhsT, oT = sb("rhsT", P, GH, NS), sb("oT", P, GH, NS)
        rhs, Vn, ob = (sb(n, NS, GH, P) for n in ("rhs", "Vn", "ob"))
        block = p.block(st)

        def b64(bank, half=0):
            return ps[0:NS, bank, 256 * half:256 * half + 256].rearrange("p (h n) -> p h n", h=GH)

        def b128(bank, n=NS):
            return ps[0:n, bank, :].rearrange("p (h n) -> p h n", h=GH)

        def c64(bank):
            return ps[:, bank, 0:256].rearrange("p (h n) -> p h n", h=GH)

        @block.sync
        def _(sp):
            sp.dma_start(ld[:, :, :], p.chan[0:12].rearrange("c p n -> p c n")[:, :, 0:NS]).then_inc(s["loaded"], 16)
            sp.dma_start(S[:, :, :, :].rearrange("p b h n -> p (b h) n"), p.io["state_gdn"][0].rearrange("b h k v -> k (b h) v")).then_inc(s["loaded"], 16)
            sp.wait_ge(s["o_ready"], START + 1)
            sp.dma_start(p.o_rows[0][0:NS, 0:HALF], ob[:, :, :].rearrange("p h n -> p (h n)")).then_inc(s["stored"], 16)
            sp.wait_ge(s["s_ready"], START + SEQS)
            sp.dma_start(p.io["gdn_sample"][0].rearrange("b h k v -> k (b h) v"), S[:, :, :, :].rearrange("p b h n -> p (b h) n")).then_inc(s["stored"], 16)
            sp.wait_ge(s["stored"], START + 32)

        @block.tensor
        def _(pe):
            pe.wait_ge(s["spread"], START + 1)
            for h in range(GH):
                pe.matmul(c64(0)[:, h, :], gB[:, h, :], u8, start=True, stop=True)
            pe.matmul(ps[0:NS, 1, 0:GH], u8, p.g_s[0:NS, :], start=True, stop=True).then_inc(s["G_acc"], 1)
            pe.wait_ge(s["loaded"], START + 32)
            for h in range(GH):
                pe.matmul(b64(2)[:, h, :], ld[:, GH + h, :], ld[:, GH + h, :], start=True, stop=True)
                m = pe.matmul(b64(3)[:, h, :], ld[:, GH + h, :], ld[:, h, :], start=True, stop=True)
            m.then_inc(s["kk_acc"], 1)
            for h in range(GH):
                m = pe.transpose(b128(4)[:, h, :], ld[:, GH + h, :], p.ident)
            m.then_inc(s["k_turned"], 1)
            pe.wait_ge(s["masked"], START + 3)
            for h in range(GH):
                m = pe.transpose(b64(5)[:, h, :], ML[:, 0, h, :], ident)
            m.then_inc(s["m0_turned"], 1)
            pe.wait_ge(s["scaled"], START + 2)
            for b in range(SEQS):
                for h in range(GH):
                    m = pe.matmul(c64(6)[:, h, STEPS * b:STEPS * b + STEPS], S[:, b, h, :], kE[:, h, STEPS * b:STEPS * b + STEPS], start=True, stop=True)
            m.then_inc(s["ks_acc"], 1)
            pe.wait_ge(s["T_begun"], START + 1)
            for l in (1, 2):
                if l == 2:
                    pe.wait_ge(s["UT_done"], START + 1)
                for h in range(GH):
                    m = pe.matmul(b64(5)[:, h, :], ML[:, l, h, :], U[:, h, :], start=True, stop=True)
                m.then_inc(s["Q_acc"], 1)
                pe.wait_ge(s["Q_out"], START + l)
                for h in range(GH):
                    m = pe.matmul(b64(2)[:, h, :], T[:, h, :], Qs[:, h, :], start=True, stop=True)
                    if l == 1:
                        m = pe.matmul(b64(3)[:, h, :], Qs[:, h, :], T[:, h, :], start=True, stop=True)
                m.then_inc(s["UT_acc"], 1)
            pe.wait_ge(s["rhsT_ready"], START + 1)
            for h in range(GH):
                m = pe.transpose(b128(7)[:, h, :], rhsT[:, h, :], p.ident)
            m.then_inc(s["rhs_turned"], 1)
            pe.wait_ge(s["rhs_ready"], START + 1)
            pe.wait_ge(s["Ub_ready"], START + 1)
            for h in range(GH):
                m = pe.matmul(b128(1)[:, h, :], Ub[:, h, :], rhs[:, h, :], start=True, stop=True)
            m.then_inc(s["vn_acc"], 1)
            pe.wait_ge(s["vn_ready"], START + 1)
            for h in range(GH):
                pe.matmul(c64(0)[:, h, :], Vn[:, h, :], QK[:, h, :], start=True, stop=False)
                for b in range(SEQS):
                    m = pe.matmul(c64(0)[:, h, STEPS * b:STEPS * b + STEPS], S[:, b, h, :], qE[:, h, STEPS * b:STEPS * b + STEPS],
                                  start=False, stop=(b == SEQS - 1))
            m.then_inc(s["oT_acc"], 1)
            pe.wait_ge(s["kd_ready"], START + SEQS)
            for b in range(SEQS):
                if b >= 2:
                    pe.wait_ge(s["s_ready"], START + b - 1)
                for h in range(GH):
                    m = pe.matmul(b128(2 + b % 2, P)[:, h, :], kd[:, b, h, :], Vn[:, h, :], start=True, stop=True)
                m.then_inc(s["ds_acc"], 1)
            pe.wait_ge(s["oT_ready"], START + 1)
            for h in range(GH):
                m = pe.transpose(b128(5)[:, h, :], oT[:, h, :], p.ident)
            m.then_inc(s["o_turned"], 1)

        @block.vector
        def _(dve):
            beta = p.beta[0:NS, 0, :]
            dve.tensor_copy(gB[:, :, :], p.g_s[0:NS, :].unsqueeze(2).broadcast_to([NS, GH, P])).then_inc(s["spread"], 1)
            dve.wait_ge(s["G_acc"], START + 1)
            dve.tensor_copy(Gc[:, :], ps[0:NS, 1, 0:GH]).then_inc(s["G_col"], 1)
            dve.wait_ge(s["G_col"], START + 1)
            dve.tensor_tensor(dif[:, :, :], c64(0)[0:NS], Gc[:, :].unsqueeze(2).broadcast_to(bc), ALU.subtract).then_inc(s["dif"], 1)
            dve.wait_ge(s["dif"], START + 1)
            dve.tensor_scalar(E1[:, :, :], dif[:, :, :], 0.0, None, ALU.max).then_inc(s["clamped"], 1)
            dve.tensor_scalar(E2[:, :, :], dif[:, :, :], 0.0, None, ALU.min).then_inc(s["clamped"], 1)
            dve.wait_ge(s["decays"], START + 3)
            dve.wait_ge(s["kk_acc"], START + 1)
            for h in range(GH):
                m = dve.scalar_tensor_tensor(out=A[:, h, :], in0=b64(2)[:, h, :], scalar=beta[:, h:h + 1], in1=E1[:, h, :], op0=ALU.mult, op1=ALU.mult)
            m.then_inc(s["A_ready"], 1)
            dve.wait_ge(s["E2_masked"], START + 1)
            dve.tensor_tensor(QK[:, :, :], b64(3), E2[:, :, :], ALU.mult).then_inc(s["QK_ready"], 1)
            dve.wait_ge(s["k_turned"], START + 1)
            for b in range(SEQS):
                c = STEPS * b + STEPS - 1
                dve.tensor_tensor(kd[:, b, :, :], b128(4), E2[:, :, c:c + 1].broadcast_to([NS, GH, P]), ALU.mult).then_inc(s["kd_ready"], 1)
            dve.wait_ge(s["m0_turned"], START + 1)
            eye = ident.unsqueeze(1).broadcast_to(bc)
            dve.tensor_tensor(T[:, :, :], eye, ML[:, 0, :, :], ALU.subtract)
            dve.tensor_tensor(U[:, :, :], eye, b64(5), ALU.subtract).then_inc(s["T_begun"], 1)
            dve.wait_ge(s["ks_acc"], START + 1)
            dve.tensor_tensor(rhsT[:, :, :], ld[:, 2 * GH:3 * GH, :], c64(6), ALU.subtract).then_inc(s["rhsT_ready"], 1)
            dve.wait_ge(s["UT_acc"], START + 1)
            dve.tensor_tensor(T[:, :, :], T[:, :, :], b64(3), ALU.subtract)
            dve.tensor_tensor(U[:, :, :], U[:, :, :], b64(2), ALU.subtract).then_inc(s["UT_done"], 1)
            dve.wait_ge(s["UT_acc"], START + 2)
            dve.wait_ge(s["UT_done"], START + 1)
            dve.tensor_tensor(U[:, :, :], U[:, :, :], b64(2), ALU.subtract).then_inc(s["UT_done"], 1)
            dve.wait_ge(s["UT_done"], START + 2)
            dve.tensor_tensor(Ub[:, :, :], U[:, :, :], beta.unsqueeze(2).broadcast_to(bc), ALU.mult).then_inc(s["Ub_ready"], 1)
            dve.wait_ge(s["oT_acc"], START + 1)
            for b in range(SEQS):
                c = STEPS * b + STEPS - 1
                dve.wait_ge(s["ds_acc"], START + b + 1)
                for h in range(GH):
                    m = dve.scalar_tensor_tensor(out=S[:, b, h, :], in0=S[:, b, h, :], scalar=EG[:, h, c:c + 1], in1=b128(2 + b % 2, P)[:, h, :], op0=ALU.mult, op1=ALU.add)
                m.then_inc(s["s_ready"], 1)

        @block.scalar
        def _(act):
            act.wait_ge(s["clamped"], START + 2)
            act.activation(E1[:, :, :], E1[:, :, :], ACT.Exp, scale=-1.0).then_inc(s["decays"], 1)
            act.activation(E2[:, :, :], E2[:, :, :], ACT.Exp).then_inc(s["decays"], 1)
            act.activation(EG[:, :, :], c64(0), ACT.Exp).then_inc(s["decays"], 1)
            for l in (1, 2):
                act.wait_ge(s["Q_acc"], START + l)
                act.activation(Qs[:, :, :], b64(5), ACT.Copy).then_inc(s["Q_out"], 1)
            act.wait_ge(s["rhs_turned"], START + 1)
            act.activation(rhs[:, :, :], b128(7), ACT.Copy).then_inc(s["rhs_ready"], 1)
            act.wait_ge(s["vn_acc"], START + 1)
            act.activation(Vn[:, :, :], b128(1), ACT.Copy).then_inc(s["vn_ready"], 1)
            act.wait_ge(s["oT_acc"], START + 1)
            act.activation(oT[:, :, :], c64(0), ACT.Copy).then_inc(s["oT_ready"], 1)
            act.wait_ge(s["o_turned"], START + 1)
            act.activation(ob[:, :, :], b128(5), ACT.Copy).then_inc(s["o_ready"], 1)

        @block.gpsimd
        def _(pool):
            pool.wait_ge(s["decays"], START + 3)
            pool.tensor_tensor(E2[:, :, :], E2[:, :, :], u8.unsqueeze(1).broadcast_to(bc), ALU.mult).then_inc(s["E2_masked"], 1)
            pool.wait_ge(s["loaded"], START + 32)
            pool.tensor_tensor(kE[:, :, :], ld[:, GH:2 * GH, :], EG[:, :, :], ALU.mult).then_inc(s["scaled"], 1)
            pool.tensor_tensor(qE[:, :, :], ld[:, 0:GH, :], EG[:, :, :], ALU.mult).then_inc(s["scaled"], 1)
            pool.wait_ge(s["A_ready"], START + 1)
            for l in range(3):
                mask = p.con[0:NS, C_LM + l * P:C_LM + l * P + NS].unsqueeze(1).broadcast_to(bc)
                pool.tensor_tensor(ML[:, l, :, :], A[:, :, :], mask, ALU.mult).then_inc(s["masked"], 1)


ROWS = SEQ // P
LAG = 3
RING = 4


def row_pieces(t):
    w = N_META + P * t
    n = -(-w // 1024)
    cut = [min(w, P * -(-(w * i // n) // P)) for i in range(n)] + [w]
    return [(a, b) for a, b in zip(cut, cut[1:])]


def prompt_attention(p):
    nc, ps = p.nc, p.ps
    W = TOK
    pieces = [row_pieces(r + 1) for r in range(ROWS)]
    first_piece = np.cumsum([0] + [len(x) for x in pieces]).tolist()
    groups = [-(-(r + 2) // 4) for r in range(ROWS)]
    first_group = np.cumsum([0] + groups).tolist()
    NPC, NG = first_piece[-1], first_group[-1]
    assert NPC % 2 == 0 and NG % 4 == 0 and ROWS % RING == 0
    v_loaded, qk_loaded = p.sem("pv_loaded"), p.sem("qk_loaded")
    z_acc, z_read, scanned, weighed = p.sem("z_acc"), p.sem("z_read"), p.sem("scanned"), p.sem("weighed")
    turned, evacuated, av_done = p.sem("A_turned"), p.sem("AT_evacuated"), p.sem("av_done")
    o_copied, o_stored, filled = p.sem("po_copied"), p.sem("po_stored"), p.sem("pa_filled")
    ready = p.sem("pa_bias_ready")
    with ExitStack() as st:
        def sb(name, *shape):
            return p.sb("f_" + name, list(shape), stack=st)

        v = sb("v", P, ROWS + 1, HALF + SD)
        q, k = sb("q", P, SEQ), sb("k", P, N_META + SEQ)
        keep = [sb(f"keep{i}", P, N_META + SEQ) for i in range(RING)]
        a = [sb(f"a{i}", P, W) for i in range(RING)]
        x = [sb(f"x{i}", P, N_META + SEQ + 1) for i in range(2)]
        at = [sb(f"at{i}", P, 512) for i in range(4)]
        ob, bias = sb("ob", P, ROWS, SD), sb("bias", P, 2)
        block = p.block(st)
        Z_BANK, T_BANK, O_BANK = 0, 4, 7
        L = N_META + SEQ

        SCAN_AT = 2
        AHEAD = 2

        def pair_columns(h):
            return ds(SD * h, P)

        def at_row(h, r):
            return (h, r) if r >= 0 else (h - 1, r + ROWS)

        def wait(eng, sem, n):
            if not isinstance(n, int) or n > 0:
                eng.wait_ge(sem, START + n)

        def over_heads(eng, step, flush):
            for r in range(ROWS):
                step(0, r)
            with eng.Fori(1, SH) as h:
                for r in range(ROWS):
                    step(h, r)
            for r in range(ROWS - LAG, ROWS):
                flush(SH - 1, r)

        @block.sync
        def _(sp):
            sp.wait_ge(filled, START + 1)
            sp.dma_start(v[M0:P, 0, 0:HALF], p.io["v_prompt"][0, 0, 0:N_META].rearrange("l h d -> l (h d)")).then_inc(v_loaded, 16)
            sp.dma_start(v[:, 1:, 0:HALF], p.io["v_prompt"][0, 0, N_META:].rearrange("(t p) h d -> p t (h d)", p=P)).then_inc(v_loaded, 16)

            def load(h, pair, half):
                wait(sp, z_acc, NPC * h)
                sp.dma_start(q[0:SD, :], p.chan[ds(pair + 12, 1), half * SD:half * SD + SD, P:TOK].rearrange("a p n -> (a p) n")).then_inc(qk_loaded, 16)
                sp.dma_start(k[0:SD, :], p.chan[ds(pair + 16, 1), half * SD:half * SD + SD, M0:TOK].rearrange("a p n -> (a p) n")).then_inc(qk_loaded, 16)

            def store(h):
                sp.wait_ge(o_copied, START + ROWS * (h + 1))
                sp.dma_start(p.o_rows[1:, :, ds(HALF + SD * h, SD)].rearrange("t p n -> p t n"), ob[:, :, :]).then_inc(o_stored, 16)

            load(0, 0, 0)
            load(1, 0, 1)
            store(0)
            with sp.Fori(1, PAIRS) as j:
                load(2 * j, j, 0)
                store(2 * j - 1)
                load(2 * j + 1, j, 1)
                store(2 * j)
            store(SH - 1)
            sp.wait_ge(o_stored, START + 16 * SH)

        @block.tensor
        def _(pe):
            def scores(h, r):
                if r == 0:
                    pe.wait_ge(qk_loaded, START + 32 * (h + 1))
                for i, (c0, c1) in enumerate(pieces[r]):
                    n = first_piece[r] + i
                    wait(pe, z_read, NPC * h + n - 1)
                    for lo in range(c0, c1, 512):
                        hi = min(lo + 512, c1)
                        bank = ps[:, Z_BANK + 2 * (n % 2) + (lo - c0) // 512, :]
                        last = hi == pieces[r][-1][1]
                        m = pe.matmul(bank[:, 0:hi - lo], q[:, r * P:(r + 1) * P], k[:, lo:hi], start=True, stop=not last)
                        if last:
                            cut = max(lo, c1 - P)
                            if cut > c1 - P:
                                pe.matmul(ps[:, Z_BANK + 2 * (n % 2), lo - c0 - (cut - c1 + P):512], p.ident, p.con[:, C_NM:C_NM + cut - c1 + P], start=False, stop=True, skip_group_check=True)
                            m = pe.matmul(bank[:, cut - lo:hi - lo], p.ident, p.con[:, C_NM + P - (c1 - cut):C_NM + P], start=False, stop=True)
                    m.then_inc(z_acc, 1)

            row_of = [r for r in range(ROWS) for _ in range(groups[r])]

            def turn(h, n):
                h, n = (h, n) if n < NG else (h + 1, n - NG)
                r = row_of[n]
                g = n - first_group[r]
                if g == 0:
                    pe.wait_ge(weighed, START + ROWS * h + r + 1)
                if n >= 3 or not isinstance(h, int) or h > 0:
                    hh, mm = (h, n - 3) if n >= 3 else (h - 1, max(m for m in range(NG) if m % 3 == n))
                    pe.wait_ge(evacuated, START + NG * hh + mm + 1)
                c = W - L + (L - N_META - P * (r + 1)) - M0
                for j in range(min(4, r + 2 - 4 * g)):
                    b = 4 * g + j
                    m = pe.transpose(ps[:, T_BANK + n % 3, j * P:(j + 1) * P], a[r % RING][:, c + b * P:c + (b + 1) * P], p.ident)
                m.then_inc(turned, 1)

            def values(h, r, g):
                n = first_group[r] + g
                pe.wait_ge(evacuated, START + NG * h + n + 1)
                if g == 0:
                    wait(pe, o_copied, ROWS * h + r - 1)
                for j in range(min(4, r + 2 - 4 * g)):
                    b = 4 * g + j
                    m = pe.matmul(ps[:, O_BANK, P * (r % 2):P * (r % 2) + P], at[n % 4][:, j * P:(j + 1) * P],
                                  v[:, b, pair_columns(h)], start=(b == 0), stop=(b == r + 1))
                m.then_inc(av_done, 1)

            def second(h, r):
                for g in range(groups[r]):
                    n = first_group[r] + g
                    if isinstance(h, int) and h == 0 and n == 0:
                        turn(h, 0)
                        turn(h, 1)
                    if n + AHEAD < NG or not (isinstance(h, int) and h == SH - 1):
                        turn(h, n + AHEAD)
                    values(h, r, g)

            def step(h, r):
                scores(h, r)
                if not isinstance(h, int) or r >= LAG:
                    second(*at_row(h, r - LAG))

            pe.wait_ge(filled, START + 1)
            pe.wait_ge(v_loaded, START + 32)
            over_heads(pe, step, second)

        @block.scalar
        def _(act):
            def gates(h, r):
                off = L - pieces[r][-1][1]
                for i, (c0, c1) in enumerate(pieces[r]):
                    n = first_piece[r] + i
                    if n == 0:
                        act.wait_ge(ready, START + h + 1)
                    act.wait_ge(z_acc, START + NPC * h + n + 1)
                    if i == 0:
                        wait(act, scanned, ROWS * h + r - RING + 1)
                        hh, rr = at_row(h, r - RING)
                        if not isinstance(hh, int) or hh >= 0:
                            act.wait_ge(turned, START + NG * hh + first_group[rr + 1])
                    z = ps[:, Z_BANK + 2 * (n % 2):Z_BANK + 2 * (n % 2) + 2, :].rearrange("p a n -> p (a n)")[:, 0:c1 - c0]
                    act.activation(keep[r % RING][:, off + c0:off + c1], z, ACT.Sigmoid, scale=-SD ** -0.5, bias=bias[:, 1:2])
                    act.activation(a[r % RING][:, M0 + off + c0:M0 + off + c1], z, ACT.Sigmoid, scale=SD ** -0.5, bias=bias[:, 0:1]).then_inc(z_read, 1)

            over_heads(act, gates, lambda h, r: None)

        @block.vector
        def _(dve):
            def scan(h, r):
                n = pieces[r][-1][1]
                dve.wait_ge(z_read, START + NPC * h + first_piece[r + 1])
                wait(dve, weighed, ROWS * h + r - 1)
                out, src = x[r % 2][:, L - n:L], keep[r % RING][:, L - n:L]
                dve.tensor_tensor_scan(out[:, ::-1], src[:, ::-1], src[:, ::-1], 1.0, ALU.mult, ALU.bypass).then_inc(scanned, 1)

            def second(h, r, late):
                for g in range(groups[r]):
                    if g == min(SCAN_AT, groups[r] - 1):
                        late()
                    n = first_group[r] + g
                    dve.wait_ge(turned, START + NG * h + n + 1)
                    wait(dve, av_done, NG * h + n - 3)
                    nb = min(4, r + 2 - 4 * g) * P
                    dve.tensor_copy(at[n % 4][:, 0:nb], ps[:, T_BANK + n % 3, 0:nb]).then_inc(evacuated, 1)
                dve.wait_ge(av_done, START + NG * h + first_group[r + 1])
                if r == 0:
                    wait(dve, o_stored, 16 * h)
                dve.tensor_copy(ob[:, r, :], ps[:, O_BANK, P * (r % 2):P * (r % 2) + SD]).then_inc(o_copied, 1)

            def head_bias(h):
                wait(dve, z_read, NPC * h)
                for i in range(2):
                    m = dve.tensor_copy(bias[:, i:i + 1], p.small[:, ds(h + 8 + 8 * i, 1)])
                m.then_inc(ready, 1)

            def step(h, r):
                def late():
                    if r or not isinstance(h, int):
                        scan(*at_row(h, r - 1))
                if r == 0:
                    head_bias(h)
                if not isinstance(h, int) or r >= LAG:
                    second(*at_row(h, r - LAG), late)
                else:
                    late()

            def flush(h, r):
                second(h, r, lambda: scan(h, ROWS - 1) if r == ROWS - LAG else None)

            dve.memset(v[:, 0, :], 0.0)
            dve.memset(v[:, 1:, HALF:HALF + SD], 0.0)
            dve.memset(q[SD:P, :], 0.0)
            dve.memset(k[SD:P, :], 0.0)
            for i in range(2):
                dve.memset(x[i][:, L:L + 1], 1.0)
            for i in range(RING - 1):
                dve.memset(a[i][:, :], 0.0)
            dve.memset(a[RING - 1][:, :], 0.0).then_inc(filled, 1)
            over_heads(dve, step, flush)

        @block.gpsimd
        def _(pool):
            def step(h, r):
                n = pieces[r][-1][1]
                pool.wait_ge(scanned, START + ROWS * h + r + 1)
                w = a[r % RING][:, M0 + L - n:M0 + L]
                pool.tensor_tensor(w, w, x[r % 2][:, L - n + 1:L + 1], ALU.mult).then_inc(weighed, 1)

            over_heads(pool, step, lambda h, r: None)


def sample_attention(p):
    nc, ps = p.nc, p.ps
    GP = 4
    G = PAGES // GP
    W = GP * PAGE
    ITS = SEQS // 2
    Z_BANK, A_BANK, O_BANK = 4, 6, 7
    once_act, zeroed, passed = p.sem("s_once_act"), p.sem("s_zeroed"), p.sem("s_passed")
    once, q_placed, mask_ready = p.sem("s_once"), p.sem("q_placed"), p.sem("mask_ready")
    table = p.sem("table")
    k_loaded, v_loaded = [p.sem(f"k{s}_loaded") for s in range(2)], [p.sem("v_even_loaded"), p.sem("v_odd_loaded")]
    k_turned, kT_act, kT_dve = p.sem("s_k_turned"), p.sem("kT_by_scalar"), p.sem("kT_by_vector")
    z_acc, gated, scanned, carried, weighed = p.sem("sz_acc"), p.sem("s_gated"), p.sem("s_scanned"), p.sem("s_carried"), p.sem("s_weighed")
    new_acc, new_gated, new_hidden, new_scanned, new_weighed = (p.sem("new_" + n) for n in ("acc", "gated", "hidden", "scanned", "weighed"))
    a_turned, at_out = p.sem("s_a_turned"), p.sem("s_at_out")
    av_done, o_out, stored = p.sem("s_av_done"), p.sem("so_out"), p.sem("so_stored")
    with ExitStack() as st:
        def sb(name, *shape, dt=F32):
            return p.sb("j_" + name, list(shape), dt, stack=st)

        pages = sb("pages", 1, SEQS * PAGES, dt=I32)
        qs, ks, vs = sb("qs", P, PAIRS, NS), sb("ks", P, PAIRS, NS), sb("vs", NS, HALF)
        qb = [sb(f"qb{s}", P, PAIRS * 80) for s in range(2)]
        kp, kT = ([sb(f"{n}{s}", P, 4, HALF) for s in range(2)] for n in ("kp", "kT"))
        v = [sb(f"v{b}", P, 2, GP, HALF) for b in range(2)]
        keep, a = ([sb(f"{n}{b}", P, W) for b in range(2)] for n in ("keep", "a"))
        x = [sb(f"x{b}", P, W + 1) for b in range(2)]
        keep_new, a_new, x_new = sb("keep_new", P, NS), sb("a_new", P, NS), sb("x_new", P, NS + 1)
        mask, unmask = sb("mask", P, NS), sb("unmask", P, NS)
        at, at_new = [sb(f"at{b}", P, GP, P) for b in range(2)], sb("at_new", NS, P)
        ob = sb("ob", P, ITS, 2 * P)
        bias, nil = sb("bias", P, 2), sb("nil", P, 2 * P)
        block = p.block(st)

        def after(eng, sem, n):
            if not isinstance(n, int) or n > 0:
                eng.wait_ge(sem, START + n)

        @block.sync
        def _(sp):
            sp.dma_start(pages[:, :], p.io["page_table"].rearrange("b n -> (b n)").rearrange("(a n) -> a n", a=1)).then_inc(table, 16)
            sp.dma_start(qs[:, :, :], p.chan[12:16, :, 0:NS].rearrange("c p n -> p c n")).then_inc(once, 16)
            sp.dma_start(ks[:, :, :], p.chan[16:20, :, 0:NS].rearrange("c p n -> p c n")).then_inc(once, 16)
            sp.dma_start(vs[:, :], p.io["v_sample"][0].rearrange("b t h d -> (b t) (h d)")).then_inc(once, 16)
            for i in range(2 * SH):
                sp.dma_start(bias[STEPS * i:STEPS * i + STEPS, 0:1], p.io["sb_bias"][0, i % SH:i % SH + 1].partition_broadcast(STEPS)).then_inc(once, 16)
            sp.wait_ge(table, START + 16)

            def load(page, cache, dst, sem):
                sp.dma_start(dst, cache[0, ds(page, 1)].rearrange("a t h d -> t a (h d)")).then_inc(sem, 16)

            def step(it, g):
                phys = {}
                for s in range(2):
                    after(sp, k_turned, 4 * (2 * (G * it + g) + s - 1))
                    sp.sem_inc(passed, 1)
                    for i in range(GP):
                        at_page = 2 * PAGES * it + PAGES * s + GP * (G - 1 - g) + i
                        phys[s, i] = sp.value_load(pages[0:1, ds(at_page, 1)])
                        load(phys[s, i], p.io["cache_k"], kp[s][:, i:i + 1, :], k_loaded[s])
                after(sp, av_done, G * it + g - 1)
                sp.sem_inc(passed, 1)
                for s in range(2):
                    for i in range(GP):
                        load(phys[s, i], p.io["cache_v"], v[g % 2][:, s, i:i + 1, :], v_loaded[g % 2])

            for g in range(G):
                step(0, g)
            with sp.Fori(1, ITS) as it:
                for g in range(G):
                    step(it, g)
            sp.wait_ge(o_out, START + ITS)
            for c in range(PAIRS):
                for i in range(2):
                    src = ob[32 * c + STEPS * i:32 * c + STEPS * i + STEPS, :, :].rearrange("q a (s n) -> q (a s) n", s=2)
                    sp.dma_start(p.o_rows[0][0:NS, HALF + P * c + SD * i:HALF + P * c + SD * i + SD].rearrange("(a q) n -> q a n", q=STEPS),
                                 src[:, :, SD * i:SD * i + SD]).then_inc(stored, 16)
            sp.wait_ge(stored, START + 16 * SH)

        @block.tensor
        def _(pe):
            def turn_keys(it, g, s):
                j = G * it + g
                if g == 2 and s == 0:
                    pe.wait_ge(at_out, START + j - 1)
                pe.wait_ge(k_loaded[s], START + 64 * j + 64)
                for c in range(PAIRS):
                    after(pe, (kT_act, kT_dve)[c // 2], 2 * (2 * j + s) - 1 + c % 2)
                    for i in range(GP):
                        m = pe.transpose(ps[:, c, i * PAGE:(i + 1) * PAGE], kp[s][:, i, c * P:(c + 1) * P], p.ident)
                    m.then_inc(k_turned, 1)

            def turn_weights(it, g):
                j = G * it + g
                pe.wait_ge(weighed, START + j + 1)
                after(pe, at_out, j)
                if g == 0:
                    pe.wait_ge(new_weighed, START + it + 1)
                    pe.wait_ge(kT_act, START + 2 * (2 * j + 3) + 1)
                for i in range(GP):
                    m = pe.transpose(ps[:, A_BANK, i * P:(i + 1) * P], a[g % 2][:, i * P:(i + 1) * P], p.ident)
                if g == 0:
                    m = pe.transpose(ps[0:NS, 0, 0:P], a_new[:, :], p.ident)
                m.then_inc(a_turned, 1)

            def scores(it, g):
                j = G * it + g
                after(pe, gated, j - 1)
                if g == 0:
                    pe.wait_ge(q_placed, START + 2 * it + 2)
                    for s in range(2):
                        for c in range(PAIRS):
                            m = pe.matmul(ps[NS * s:NS * s + NS, Z_BANK, 0:NS], qb[s][:, NS * c:NS * c + NS], ks[:, c, :],
                                          start=(c == 0), stop=(c == PAIRS - 1))
                    m.then_inc(new_acc, 1)
                    pe.wait_ge(new_gated, START + it + 1)
                for c in range(PAIRS):
                    for s in range(2):
                        pe.wait_ge((kT_act, kT_dve)[c // 2], START + 2 * (2 * j + s) + 1 + c % 2)
                        m = pe.matmul(ps[NS * s:NS * s + NS, Z_BANK + g % 2, :], qb[s][:, NS * c:NS * c + NS], kT[s][:, c, :],
                                      start=(c == 0), stop=(c == PAIRS - 1))
                        if c == PAIRS - 1:
                            m.then_inc(z_acc, 1)

            def values(it, g):
                j = G * it + g
                pe.wait_ge(at_out, START + j + 1)
                pe.wait_ge(v_loaded[g % 2], START + 128 * (2 * it + g // 2 + 1))
                if g == 0:
                    after(pe, o_out, it)
                    pe.matmul(ps[:, O_BANK, 0:2 * P], p.ident, nil[:, :], start=True, stop=False)
                for s in range(2):
                    for i in range(-1 if g == 0 else 0, GP):
                        for c in range(PAIRS):
                            cols = slice(NS * s + 16 * c, NS * s + 16 * c + 16)
                            out = ps[32 * c:32 * c + 16, O_BANK, P * s:P * s + P]
                            if i < 0:
                                pe.matmul(out, at_new[:, cols], vs[:, P * c:P * c + P], start=False, stop=False)
                            else:
                                m = pe.matmul(out, at[g % 2][:, i, cols], v[g % 2][:, s, i, P * c:P * c + P], start=False, stop=False)
                if g == G - 1:
                    m = pe.matmul(ps[:, O_BANK, 0:2 * P], p.ident, nil[:, :], start=False, stop=True)
                m.then_inc(av_done, 1)

            def step(it, g):
                j = G * it + g
                turn_keys(it, g, 0)
                turn_keys(it, g, 1)
                if not (isinstance(j, int) and j == 0):
                    before = (it, g - 1) if g else (it - 1, G - 1)
                    turn_weights(*before)
                scores(it, g)
                if not (isinstance(j, int) and j == 0):
                    values(*before)

            for g in range(G):
                step(0, g)
            with pe.Fori(1, ITS) as it:
                for g in range(G):
                    step(it, g)
            turn_weights(ITS - 1, G - 1)
            values(ITS - 1, G - 1)

        def keys_out(eng, j, copy, banks, sem):
            for s in range(2):
                after(eng, z_acc, 2 * j + s - 1)
                for c in banks:
                    eng.wait_ge(k_turned, START + 4 * (2 * j + s) + c + 1)
                    copy(kT[s][:, c, :], ps[:, c, :]).then_inc(sem, 1)

        @block.scalar
        def _(act):
            act.wait_ge(once, START + 16 * (3 + 2 * SH))
            act.activation(bias[:, 1:2], bias[:, 0:1], ACT.Copy, scale=-1.0).then_inc(once_act, 1)
            act.wait_ge(once_act, START + 1)

            def gates(z, keep, a):
                act.activation(keep, z, ACT.Sigmoid, scale=-SD ** -0.5, bias=bias[:, 1:2])
                return act.activation(a, z, ACT.Sigmoid, scale=SD ** -0.5, bias=bias[:, 0:1])

            def step(it, g):
                j = G * it + g
                keys_out(act, j, lambda out, src: act.activation(out, src, ACT.Copy), (0, 1), kT_act)
                if g == 0:
                    act.wait_ge(new_acc, START + it + 1)
                    gates(ps[:, Z_BANK, 0:NS], keep_new[:, :], a_new[:, :]).then_inc(new_gated, 1)
                act.wait_ge(z_acc, START + 2 * j + 2)
                gates(ps[:, Z_BANK + g % 2, :], keep[g % 2][:, :], a[g % 2][:, :]).then_inc(gated, 1)

            for g in range(G):
                step(0, g)
            with act.Fori(1, ITS) as it:
                for g in range(G):
                    step(it, g)

        @block.vector
        def _(dve):
            for s in range(2):
                dve.memset(qb[s][:, :], 0.0).then_inc(zeroed, 1)
            dve.memset(x_new[:, NS:NS + 1], 1.0).then_inc(zeroed, 1)
            dve.memset(nil[:, :], 0.0).then_inc(zeroed, 1)
            dve.wait_ge(zeroed, START + 4)
            dve.wait_ge(once, START + 16 * (3 + 2 * SH))

            def queries(it):
                after(dve, new_hidden, 2 * it)
                after(dve, z_acc, 2 * G * it)
                for s in range(2):
                    src = qs[:, :, ds(2 * STEPS * it + STEPS * s, STEPS)]
                    to = qb[s][:, :].rearrange("p (c n) -> p c n", n=80)
                    dve.tensor_copy(to[0:SD, :, 0:STEPS], src[0:SD])
                    dve.tensor_copy(to[SD:P, :, STEPS:2 * STEPS], src[SD:P]).then_inc(q_placed, 1)
                dve.tensor_copy(mask[:, :], p.con[:, ds(C_MB + 48 - 2 * STEPS * it, NS)]).then_inc(mask_ready, 1)
                dve.wait_ge(mask_ready, START + 2 * it + 1)
                dve.tensor_scalar(unmask[:, :], mask[:, :], -1.0, 1.0, ALU.mult, ALU.add).then_inc(mask_ready, 1)

            def weights_out(it, g):
                j = G * it + g
                dve.wait_ge(a_turned, START + j + 1)
                after(dve, av_done, j - 1)
                if g == 0:
                    dve.tensor_copy(at_new[:, :], ps[0:NS, 0, 0:P])
                dve.tensor_copy(at[g % 2][:, :, :].rearrange("p b n -> p (b n)"), ps[:, A_BANK, :]).then_inc(at_out, 1)

            def new_keys(it):
                dve.wait_ge(new_gated, START + it + 1)
                dve.wait_ge(mask_ready, START + 2 * it + 2)
                dve.tensor_tensor(keep_new[:, :], keep_new[:, :], unmask[:, :], ALU.max).then_inc(new_hidden, 1)
                dve.tensor_tensor(a_new[:, :], a_new[:, :], mask[:, :], ALU.mult).then_inc(new_hidden, 1)
                dve.wait_ge(new_hidden, START + 2 * it + 2)
                after(dve, new_weighed, it)
                dve.tensor_tensor_scan(x_new[:, 0:NS][:, ::-1], keep_new[:, ::-1], keep_new[:, ::-1], 1.0, ALU.mult, ALU.bypass).then_inc(new_scanned, 1)
                dve.wait_ge(new_scanned, START + it + 1)
                after(dve, weighed, G * it)
                dve.tensor_copy(x[0][:, W:W + 1], x_new[:, 0:1]).then_inc(carried, 1)
                dve.tensor_tensor(a_new[:, :], a_new[:, :], x_new[:, 1:NS + 1], ALU.mult).then_inc(new_weighed, 1)

            def weigh(it, g):
                j, b = G * it + g, g % 2
                dve.wait_ge(gated, START + j + 1)
                dve.wait_ge(carried, START + j + 1)
                after(dve, weighed, j)
                dve.tensor_tensor_scan(x[b][:, 0:W][:, ::-1], keep[b][:, ::-1], keep[b][:, ::-1], x[b][:, W:W + 1], ALU.mult, ALU.bypass).then_inc(scanned, 1)
                dve.wait_ge(scanned, START + j + 1)
                if g < G - 1:
                    dve.tensor_copy(x[1 - b][:, W:W + 1], x[b][:, 0:1]).then_inc(carried, 1)
                dve.tensor_tensor(a[b][:, :], a[b][:, :], x[b][:, 1:W + 1], ALU.mult).then_inc(weighed, 1)

            def outputs(it):
                dve.wait_ge(av_done, START + G * it + G)
                dve.tensor_copy(ob[:, ds(it, 1), :].rearrange("p a n -> p (a n)"), ps[:, O_BANK, 0:2 * P]).then_inc(o_out, 1)

            def step(it, g):
                j = G * it + g
                keys_out(dve, j, dve.tensor_copy, (2, 3), kT_dve)
                if not (isinstance(j, int) and j == 0):
                    weights_out(*((it, g - 1) if g else (it - 1, G - 1)))
                if g == 0:
                    new_keys(it)
                weigh(it, g)
                if g == 0 and not (isinstance(j, int) and j == 0):
                    outputs(it - 1)

            queries(0)
            for g in range(G):
                step(0, g)
            with dve.Fori(1, ITS) as it:
                queries(it)
                for g in range(G):
                    step(it, g)
            weights_out(ITS - 1, G - 1)
            outputs(ITS - 1)


def merge(p):
    nc, io, ps = p.nc, p.io, p.ps
    loaded, g_once = [p.sem("m_even_loaded"), p.sem("m_odd_loaded")], p.sem("m_rows_loaded")
    rows_once = p.sem("m_out_rows_loaded")
    h_loaded = [p.sem("m_h_even_loaded"), p.sem("m_h_odd_loaded")]
    names = ("once", "zeroed", "squares", "mean_sq", "rms", "gated", "mixed", "turned", "mT_ready", "y_acc", "summed",
             "stats", "var", "rstd", "normed", "gained", "biased", "junked")
    s = {n: p.sem("m_" + n) for n in names}
    stored = [p.sem("y_even_stored"), p.sem("y_odd_stored")]
    with ExitStack() as st:
        def sb(name, *shape):
            return p.sb("m_" + name, list(shape), stack=st)

        w = sb("w", P, KC, D)
        gn, lng, lnb = sb("gn", P, DK), sb("lng", P, D), sb("lnb", P, D)
        o, gt, hh, mix, yb = ([sb(f"{n}{b}", P, D) for b in range(2)] for n in ("o", "gt", "hh", "mix", "yb"))
        mT = [sb(f"mT{b}", P, KC, P) for b in range(2)]
        junk, ss, rs = sb("junk", P, GH, DK), sb("ss", P, 4), sb("rs", P, 4)
        st6, mv = sb("st6", P, 2, 6), sb("mv", P, 4)
        block = p.block(st)

        def after(eng, sem, n):
            if not isinstance(n, int) or n > 0:
                eng.wait_ge(sem, START + n)

        @block.sync
        def _(sp):
            def load(t, b):
                if not isinstance(t, int) or t >= 2:
                    sp.wait_ge(s["mixed"], START + t - 1)
                for dst, src in ((o[b], p.o_rows), (gt[b], p.gates)):
                    sp.dma_start(dst[:, :], src[ds(t, 1)].rearrange("a p d -> (a p) d")).then_inc(loaded[b], 16)

            def load_h(t, b):
                if not isinstance(t, int) or t >= 2:
                    sp.wait_ge(s["summed"], START + t - 1)
                sp.dma_start(hh[b][:, :], p.h_rows[ds(t, 1)].rearrange("a p d -> (a p) d")).then_inc(h_loaded[b], 16)

            def store(t, b):
                sp.wait_ge(s["biased"], START + t + 1)
                sp.dma_start(io["y_prompt"][0, ds((t - 1) * P, P), :], yb[b][:, :]).then_inc(stored[b], 16)

            sp.wait_ge(s["zeroed"], START + 1)
            sp.dma_start(o[0][0:NS, :], p.o_rows[0][0:NS, :]).then_inc(loaded[0], 16)
            sp.dma_start(gt[0][:, :], p.gates[0]).then_inc(loaded[0], 16)
            sp.dma_start(gn[:, :], row(io["gdn_norm_g"][0])).then_inc(g_once, 16)
            load(1, 1)
            sp.dma_start(w[:, 0:KC // 2, :], io["w_out"][0].rearrange("(c p) n -> p c n", p=P)[:, 0:KC // 2, :]).then_inc(s["once"], 16)
            sp.dma_start(w[:, KC // 2:KC, :], io["w_out"][0].rearrange("(c p) n -> p c n", p=P)[:, KC // 2:KC, :]).then_inc(s["once"], 16)
            load_h(0, 0)
            sp.dma_start(lng[:, :], row(io["ln_out_g"][0])).then_inc(rows_once, 16)
            sp.dma_start(lnb[:, :], row(io["ln_out_b"][0])).then_inc(rows_once, 16)
            load_h(1, 1)
            load(2, 0)
            load(3, 1)
            load(4, 0)
            load_h(2, 0)
            sp.wait_ge(s["biased"], START + 1)
            sp.dma_start(io["y_sample"].rearrange("b t d -> (b t) d"), yb[0][0:NS, :]).then_inc(stored[0], 16)
            with sp.Fori(0, (NT - 5) // 2) as i:
                load(2 * i + 5, 1)
                load_h(2 * i + 3, 1)
                store(2 * i + 1, 1)
                load(2 * i + 6, 0)
                load_h(2 * i + 4, 0)
                store(2 * i + 2, 0)
            load_h(NT - 2, 1)
            store(NT - 4, 1)
            load_h(NT - 1, 0)
            store(NT - 3, 0)
            store(NT - 2, 1)
            store(NT - 1, 0)
            sp.wait_ge(stored[0], START + 16 * (NT // 2 + 1))
            sp.wait_ge(stored[1], START + 16 * (NT // 2))

        @block.tensor
        def _(pe):
            def turn(t, b):
                pe.wait_ge(s["mixed"], START + t + 1)
                after(pe, s["mT_ready"], t)
                for c in range(KC):
                    m = pe.transpose(ps[:, c // 4, (c % 4) * P:(c % 4 + 1) * P], mix[b][:, c * P:(c + 1) * P], p.ident)
                m.then_inc(s["turned"], 1)

            def products(t, b):
                pe.wait_ge(s["mT_ready"], START + t + 1)
                if not isinstance(t, int) or t >= 2:
                    pe.wait_ge(s["summed"], START + t)
                for f in range(2):
                    for c in range(KC):
                        m = pe.matmul(ps[:, 2 + 2 * b + f, :], mT[b][:, c, :], w[:, c, 512 * f:512 * f + 512], start=(c == 0), stop=(c == KC - 1))
                m.then_inc(s["y_acc"], 1)

            turn(0, 0)
            pe.wait_ge(s["once"], START + 32)
            with pe.Fori(0, (NT - 1) // 2) as i:
                turn(2 * i + 1, 1)
                products(2 * i, 0)
                turn(2 * i + 2, 0)
                products(2 * i + 1, 1)
            products(NT - 1, 0)

        def pipelined(eng, first, second):
            first(0, 0, 32)
            first(1, 1, 32)
            with eng.Fori(0, (NT - 3) // 2) as i:
                first(2 * i + 2, 0, 32 * i + 64)
                second(2 * i, 0, 16 * i)
                first(2 * i + 3, 1, 32 * i + 64)
                second(2 * i + 1, 1, 16 * i)
            first(NT - 1, 0, 16 * (NT + 1))
            second(NT - 3, 0, 8 * (NT - 3))
            second(NT - 2, 1, 8 * (NT - 3))
            second(NT - 1, 0, 8 * (NT - 1))

        @block.scalar
        def _(act):
            def squares(t, b, ld):
                act.wait_ge(loaded[b], START + ld)
                after(act, s["rms"], t)
                for h in range(GH):
                    m = act.activation(junk[:, h, :], o[b][:, h * DK:(h + 1) * DK], ACT.Square, accum_out=ss[:, h:h + 1])
                m.then_inc(s["squares"], 1)

            def evacuate(t, b):
                act.wait_ge(s["turned"], START + t + 1)
                if not isinstance(t, int) or t >= 2:
                    act.wait_ge(s["y_acc"], START + t - 1)
                for f in range(2):
                    m = act.activation(mT[b][:, 4 * f:4 * f + 4, :].rearrange("p c n -> p (c n)"), ps[:, f, :], ACT.Copy)
                m.then_inc(s["mT_ready"], 1)

            squares(0, 0, 32)
            squares(1, 1, 32)
            evacuate(0, 0)
            with act.Fori(0, (NT - 3) // 2) as i:
                squares(2 * i + 2, 0, 32 * i + 64)
                evacuate(2 * i + 1, 1)
                squares(2 * i + 3, 1, 32 * i + 64)
                evacuate(2 * i + 2, 0)
            squares(NT - 1, 0, 16 * (NT + 1))
            evacuate(NT - 2, 1)
            evacuate(NT - 1, 0)

        @block.vector
        def _(dve):
            def first(t, b, ld):
                dve.wait_ge(s["squares"], START + t + 1)
                after(dve, s["mixed"], t)
                dve.tensor_scalar(rs[:, :], ss[:, :], 1.0 / DK, RMS_EPS, ALU.mult, ALU.add).then_inc(s["mean_sq"], 1)
                dve.wait_ge(s["rms"], START + t + 1)
                dve.wait_ge(s["gated"], START + t + 1)
                if not isinstance(t, int) or t >= 2:
                    dve.wait_ge(s["turned"], START + t - 1)
                for h in range(GH):
                    c = slice(h * DK, (h + 1) * DK)
                    dve.scalar_tensor_tensor(out=mix[b][:, c], in0=o[b][:, c], scalar=rs[:, h:h + 1], in1=gt[b][:, c], op0=ALU.mult, op1=ALU.mult)
                dve.tensor_tensor(mix[b][:, HALF:D], o[b][:, HALF:D], gt[b][:, HALF:D], ALU.mult).then_inc(s["mixed"], 1)

            def second(t, b, before):
                dve.wait_ge(s["y_acc"], START + t + 1)
                if not isinstance(t, int) or t >= 2:
                    dve.wait_ge(stored[b], START + before)
                dve.wait_ge(h_loaded[b], START + before + 16)
                for f in range(2):
                    c = slice(512 * f, 512 * f + 512)
                    dve.scalar_tensor_tensor(out=yb[b][:, c], in0=hh[b][:, c], scalar=ALPHA, in1=ps[:, 2 + 2 * b + f, :], op0=ALU.mult, op1=ALU.add).then_inc(s["junked"], 1)
                dve.wait_ge(s["junked"], START + 2 * t + 2)
                dve.tensor_copy(mv[:, 3:4], yb[b][:, 0:1]).then_inc(s["summed"], 1)
                dve.bn_stats(st6[:, 0, :], yb[b][:, 0:512]).then_inc(s["stats"], 1)
                dve.bn_stats(st6[:, 1, :], yb[b][:, 512:1024]).then_inc(s["stats"], 1)
                dve.wait_ge(s["stats"], START + 3 * t + 2)
                dve.tensor_copy(mv[:, 2:3], st6[:, 1, 0:1])
                dve.bn_aggr(mv[:, 0:2], st6[:, :, :].rearrange("p a b -> p (a b)")).then_inc(s["stats"], 1)
                dve.wait_ge(s["stats"], START + 3 * t + 3)
                dve.tensor_scalar(mv[:, 2:3], mv[:, 1:2], LN_EPS, None, ALU.add).then_inc(s["var"], 1)
                dve.wait_ge(s["rstd"], START + t + 1)
                dve.tensor_scalar(yb[b][:, :], yb[b][:, :], mv[:, 0:1], mv[:, 3:4], ALU.subtract, ALU.mult).then_inc(s["normed"], 1)

            pipelined(dve, first, second)

        @block.gpsimd
        def _(pool):
            pool.memset(o[0][NS:P, :], 0.0).then_inc(s["zeroed"], 1)
            pool.wait_ge(g_once, START + 16)

            def first(t, b, ld):
                pool.wait_ge(s["mean_sq"], START + t + 1)
                pool.tensor_tensor(rs[:, :], rs[:, :], p.con[:, C_MH:C_MH + 1].broadcast_to([P, 4]), ALU.pow).then_inc(s["rms"], 1)
                pool.wait_ge(loaded[b], START + ld)
                v = gt[b][:, 0:HALF].rearrange("p (h n) -> p h n", h=GH)
                pool.tensor_tensor(v, v, gn[:, :].unsqueeze(1).broadcast_to([P, GH, DK]), ALU.mult).then_inc(s["gated"], 1)

            def second(t, b, before):
                pool.wait_ge(s["var"], START + t + 1)
                pool.tensor_tensor(mv[:, 3:4], mv[:, 2:3], p.con[:, C_MH:C_MH + 1], ALU.pow).then_inc(s["rstd"], 1)
                pool.wait_ge(rows_once, START + 32)
                pool.wait_ge(s["normed"], START + t + 1)
                pool.tensor_tensor(yb[b][:, :], yb[b][:, :], lng[:, :], ALU.mult).then_inc(s["gained"], 1)
                pool.wait_ge(s["gained"], START + t + 1)
                pool.tensor_tensor(yb[b][:, :], yb[b][:, :], lnb[:, :], ALU.add).then_inc(s["biased"], 1)

            pipelined(pool, first, second)


def build(nc, io, debug=False, stages=99):
    with ExitStack() as stack:
        p = Program(nc, io, stack, debug)
        p.run(setup)
        with ExitStack() as st:
            hT = p.sb("hT", [P, KC, TOK], stack=st)
            p.run(token_major, hT)
            if stages >= 2:
                p.run(channel_major, hT)
            if stages >= 3:
                p.run(attention_heads, hT)
        later = [(4, delta_gates), (4, conv_states), (4, delta_net), (4, sample_delta),
                 (5, prompt_attention), (6, sample_attention), (7, merge)]
        for n, stage in later:
            if stages >= n:
                p.run(stage)


_INS = ["x_prompt", "x_sample", "cache_k", "cache_v", "page_table", "state_gdn", "state_conv", "meta_tokens",
        "ln_in_g", "ln_in_b", "w_in", "conv_w", "a_log", "dt_bias", "gdn_norm_g", "sb_bias", "w_out", "ln_out_g", "ln_out_b"]
_OUTS = [("y_prompt", (1, SEQ, D)), ("y_sample", (SEQS, STEPS, D)),
         ("k_prompt", (1, 1, N_META + SEQ, SH, SD)), ("v_prompt", (1, 1, N_META + SEQ, SH, SD)),
         ("k_sample", (1, SEQS, STEPS, SH, SD)), ("v_sample", (1, SEQS, STEPS, SH, SD)),
         ("gdn_prompt", (1, 1, GH, DK, DK)), ("gdn_sample", (1, SEQS, GH, DK, DK)),
         ("conv_prompt", (1, 1, CONV - 1, 3 * HALF)), ("conv_sample", (1, SEQS, CONV - 1, 3 * HALF))]


def kernel(**inputs):
    import numpy as _np
    import concourse.bacc as _bacc
    from concourse import mybir as _mybir
    from concourse.bass_utils import run_bass_kernel_spmd as _run

    nc = _bacc.Bacc("TRN2", target_bir_lowering=False, num_devices=1)
    arrays, io = {}, {}
    for name in _INS:
        arrays[name] = _np.ascontiguousarray(inputs[name])
    arrays["consts"] = shape_constants()
    for name, a in arrays.items():
        io[name] = nc.dram_tensor(name, a.shape, _mybir.dt.from_np(a.dtype), kind="ExternalInput").ap()
    for name, shape in _OUTS:
        io[name] = nc.dram_tensor(name, shape, F32, kind="ExternalOutput").ap()
    build(nc, io)
    r = _run(nc, [arrays], core_ids=[0])
    return tuple(r.results[0][name] for name, _ in _OUTS)
```
